# Optimizing a Trainium2 kernel written in Bass

```python
import math
import jax
import jax.numpy as jnp
from jax import lax
import numpy as np

D_MODEL = 1024
BATCH = 1
SEQ = 1024
DEPTH = 2

EPS = 1e-6
D_ATT = D_MODEL // 2
D_HY = D_MODEL - D_ATT
ATT_HEADS = 4
ATT_V_DIM = D_ATT // ATT_HEADS
ATT_QK_DIM = ATT_V_DIM // 2
ROPE_DIM = ATT_QK_DIM // 4
ROPE_THETA = 500000.0
Q_BLOCK = 128
HY_SHORT_CONV = 3
HY_EMB_BANDS = 16
HY_EMB_DIM = 1 + 2 * HY_EMB_BANDS
HY_FILTER_FF = 64
HY_TARGET = 1e-2
HY_FAST_DECAY = 0.3
HY_SLOW_DECAY = 1.5
HY_MIN_DECAY = math.log(HY_TARGET) / HY_SLOW_DECAY
HY_MAX_DECAY = math.log(HY_TARGET) / HY_FAST_DECAY
IN_EVEN = 3 * D_ATT + 3 * D_HY
ML_HEADS = 4
ML_V_DIM = D_MODEL // ML_HEADS
ML_QK_DIM = ML_V_DIM // 2
ML_CHUNK = 128
SHORT_CONV = 3
ML_QK_W = 2 * ML_HEADS * ML_QK_DIM
IN_ODD = ML_QK_W + 2 * D_MODEL + 4 * ML_HEADS
N_GROUPS = 4
EXPERTS_PER_GROUP = 8
N_EXPERTS = N_GROUPS * EXPERTS_PER_GROUP
TOP_K = 2
D_EXPERT = D_MODEL // 2
MOE_BLOCK = 128
N_EVEN = (DEPTH + 1) // 2
N_ODD = DEPTH // 2

kernel_name = 'hybrid_diffattn_hyena_mlstm_hmoe_encoder'

def rms_norm(x, g):
    xf = x.astype(jnp.float32)
    y = xf * lax.rsqrt(jnp.mean(xf * xf, axis=-1, keepdims=True) + EPS)
    return (y * g.astype(jnp.float32)).astype(x.dtype)

def centered_dwconv(x, w, b):
    k = w.shape[0]
    pad = k // 2
    s = x.shape[1]
    xp = jnp.pad(x, ((0, 0), (pad, pad), (0, 0)))
    out = b
    for j in range(k):
        out = out + xp[:, j:j + s] * w[j]
    return out

def rope_tables(seq):
    inv_freq = 1.0 / (ROPE_THETA ** (jnp.arange(0, ROPE_DIM, 2, dtype=jnp.float32) / ROPE_DIM))
    ang = jnp.arange(seq, dtype=jnp.float32)[:, None] * inv_freq[None, :]
    return jnp.cos(ang), jnp.sin(ang)

def partial_rope(x, cos, sin):
    half = ROPE_DIM // 2
    x1 = x[..., :half]
    x2 = x[..., half:ROPE_DIM]
    c = cos.astype(x.dtype)
    s = sin.astype(x.dtype)
    return jnp.concatenate([x1 * c - x2 * s, x2 * c + x1 * s, x[..., ROPE_DIM:]], axis=-1)

def diff_attention(u, q_norm, k_norm, lam_q1, lam_k1, lam_q2, lam_k2, subln, lambda_init, cos, sin):
    b, s, _ = u.shape
    h, dk, dv = ATT_HEADS, ATT_QK_DIM, ATT_V_DIM
    q, k, v = jnp.split(u, 3, axis=-1)
    q = q.reshape(b, s, h, 2, dk).transpose(0, 2, 3, 1, 4)
    k = k.reshape(b, s, h, 2, dk).transpose(0, 2, 3, 1, 4)
    v = v.reshape(b, s, h, dv).transpose(0, 2, 1, 3)
    q = partial_rope(rms_norm(q, q_norm), cos, sin) * (dk ** -0.5)
    k = partial_rope(rms_norm(k, k_norm), cos, sin)
    f32 = jnp.float32
    lam = (jnp.exp(jnp.sum(lam_q1.astype(f32) * lam_k1.astype(f32)))
           - jnp.exp(jnp.sum(lam_q2.astype(f32) * lam_k2.astype(f32))) + lambda_init)
    nb = s // Q_BLOCK
    qb = q.reshape(b, h, 2, nb, Q_BLOCK, dk).transpose(3, 0, 1, 2, 4, 5)

    def attend(q_blk):
        sc = jnp.einsum('bhcqd,bhckd->bhcqk', q_blk, k).astype(f32)
        p = jax.nn.softmax(sc, axis=-1)
        w = p[:, :, 0] - lam * p[:, :, 1]
        return jnp.einsum('bhqk,bhkd->bhqd', w.astype(v.dtype), v)

    o = lax.map(attend, qb)
    o = o.transpose(1, 0, 3, 2, 4).reshape(b, s, h, dv)
    o = rms_norm(o, subln) * (1.0 - lambda_init)
    return o.reshape(b, s, h * dv)

def hyena_filter(length, w1, b1, freq, w2, b2, w3):
    f32 = jnp.float32
    w1, b1, freq, w2, b2, w3 = (a.astype(f32) for a in (w1, b1, freq, w2, b2, w3))
    t = jnp.linspace(0.0, 1.0, length, dtype=f32)[:, None]
    bands = jnp.linspace(1e-4, HY_EMB_BANDS - 1, HY_EMB_BANDS, dtype=f32)[None, :]
    ang = (2.0 * math.pi / length) * jnp.arange(length, dtype=f32)[:, None] * bands
    z = jnp.concatenate([t, jnp.cos(ang), -jnp.sin(ang)], axis=-1)
    hdn = jnp.sin(freq * (z @ w1 + b1))
    hdn = jnp.sin(freq * (hdn @ w2 + b2))
    filt = hdn @ w3
    deltas = jnp.abs(jnp.linspace(HY_MIN_DECAY, HY_MAX_DECAY, D_HY, dtype=f32))
    decay = jnp.exp(-t * deltas[None, :])
    h_fwd = filt[:, :D_HY] * decay
    h_bwd = filt[:, D_HY:] * decay
    kern = jnp.concatenate([h_fwd.at[0].add(h_bwd[0]), jnp.zeros((1, D_HY), f32), h_bwd[:0:-1]], axis=0)
    return kern / (jnp.sum(jnp.abs(kern), axis=0, keepdims=True) + EPS)

def hyena_mixer(u, conv_w, conv_b, f_w1, f_b1, f_freq, f_w2, f_b2, f_w3, skip):
    length = u.shape[1]
    uc = centered_dwconv(u, conv_w, conv_b)
    x1, x2, v = jnp.split(uc, 3, axis=-1)
    z = (v * x2).astype(jnp.float32)
    kern = hyena_filter(length, f_w1, f_b1, f_freq, f_w2, f_b2, f_w3)
    n = 2 * length
    zf = jnp.fft.rfft(z, n=n, axis=1)
    kf = jnp.fft.rfft(kern, n=n, axis=0)
    y = jnp.fft.irfft(zf * kf[None], n=n, axis=1)[:, :length]
    y = y + z * skip.astype(jnp.float32)
    return (y * x1.astype(jnp.float32)).astype(u.dtype)

def mlstm_chunkwise(q, k, v, log_i, log_f):
    f32 = jnp.float32
    b, g, s, dk = q.shape
    dv = v.shape[-1]
    lc = ML_CHUNK
    nc = s // lc
    qc = jnp.moveaxis(q.astype(f32).reshape(b, g, nc, lc, dk), 2, 0)
    kc = jnp.moveaxis(k.astype(f32).reshape(b, g, nc, lc, dk), 2, 0)
    vc = jnp.moveaxis(v.astype(f32).reshape(b, g, nc, lc, dv), 2, 0)
    ic = jnp.moveaxis(log_i.astype(f32).reshape(b, g, nc, lc), 2, 0)
    fc = jnp.moveaxis(log_f.astype(f32).reshape(b, g, nc, lc), 2, 0)
    mask = jnp.tril(jnp.ones((lc, lc), dtype=bool))

    def step(carry, inp):
        c_st, n_st, m_st = carry
        qj, kj, vj, lij, lfj = inp
        bcum = jnp.cumsum(lfj, axis=-1)
        dmat = bcum[..., :, None] - bcum[..., None, :] + lij[..., None, :]
        dmat = jnp.where(mask, dmat, -jnp.inf)
        inter = bcum + m_st[..., None]
        m_t = jnp.maximum(inter, jnp.max(dmat, axis=-1))
        w_intra = jnp.exp(dmat - m_t[..., None])
        w_inter = jnp.exp(inter - m_t)
        sc = jnp.einsum('bgtd,bgsd->bgts', qj, kj) * w_intra
        num = (w_inter[..., None] * jnp.einsum('bgtd,bgde->bgte', qj, c_st)
               + jnp.einsum('bgts,bgse->bgte', sc, vj))
        den = w_inter * jnp.einsum('bgtd,bgd->bgt', qj, n_st) + jnp.sum(sc, axis=-1)
        h = num / jnp.maximum(jnp.abs(den), jnp.exp(-m_t))[..., None]
        b_last = bcum[..., -1]
        g_s = b_last[..., None] - bcum + lij
        m_next = jnp.maximum(b_last + m_st, jnp.max(g_s, axis=-1))
        a_prev = jnp.exp(b_last + m_st - m_next)
        kw = kj * jnp.exp(g_s - m_next[..., None])[..., None]
        c_new = a_prev[..., None, None] * c_st + jnp.einsum('bgsd,bgse->bgde', kw, vj)
        n_new = a_prev[..., None] * n_st + jnp.sum(kw, axis=2)
        return (c_new, n_new, m_next), h

    init = (jnp.zeros((b, g, dk, dv), f32), jnp.zeros((b, g, dk), f32), jnp.zeros((b, g), f32))
    _, hs = lax.scan(step, init, (qc, kc, vc, ic, fc))
    return jnp.moveaxis(hs, 0, 2).reshape(b, g, s, dv)

def mlstm_mixer(u, conv_w, conv_b, gate_b, out_norm):
    b, s, _ = u.shape
    h, dk, dv = ML_HEADS, ML_QK_DIM, ML_V_DIM
    qk, v, o, gates = jnp.split(u, [ML_QK_W, ML_QK_W + D_MODEL, ML_QK_W + 2 * D_MODEL], axis=-1)
    qk = jax.nn.silu(centered_dwconv(qk, conv_w, conv_b))
    q, k = jnp.split(qk, 2, axis=-1)
    q = q.reshape(b, s, h, dk).transpose(0, 2, 1, 3) * (dk ** -0.5)
    k = k.reshape(b, s, h, dk).transpose(0, 2, 1, 3)
    v = v.reshape(b, s, h, dv).transpose(0, 2, 1, 3)
    gates = (gates.astype(jnp.float32) + gate_b.astype(jnp.float32)).reshape(b, s, 4, h).transpose(0, 2, 3, 1)

    def flip(a):
        return jnp.flip(a, axis=2)

    log_i = jnp.concatenate([gates[:, 0], flip(gates[:, 2])], axis=1)
    log_f = jax.nn.log_sigmoid(jnp.concatenate([gates[:, 1], flip(gates[:, 3])], axis=1))
    hs = mlstm_chunkwise(jnp.concatenate([q, flip(q)], axis=1), jnp.concatenate([k, flip(k)], axis=1),
                         jnp.concatenate([v, flip(v)], axis=1), log_i, log_f)
    hsum = hs[:, :h] + flip(hs[:, h:])
    hsum = hsum.transpose(0, 2, 1, 3).astype(u.dtype)
    hsum = rms_norm(hsum, out_norm.reshape(h, dv)).reshape(b, s, D_MODEL)
    return hsum * jax.nn.sigmoid(o)

def hier_moe(x, wg, bg, we, be, w1, w3, w2):
    f32 = jnp.float32
    b, s, d = x.shape
    t = b * s
    xt = x.reshape(t, d)
    g_logits = (xt @ wg).astype(f32) + bg.astype(f32)
    g_prob = jax.nn.softmax(g_logits, axis=-1)
    g_idx = jnp.argmax(g_logits, axis=-1)
    g_w = jnp.take_along_axis(g_prob, g_idx[:, None], axis=-1)[:, 0]
    e_logits = ((xt @ we).astype(f32) + be.astype(f32)).reshape(t, N_GROUPS, EXPERTS_PER_GROUP)
    e_logits = jnp.take_along_axis(e_logits, g_idx[:, None, None], axis=1)[:, 0]
    top_p, top_e = lax.top_k(jax.nn.softmax(e_logits, axis=-1), TOP_K)
    top_p = top_p / jnp.sum(top_p, axis=-1, keepdims=True)
    gate = (g_w[:, None] * top_p).reshape(-1)
    eid = (g_idx[:, None] * EXPERTS_PER_GROUP + top_e).reshape(-1).astype(jnp.int32)
    tok = jnp.arange(t * TOP_K, dtype=jnp.int32) // TOP_K
    order = jnp.argsort(eid)
    se = eid[order]
    counts = jnp.bincount(eid, length=N_EXPERTS)
    starts = jnp.cumsum(counts) - counts
    padded = (counts + MOE_BLOCK - 1) // MOE_BLOCK * MOE_BLOCK
    pad_end = jnp.cumsum(padded)
    pad_start = pad_end - padded
    dest = pad_start[se] + (jnp.arange(t * TOP_K) - starts[se])
    cap = t * TOP_K + N_EXPERTS * MOE_BLOCK
    nb = cap // MOE_BLOCK
    buf_tok = jnp.zeros((cap,), jnp.int32).at[dest].set(tok[order])
    buf_gate = jnp.zeros((cap,), f32).at[dest].set(gate[order])
    blk_e = jnp.minimum(jnp.searchsorted(pad_end, jnp.arange(nb) * MOE_BLOCK, side='right'), N_EXPERTS - 1)
    xb = xt[buf_tok].reshape(nb, MOE_BLOCK, d)

    def expert_block(args):
        xe, e = args
        hid = jax.nn.silu(xe @ w1[e]) * (xe @ w3[e])
        return hid @ w2[e]

    yb = lax.map(expert_block, (xb, blk_e)).reshape(cap, d)
    out = jax.ops.segment_sum(yb.astype(f32) * buf_gate[:, None], buf_tok, num_segments=t)
    return out.astype(x.dtype).reshape(b, s, d)

def setup_inputs(seed: int = 0) -> dict:
    key = jax.random.key(seed)
    keys = iter(jax.random.split(key, 48))
    f32 = jnp.float32

    def normal(shape, scale):
        return jax.random.normal(next(keys), shape, f32) * scale

    def gain(shape):
        return 1.0 + normal(shape, 0.02)

    ne, no, d = N_EVEN, N_ODD, D_MODEL
    h = ML_HEADS
    f_bias = jnp.linspace(3.0, 6.0, h, dtype=f32)
    gate_b = jnp.concatenate([normal((no, h), 0.1), f_bias + normal((no, h), 0.1),
                              normal((no, h), 0.1), f_bias + normal((no, h), 0.1)], axis=-1)
    return {
        'x': normal((BATCH, SEQ, d), 1.0),
        'mix_norm': gain((DEPTH, d)),
        'ffn_norm': gain((DEPTH, d)),
        'ev_w_in': normal((ne, d, IN_EVEN), d ** -0.5),
        'ev_q_norm': gain((ne, ATT_QK_DIM)),
        'ev_k_norm': gain((ne, ATT_QK_DIM)),
        'ev_lam_q1': normal((ne, ATT_QK_DIM), 0.1),
        'ev_lam_k1': normal((ne, ATT_QK_DIM), 0.1),
        'ev_lam_q2': normal((ne, ATT_QK_DIM), 0.1),
        'ev_lam_k2': normal((ne, ATT_QK_DIM), 0.1),
        'ev_subln': gain((ne, ATT_V_DIM)),
        'ev_hy_conv_w': normal((ne, HY_SHORT_CONV, 3 * D_HY), HY_SHORT_CONV ** -0.5),
        'ev_hy_conv_b': normal((ne, 3 * D_HY), 0.02),
        'ev_hy_f_w1': normal((ne, HY_EMB_DIM, HY_FILTER_FF), HY_EMB_DIM ** -0.5),
        'ev_hy_f_b1': normal((ne, HY_FILTER_FF), 0.02),
        'ev_hy_f_freq': 1.0 + normal((ne, HY_FILTER_FF), 0.1),
        'ev_hy_f_w2': normal((ne, HY_FILTER_FF, HY_FILTER_FF), HY_FILTER_FF ** -0.5),
        'ev_hy_f_b2': normal((ne, HY_FILTER_FF), 0.02),
        'ev_hy_f_w3': normal((ne, HY_FILTER_FF, 2 * D_HY), HY_FILTER_FF ** -0.5),
        'ev_hy_skip': normal((ne, D_HY), 0.5),
        'ev_w_out': normal((ne, d, d), d ** -0.5),
        'od_w_in': normal((no, d, IN_ODD), d ** -0.5),
        'od_conv_w': normal((no, SHORT_CONV, ML_QK_W), SHORT_CONV ** -0.5),
        'od_conv_b': normal((no, ML_QK_W), 0.02),
        'od_gate_b': gate_b,
        'od_out_norm': gain((no, d)),
        'od_w_out': normal((no, d, d), d ** -0.5),
        'moe_wg': normal((DEPTH, d, N_GROUPS), d ** -0.5),
        'moe_bg': normal((DEPTH, N_GROUPS), 0.01),
        'moe_we': normal((DEPTH, d, N_EXPERTS), d ** -0.5),
        'moe_be': normal((DEPTH, N_EXPERTS), 0.01),
        'moe_w1': normal((DEPTH, N_EXPERTS, d, D_EXPERT), d ** -0.5),
        'moe_w3': normal((DEPTH, N_EXPERTS, d, D_EXPERT), d ** -0.5),
        'moe_w2': normal((DEPTH, N_EXPERTS, D_EXPERT, d), D_EXPERT ** -0.5),
    }

def reference(x, mix_norm, ffn_norm, ev_w_in, ev_q_norm, ev_k_norm, ev_lam_q1, ev_lam_k1, ev_lam_q2,
              ev_lam_k2, ev_subln, ev_hy_conv_w, ev_hy_conv_b, ev_hy_f_w1, ev_hy_f_b1, ev_hy_f_freq,
              ev_hy_f_w2, ev_hy_f_b2, ev_hy_f_w3, ev_hy_skip, ev_w_out, od_w_in, od_conv_w, od_conv_b,
              od_gate_b, od_out_norm, od_w_out, moe_wg, moe_bg, moe_we, moe_be, moe_w1, moe_w3, moe_w2):
    cos, sin = rope_tables(x.shape[1])
    for layer in range(DEPTH):
        j = layer // 2
        hn = rms_norm(x, mix_norm[layer])
        if layer % 2 == 0:
            u = hn @ ev_w_in[j]
            lambda_init = 0.8 - 0.6 * math.exp(-0.3 * layer)
            y_att = diff_attention(u[..., :3 * D_ATT], ev_q_norm[j], ev_k_norm[j], ev_lam_q1[j],
                                   ev_lam_k1[j], ev_lam_q2[j], ev_lam_k2[j], ev_subln[j],
                                   lambda_init, cos, sin)
            y_hy = hyena_mixer(u[..., 3 * D_ATT:], ev_hy_conv_w[j], ev_hy_conv_b[j], ev_hy_f_w1[j],
                               ev_hy_f_b1[j], ev_hy_f_freq[j], ev_hy_f_w2[j], ev_hy_f_b2[j],
                               ev_hy_f_w3[j], ev_hy_skip[j])
            y = jnp.concatenate([y_att, y_hy], axis=-1) @ ev_w_out[j]
        else:
            u = hn @ od_w_in[j]
            y = mlstm_mixer(u, od_conv_w[j], od_conv_b[j], od_gate_b[j], od_out_norm[j]) @ od_w_out[j]
        x = x + y
        x = x + hier_moe(rms_norm(x, ffn_norm[layer]), moe_wg[layer], moe_bg[layer], moe_we[layer],
                         moe_be[layer], moe_w1[layer], moe_w3[layer], moe_w2[layer])
    return x


_drawn_inputs = setup_inputs


def setup_inputs(seed=0):
    import zlib

    import numpy as np

    out = dict(_drawn_inputs(seed))
    spreads = {}
    factors = {'ev_lam_q1': 2.959,
     'ev_hy_f_b1': 7.208,
     'ev_hy_f_freq': 3.047,
     'ev_hy_f_b2': 6.516,
     'od_conv_b': 3.544,
     'od_out_norm': 3.438,
     'moe_bg': 2.77}
    for name, (base, spread) in spreads.items():
        noise = np.random.default_rng([zlib.crc32(name.encode()), seed]).standard_normal(out[name].shape)
        drawn = base * np.exp(spread * noise) if base else spread * noise
        out[name] = jnp.asarray(drawn.astype(out[name].dtype))
    for name, factor in factors.items():
        out[name] = (out[name] * factor).astype(out[name].dtype)
    return out
```

```python
from contextlib import ExitStack

import numpy as np

import concourse.bass as bass
from concourse import mybir

F32 = mybir.dt.float32
F32R = mybir.dt.float32r
I32 = mybir.dt.int32
ALU = mybir.AluOpType
ACT = mybir.ActivationFunctionType
AX = mybir.AxisListType.X

P = 128
D = 1024
T = 1024
NT = T // P
KD = D // P
HALF = 512
EPS = 1e-6

AH = 4
DK = 64
DV = 128
ROPE = 16
NC = 2 * AH
HC = 512 // P
FF = 64
EMB = 33
NF = 4

MH = 4
MV = 256
MVA = MV + 1
GROWS = 36
NEG = -1e30
KSCALE = 128 ** -0.5

NG = 4
EG = 8
NE = NG * EG
DE = 512
OVER = 15
NBLK = NE + OVER
NBLKP = 48

RING = 3
S_ATT, S_HY, S_OUT0, S_MOE0 = 0, 3, 6, 8
S_ML, S_OUT1, S_MOE1, S_END = 104, 110, 112, 208

LAST_PHASE = [99]


class Tally:

    def __init__(self, sem):
        self.sem = sem
        self.n = 0

    def __call__(self, ins):
        ins.then_inc(self.sem, 1)
        self.n += 1
        return self.n


def build(nc, I, out):
    ctx = ExitStack()
    with ctx:
        POOL = 28
        pool = [nc.alloc_semaphore(f"phase_sem{i}") for i in range(POOL)]
        pool_range = range(pool[0].num, pool[0].num + POOL)
        chunk_in = [nc.alloc_semaphore(f"chunk_in{i}") for i in range(RING)]
        consts_in = nc.alloc_semaphore("consts_in")
        y_filled = nc.alloc_semaphore("y_filled")
        gather_in = [nc.alloc_semaphore(f"gather_in{i}") for i in range(2)]
        gathered = [0, 0]
        over_in = [nc.alloc_semaphore(f"over_in{i}") for i in range(2)]
        phases = [0]
        issued = [0] * RING

        def take(n):
            assert n <= POOL, n
            return pool[:n]

        def phase(program):
            def run(*a):
                if phases[0] < LAST_PHASE[0]:
                    program(*a)
            return run

        def end_phase():
            nc.all_engine_barrier(sems_to_clear=pool_range)
            phases[0] += 1

        def sb(stack, name, shape, dt=F32):
            return stack.enter_context(nc.sbuf_tensor(name, shape, dt))

        xs = nc.dram_tensor("x_scratch", (T, D), F32).ap()
        xn_d = nc.dram_tensor("xn_scratch", (T, D), F32).ap()
        so_d = nc.dram_tensor("sigmoid_o_scratch", (T, D), F32).ap()
        y_d = nc.dram_tensor("y_scratch", (NBLK * P, D), F32).ap()

        ring = sb(ctx, "ring", [P, RING, 4096])
        ident = sb(ctx, "ident", [P, P])
        flip = sb(ctx, "flip", [P, P])
        ones = sb(ctx, "ones", [P, P])
        upper = sb(ctx, "upper", [P, P])
        cap_f = sb(ctx, "cap_f", [P, P])
        cap_b = sb(ctx, "cap_b", [P, P])
        xnT = sb(ctx, "xnT", [P, KD, T])
        psum = ctx.enter_context(nc.psum_tensor("psum", [P, 8, 512], F32))

        def half_chunk(w, c0):
            return w[:, c0:c0 + HALF].rearrange("(k p) c -> p k c", p=P)

        def chunk_src(n):
            if n < S_HY:
                return half_chunk(I["ev_w_in"], 512 * (n - S_ATT))
            if n < S_OUT0:
                return half_chunk(I["ev_w_in"], 1536 + 512 * (2 - (n - S_HY)))
            if n < S_MOE0:
                return half_chunk(I["ev_w_out"], 512 * (n - S_OUT0))
            if S_ML <= n < S_OUT1:
                return half_chunk(I["od_w_in"], 512 * (n - S_ML))
            if S_OUT1 <= n < S_MOE1:
                return half_chunk(I["od_w_out"], 512 * (n - S_OUT1))
            layer, m = (0, n - S_MOE0) if n < S_ML else (1, n - S_MOE1)
            return expert_src(layer, m // 3, m % 3)

        def expert_src(layer, e, c):
            w = I[("moe_w1", "moe_w3", "moe_w2")[c]]
            rows = 1024 if c < 2 else 512
            r0 = (e + layer * NE) * rows
            return w[bass.ds(r0, rows), :].rearrange("(k p) c -> p k c", p=P)

        def chunk_dst(slot, src):
            k = src.shape[1]
            return ring[:, slot, :].rearrange("p (k c) -> p k c", k=k)

        def load_chunk(sp, n):
            src = chunk_src(n)
            sp.dma_start(chunk_dst(n % RING, src), src).then_inc(chunk_in[n % RING], 16)
            issued[n % RING] = n // RING + 1

        def refill(sp, first, last, done, each):
            for n in range(first, last):
                if n + RING < S_END:
                    sp.wait_ge(done, each * (n - first + 1))
                    load_chunk(sp, n + RING)

        def chunk_wait(pe, n):
            pe.wait_ge(chunk_in[n % RING], 16 * (n // RING + 1))

        def wide(n):
            return ring[:, n % RING, :].rearrange("p (k c) -> p k c", k=8)

        @phase
        def start_phase():
            (made,) = take(1)
            with nc.Block() as block:
                @block.sync
                def _(sp):
                    for t, name in ((ident, "c_ident"), (flip, "c_flip"), (ones, "c_ones"), (upper, "c_upper"),
                                    (cap_f, "c_cap_f"), (cap_b, "c_cap_b")):
                        sp.dma_start(t[:], I[name]).then_inc(consts_in, 16)
                    for n in range(RING):
                        load_chunk(sp, n)
                    sp.wait_ge(consts_in, 6 * 16)
            end_phase()

        @phase
        def norm_phase(name, src, gain, store):
            (gain_in, x_lo, x_hi, squared, mean_ok, root_ok, recip_ok, xn_ok, tr_lo, tr_hi, copied_lo,
             copied_hi, stored) = take(13)
            with ExitStack() as st:
                x_all = sb(st, f"x_all{name}", [P, NT, D])
                g_bc = sb(st, f"g_bc{name}", [P, D])
                sq = sb(st, f"sq{name}", [P, D])
                ss = sb(st, f"ss{name}", [P, NT])
                ms = sb(st, f"ms{name}", [P, NT])
                sd = sb(st, f"sd{name}", [P, NT])
                rs = sb(st, f"rs{name}", [P, NT])
                rows = src.rearrange("(j p) d -> p j d", p=P)
                with nc.Block() as block:
                    @block.sync
                    def _(sp):
                        sp.dma_start(x_all[:, 0:4, :], rows[:, 0:4, :]).then_inc(x_lo, 16)
                        sp.dma_start(x_all[:, 4:8, :], rows[:, 4:8, :]).then_inc(x_hi, 16)
                        sp.dma_start(g_bc[:], gain.partition_broadcast(P)).then_inc(gain_in, 16)
                        if store is not None:
                            for j in range(NT):
                                sp.wait_ge(xn_ok, j + 1)
                                sp.dma_start(store[j * P:(j + 1) * P, :], x_all[:, j, :]).then_inc(stored, 16)
                            sp.wait_ge(stored, 16 * NT)

                    @block.scalar
                    def _(act):
                        for j in range(NT):
                            act.wait_ge(x_lo if j < 4 else x_hi, 16)
                            if j:
                                act.wait_ge(squared, j)
                            nc.scalar.activation(sq[:], x_all[:, j, :], ACT.Square,
                                                 accum_out=ss[:, j:j + 1]).then_inc(squared, 1)
                        act.wait_ge(mean_ok, 1)
                        nc.scalar.activation(sd[:], ms[:], ACT.Sqrt).then_inc(root_ok, 1)
                        for j in range(NT):
                            act.wait_ge(tr_lo, j + 1)
                            nc.scalar.copy(xnT[:, 0:4, j * P:(j + 1) * P],
                                           psum[:, 2 * (j % 4), :].rearrange("p (k t) -> p k t", k=4)
                                           ).then_inc(copied_lo, 1)

                    @block.vector
                    def _(dve):
                        def move(j):
                            dve.wait_ge(tr_hi, j + 1)
                            nc.vector.tensor_copy(xnT[:, 4:8, j * P:(j + 1) * P],
                                                  psum[:, 2 * (j % 4) + 1, :].rearrange("p (k t) -> p k t", k=4)
                                                  ).then_inc(copied_hi, 1)

                        dve.wait_ge(squared, NT)
                        nc.vector.tensor_scalar(ms[:], ss[:], 1.0 / D, EPS, ALU.mult, ALU.add).then_inc(mean_ok, 1)
                        dve.wait_ge(root_ok, 1)
                        nc.vector.reciprocal(rs[:], sd[:]).then_inc(recip_ok, 1)
                        dve.wait_ge(recip_ok, 1)
                        dve.wait_ge(gain_in, 16)
                        for j in range(NT):
                            nc.vector.scalar_tensor_tensor(out=x_all[:, j, :], in0=x_all[:, j, :],
                                                           scalar=rs[:, j:j + 1], in1=g_bc[:], op0=ALU.mult,
                                                           op1=ALU.mult).then_inc(xn_ok, 1)
                            if j:
                                move(j - 1)
                        move(NT - 1)

                    @block.tensor
                    def _(pe):
                        for j in range(NT):
                            pe.wait_ge(xn_ok, j + 1)
                            if j >= 4:
                                pe.wait_ge(copied_lo, j - 3)
                                pe.wait_ge(copied_hi, j - 3)
                            for k in range(KD):
                                last = nc.tensor.transpose(
                                    psum[:, 2 * (j % 4) + k // 4, (k % 4) * P:(k % 4 + 1) * P],
                                    x_all[:, j, k * P:(k + 1) * P], ident[:])
                                if k == 3:
                                    last.then_inc(tr_lo, 1)
                            last.then_inc(tr_hi, 1)
                end_phase()

        @phase
        def attention_project(qkT, v):
            (proj, qk_read, squared, summed, mean_ok, root_ok, normed, turned, qk_moved, v_copied, tab_in,
             chain) = take(12)
            with ExitStack() as st:
                sq = sb(st, "sq_qk", [P, 2, 512])
                stat = sb(st, "stat_qk", [P, 3, 2, NC])
                qn = sb(st, "qn", [P, 3, 512])
                rot = sb(st, "rot", [P, NC, ROPE])
                gains = sb(st, "qk_gains", [P, 2, DK])
                cos2 = sb(st, "cos2", [P, NT, ROPE])
                sin2 = sb(st, "sin2", [P, NT, ROPE])
                STEPS = 2 * NT
                with nc.Block() as block:
                    @block.sync
                    def _(sp):
                        sp.dma_start(gains[:, 0, :], I["ev_q_norm"].partition_broadcast(P)).then_inc(tab_in, 16)
                        sp.dma_start(gains[:, 1, :], I["ev_k_norm"].partition_broadcast(P)).then_inc(tab_in, 16)
                        sp.dma_start(cos2[:], I["c_cos2"]).then_inc(tab_in, 16)
                        sp.dma_start(sin2[:], I["c_sin2"]).then_inc(tab_in, 16)
                        refill(sp, S_ATT, S_HY, proj, NT)

                    @block.tensor
                    def _(pe):
                        def turn(i):
                            pe.wait_ge(normed, i + 1)
                            if i >= 2:
                                pe.wait_ge(qk_moved, i - 1)
                            for h in range(AH):
                                last = nc.tensor.transpose(psum[:, 4 + i % 2, h * P:(h + 1) * P],
                                                           qn[:, i % 3, h * P:(h + 1) * P], ident[:])
                            last.then_inc(turned, 1)

                        for i in range(3 * NT):
                            c, j = divmod(i, NT)
                            if j == 0:
                                chunk_wait(pe, S_ATT + c)
                            if i >= 4:
                                if i - 4 < STEPS:
                                    pe.wait_ge(qk_read, i - 3)
                                else:
                                    pe.wait_ge(v_copied, i - 3 - STEPS)
                            for k in range(KD):
                                last = nc.tensor.matmul(psum[:, i % 4, :], xnT[:, k, j * P:(j + 1) * P],
                                                        wide(S_ATT + c)[:, k, :], start=(k == 0), stop=(k == KD - 1))
                            last.then_inc(proj, 1)
                            if 2 <= i <= STEPS + 1:
                                turn(i - 2)

                    @block.scalar
                    def _(act):
                        def move(i):
                            act.wait_ge(turned, i + 1)
                            c, j = divmod(i, NT)
                            nc.scalar.copy(qkT[:, c, :, j * P:(j + 1) * P],
                                           psum[:, 4 + i % 2, :].rearrange("p (h t) -> p h t", h=AH)
                                           ).then_inc(qk_moved, 1)

                        for i in range(STEPS):
                            act.wait_ge(proj, i + 1)
                            if i >= 2:
                                act.wait_ge(summed, i - 1)
                            nc.scalar.activation(sq[:, i % 2, :], psum[:, i % 4, :], ACT.Square).then_inc(squared, 1)
                            act.wait_ge(mean_ok, i + 1)
                            nc.scalar.activation(stat[:, 1, i % 2, :], stat[:, 0, i % 2, :], ACT.Sqrt,
                                                 scale=(64.0 if i < NT else 1.0)).then_inc(root_ok, 1)
                            if i >= 3:
                                move(i - 3)
                        move(STEPS - 3)
                        for j in range(NT):
                            act.wait_ge(proj, STEPS + j + 1)
                            nc.scalar.copy(v[:, j, :], psum[:, (STEPS + j) % 4, :]).then_inc(v_copied, 1)
                            if j < 2:
                                move(STEPS - 2 + j)

                    @block.vector
                    def _(dve):
                        did = Tally(chain)

                        def normalise(i):
                            c, j = divmod(i, NT)
                            q = qn[:, i % 3, :].rearrange("p (n d) -> p n d", d=DK)
                            dve.wait_ge(root_ok, i + 1)
                            n = did(nc.vector.reciprocal(stat[:, 2, i % 2, :], stat[:, 1, i % 2, :]))
                            dve.wait_ge(chain, n)
                            if i >= 3:
                                dve.wait_ge(turned, i - 2)
                            nc.vector.tensor_tensor(
                                q, psum[:, i % 4, :].rearrange("p (n d) -> p n d", d=DK),
                                stat[:, 2, i % 2, :].unsqueeze(2).broadcast_to([P, NC, DK]), ALU.mult
                            ).then_inc(qk_read, 1)
                            dve.wait_ge(qk_read, i + 1)
                            n = did(nc.vector.tensor_tensor(
                                q, q, gains[:, c, :].unsqueeze(1).broadcast_to([P, NC, DK]), ALU.mult))
                            dve.wait_ge(chain, n)
                            h = ROPE // 2
                            s = sin2[:, j, :].unsqueeze(1)
                            did(nc.vector.tensor_tensor(rot[:, :, 0:h], q[:, :, h:ROPE],
                                                        s[:, :, 0:h].broadcast_to([P, NC, h]), ALU.mult))
                            n = did(nc.vector.tensor_tensor(rot[:, :, h:ROPE], q[:, :, 0:h],
                                                            s[:, :, h:ROPE].broadcast_to([P, NC, h]), ALU.mult))
                            dve.wait_ge(chain, n)
                            n = did(nc.vector.tensor_tensor(
                                q[:, :, 0:ROPE], q[:, :, 0:ROPE],
                                cos2[:, j, :].unsqueeze(1).broadcast_to([P, NC, ROPE]), ALU.mult))
                            dve.wait_ge(chain, n)
                            nc.vector.tensor_tensor(q[:, :, 0:ROPE], q[:, :, 0:ROPE], rot[:], ALU.add
                                                    ).then_inc(normed, 1)

                        dve.wait_ge(tab_in, 64)
                        for i in range(STEPS):
                            dve.wait_ge(squared, i + 1)
                            nc.vector.tensor_reduce(
                                stat[:, 2, i % 2, :], sq[:, i % 2, :].rearrange("p (n d) -> p n d", d=DK), AX, ALU.add
                            ).then_inc(summed, 1)
                            dve.wait_ge(summed, i + 1)
                            nc.vector.tensor_scalar(stat[:, 0, i % 2, :], stat[:, 2, i % 2, :], 1.0 / DK, EPS,
                                                    ALU.mult, ALU.add).then_inc(mean_ok, 1)
                            if i:
                                normalise(i - 1)
                        normalise(STEPS - 1)
                end_phase()

        @phase
        def attention(qkT, v, o):
            (scored, max_neg, expd, comb, turned_lo, turned_hi, wt_lo, wt_hi, summed, o_copied, lam_in, lam_ok,
             chain) = take(13)
            with ExitStack() as st:
                pr = sb(st, "probs", [P, 2, 2, T])
                w = sb(st, "attn_w", [P, 2, T])
                wT = sb(st, "attn_wT", [P, 2, NT, P])
                nmx = sb(st, "neg_max", [P, 2, 2])
                l = sb(st, "row_sum", [P, 2, 2])
                r = sb(st, "row_recip", [P, 2, 2])
                lam = sb(st, "lam", [P, 4, DK])
                lp = sb(st, "lam_prod", [P, 2, DK])
                ls = sb(st, "lam_sum", [P, 4])
                STEPS = AH * NT
                LAG = 2
                TB, OB = 6, 7

                def pair(u):
                    b = 2 * (u % 3)
                    return psum[:, b:b + 2, :].rearrange("p a b -> p (a b)")

                with nc.Block() as block:
                    @block.sync
                    def _(sp):
                        for n, name in enumerate(("ev_lam_q1", "ev_lam_q2", "ev_lam_k1", "ev_lam_k2")):
                            sp.dma_start(lam[:, n, :], I[name].partition_broadcast(P)).then_inc(lam_in, 16)
                        for n in range(OVER * P // 640):
                            sp.dma_start(y_d[NE * P + 640 * n:NE * P + 640 * (n + 1), :], I["x"][0:640, :]
                                         ).then_inc(y_filled, 16)

                    @block.tensor
                    def _(pe):
                        def scores(u):
                            i, c = divmod(u, 2)
                            h, j = divmod(i, NT)
                            if u >= 3:
                                pe.wait_ge(expd, u - 2)
                            rows = slice(c * DK, (c + 1) * DK)
                            for half in range(2):
                                last = nc.tensor.matmul(psum[:, 2 * (u % 3) + half, :],
                                                        qkT[rows, 0, h, j * P:(j + 1) * P],
                                                        qkT[rows, 1, h, half * 512:(half + 1) * 512],
                                                        start=True, stop=True)
                            last.then_inc(scored, 1)

                        def turn(i, half):
                            if half == 0:
                                pe.wait_ge(comb, i + 1)
                                if i:
                                    pe.wait_ge(wt_hi, i)
                            else:
                                pe.wait_ge(wt_lo, i + 1)
                            for k in range(4):
                                last = nc.tensor.transpose(psum[:, TB, k * P:(k + 1) * P],
                                                           w[:, i % 2, (4 * half + k) * P:(4 * half + k + 1) * P],
                                                           ident[:])
                            last.then_inc(turned_hi if half else turned_lo, 1)

                        def values(i):
                            h, j = divmod(i, NT)
                            pe.wait_ge(wt_hi, i + 1)
                            if i:
                                pe.wait_ge(o_copied, i)
                            for k in range(NT):
                                last = nc.tensor.matmul(psum[:, OB, (i % 2) * DV:(i % 2 + 1) * DV], wT[:, i % 2, k, :],
                                                        v[:, k, h * DV:(h + 1) * DV], start=(k == 0), stop=(k == NT - 1))
                            last.then_inc(summed, 1)

                        for i in range(STEPS + LAG):
                            late = i - LAG
                            if late >= 0:
                                turn(late, 0)
                            if i < STEPS:
                                scores(2 * i)
                            if late >= 0:
                                turn(late, 1)
                            if i < STEPS:
                                scores(2 * i + 1)
                            if late >= 0:
                                values(late)

                    @block.vector
                    def _(dve):
                        did = Tally(chain)
                        dve.wait_ge(lam_in, 64)
                        n = did(nc.vector.tensor_tensor(lp[:], lam[:, 0:2, :], lam[:, 2:4, :], ALU.mult))
                        dve.wait_ge(chain, n)
                        nc.vector.tensor_reduce(ls[:, 0:2], lp[:], AX, ALU.add).then_inc(lam_ok, 1)
                        dve.wait_ge(lam_ok, 2)
                        n = did(nc.vector.tensor_tensor(ls[:, 0:1], ls[:, 3:4], ls[:, 2:3], ALU.subtract))
                        dve.wait_ge(chain, n)
                        lam_init = 0.8 - 0.6
                        n = did(nc.vector.tensor_scalar(ls[:, 1:2], ls[:, 0:1], -lam_init, None, ALU.add))
                        dve.wait_ge(chain, n)

                        def row_max(u):
                            i, c = divmod(u, 2)
                            dve.wait_ge(scored, u + 1)
                            if u >= 4:
                                dve.wait_ge(expd, u - 3)
                            nc.vector.tensor_reduce(nmx[:, i % 2, c:c + 1], pair(u), AX, ALU.max, negate=True
                                                    ).then_inc(max_neg, 1)

                        def combine(i):
                            b = i % 2
                            dve.wait_ge(expd, 2 * i + 2)
                            n = did(nc.vector.reciprocal(r[:, b, :], l[:, b, :]))
                            dve.wait_ge(chain, n)
                            n = did(nc.vector.tensor_tensor(r[:, b, 1:2], r[:, b, 1:2], ls[:, 1:2], ALU.mult))
                            dve.wait_ge(chain, n)
                            n = did(nc.vector.tensor_scalar(pr[:, b, 1, :], pr[:, b, 1, :], r[:, b, 1:2], None, ALU.mult))
                            dve.wait_ge(chain, n)
                            if i >= 2:
                                dve.wait_ge(turned_hi, i - 1)
                            nc.vector.scalar_tensor_tensor(out=w[:, b, :], in0=pr[:, b, 0, :], scalar=r[:, b, 0:1],
                                                           in1=pr[:, b, 1, :], op0=ALU.mult, op1=ALU.add
                                                           ).then_inc(comb, 1)

                        def move(i):
                            dve.wait_ge(turned_hi, i + 1)
                            if i >= 2:
                                dve.wait_ge(summed, i - 1)
                            nc.vector.tensor_copy(wT[:, i % 2, 4:8, :].rearrange("p k t -> p (k t)"), psum[:, TB, :]
                                                  ).then_inc(wt_hi, 1)

                        for i in range(STEPS + LAG):
                            if i < STEPS:
                                row_max(2 * i)
                            if 1 <= i <= STEPS:
                                combine(i - 1)
                            if i >= LAG:
                                move(i - LAG)
                            if i < STEPS:
                                row_max(2 * i + 1)

                    @block.scalar
                    def _(act):
                        act.wait_ge(lam_ok, 1)
                        nc.scalar.activation(ls[:, 2:4], ls[:, 0:2], ACT.Exp).then_inc(lam_ok, 1)

                        def expo(u):
                            i, c = divmod(u, 2)
                            act.wait_ge(max_neg, u + 1)
                            if i >= 2:
                                act.wait_ge(comb, i - 1)
                            nc.scalar.activation(pr[:, i % 2, c, :], pair(u), ACT.Exp, bias=nmx[:, i % 2, c:c + 1],
                                                 accum_out=l[:, i % 2, c:c + 1]).then_inc(expd, 1)

                        def move(i):
                            act.wait_ge(turned_lo, i + 1)
                            if i >= 2:
                                act.wait_ge(summed, i - 1)
                            nc.scalar.copy(wT[:, i % 2, 0:4, :].rearrange("p k t -> p (k t)"), psum[:, TB, :]
                                           ).then_inc(wt_lo, 1)

                        def keep(i):
                            h, j = divmod(i, NT)
                            act.wait_ge(summed, i + 1)
                            nc.scalar.copy(o[:, j, h * DV:(h + 1) * DV], psum[:, OB, (i % 2) * DV:(i % 2 + 1) * DV]
                                           ).then_inc(o_copied, 1)

                        for i in range(STEPS + LAG):
                            if i >= LAG:
                                move(i - LAG)
                            if i < STEPS:
                                expo(2 * i)
                            if i >= LAG + 1:
                                keep(i - LAG - 1)
                            if i < STEPS:
                                expo(2 * i + 1)
                        keep(STEPS - 1)
                end_phase()

        @phase
        def head_norm(name, o, heads, width, gain, post, gate, yT):
            (gain_in, gate_in0, gate_in1, squared, summed, mean_ok, root_ok, scaled, turned, copied,
             chain) = take(11)
            gate_in = (gate_in0, gate_in1)
            W = heads * width
            banks = W // 512
            with ExitStack() as st:
                sq = sb(st, f"sq_{name}", [P, 2, W])
                ss = sb(st, f"ss_{name}", [P, NT, heads])
                sd = sb(st, f"sd_{name}", [P, NT, heads])
                g_bc = sb(st, f"g_{name}", [P, W])
                gt = sb(st, f"gate_{name}", [P, 2, W]) if gate is not None else None
                with nc.Block() as block:
                    @block.sync
                    def _(sp):
                        sp.dma_start(g_bc[:].rearrange("p (h w) -> p h w", w=gain.shape[-1]),
                                     gain.partition_broadcast(P)).then_inc(gain_in, 16)
                        if gate is not None:
                            for j in range(NT):
                                if j >= 2:
                                    sp.wait_ge(scaled, j - 1)
                                sp.dma_start(gt[:, j % 2, :], gate[j * P:(j + 1) * P, :]
                                             ).then_inc(gate_in[j % 2], 16)

                    @block.scalar
                    def _(act):
                        for j in range(NT):
                            if j >= 2:
                                act.wait_ge(summed, j - 1)
                            nc.scalar.activation(sq[:, j % 2, :], o[:, j, :], ACT.Square).then_inc(squared, 1)
                        act.wait_ge(mean_ok, 1)
                        nc.scalar.activation(sd[:], ss[:], ACT.Sqrt).then_inc(root_ok, 1)
                        for j in range(NT):
                            for b in range(banks):
                                act.wait_ge(turned, j * banks + b + 1)
                                nc.scalar.copy(yT[:, 4 * b:4 * b + 4, j * P:(j + 1) * P],
                                               psum[:, (j * banks + b) % 4, :].rearrange("p (k t) -> p k t", k=4)
                                               ).then_inc(copied, 1)

                    @block.vector
                    def _(dve):
                        did = Tally(chain)
                        for j in range(NT):
                            dve.wait_ge(squared, j + 1)
                            nc.vector.tensor_reduce(ss[:, j, :], sq[:, j % 2, :].rearrange("p (h w) -> p h w", h=heads),
                                                    AX, ALU.add).then_inc(summed, 1)
                        dve.wait_ge(summed, NT)
                        nc.vector.tensor_scalar(ss[:], ss[:], 1.0 / width, EPS, ALU.mult, ALU.add).then_inc(mean_ok, 1)
                        dve.wait_ge(gain_in, 16)
                        if post != 1.0:
                            n = did(nc.vector.tensor_scalar(g_bc[:], g_bc[:], post, None, ALU.mult))
                        dve.wait_ge(root_ok, 1)
                        n = did(nc.vector.reciprocal(sd[:], sd[:]))
                        dve.wait_ge(chain, n)
                        for j in range(NT):
                            for h in range(heads):
                                cols = slice(h * width, (h + 1) * width)
                                ins = nc.vector.scalar_tensor_tensor(out=o[:, j, cols], in0=o[:, j, cols],
                                                                     scalar=sd[:, j, h:h + 1], in1=g_bc[:, cols],
                                                                     op0=ALU.mult, op1=ALU.mult)
                                if gate is not None:
                                    n = did(ins)
                            if gate is None:
                                ins.then_inc(scaled, 1)
                            else:
                                dve.wait_ge(chain, n)
                                dve.wait_ge(gate_in[j % 2], 16 * (j // 2 + 1))
                                nc.vector.tensor_tensor(o[:, j, :], o[:, j, :], gt[:, j % 2, :], ALU.mult
                                                        ).then_inc(scaled, 1)

                    @block.tensor
                    def _(pe):
                        for j in range(NT):
                            pe.wait_ge(scaled, j + 1)
                            for b in range(banks):
                                n = j * banks + b
                                if n >= 4:
                                    pe.wait_ge(copied, n - 3)
                                for k in range(4):
                                    last = nc.tensor.transpose(psum[:, n % 4, k * P:(k + 1) * P],
                                                               o[:, j, (4 * b + k) * P:(4 * b + k + 1) * P], ident[:])
                                last.then_inc(turned, 1)
                end_phase()

        @phase
        def out_phase(name, yT, s0, xsrc, xdst):
            (x_in, proj, added, stored) = take(4)
            with ExitStack() as st:
                x_all = sb(st, f"x_res{name}", [P, NT, D])
                rows = xsrc.rearrange("(j p) d -> p j d", p=P)
                dst = xdst.rearrange("(j p) d -> p j d", p=P)
                STEPS = 2 * NT
                with nc.Block() as block:
                    @block.sync
                    def _(sp):
                        sp.dma_start(x_all[:], rows).then_inc(x_in, 16)
                        refill(sp, s0, s0 + 2, proj, NT)

                    @block.scalar
                    def _(act):
                        for i in range(STEPS):
                            c, j = divmod(i, NT)
                            act.wait_ge(added, i + 1)
                            act.dma_start(dst[:, j, c * 512:(c + 1) * 512], x_all[:, j, c * 512:(c + 1) * 512]
                                             ).then_inc(stored, 16)
                        act.wait_ge(stored, 16 * STEPS)

                    @block.tensor
                    def _(pe):
                        for i in range(STEPS):
                            c, j = divmod(i, NT)
                            if j == 0:
                                chunk_wait(pe, s0 + c)
                            if i >= 8:
                                pe.wait_ge(added, i - 7)
                            for k in range(KD):
                                last = nc.tensor.matmul(psum[:, i % 8, :], yT[:, k, j * P:(j + 1) * P],
                                                        wide(s0 + c)[:, k, :], start=(k == 0), stop=(k == KD - 1))
                            last.then_inc(proj, 1)

                    @block.vector
                    def _(dve):
                        dve.wait_ge(x_in, 16)
                        for i in range(STEPS):
                            c, j = divmod(i, NT)
                            dve.wait_ge(proj, i + 1)
                            xp = x_all[:, j, c * 512:(c + 1) * 512]
                            nc.vector.tensor_tensor(xp, xp, psum[:, i % 8, :], ALU.add).then_inc(added, 1)
                end_phase()

        @phase
        def hyena_project(z, yT):
            (proj, padded, convolved, weights_in, edges, chain) = take(6)
            with ExitStack() as st:
                up = sb(st, "u_padded", [P, 2, T + 2])
                acc = sb(st, "conv_acc", [P, 2, T])
                cw = sb(st, "hy_conv_w", [P, 3 * HC, 3])
                cb = sb(st, "hy_conv_b", [P, 3 * HC])
                STEPS = 3 * HC
                with nc.Block() as block:
                    @block.sync
                    def _(sp):
                        sp.dma_start(cw[:], I["hy_conv_w"]).then_inc(weights_in, 16)
                        sp.dma_start(cb[:], I["hy_conv_b"]).then_inc(weights_in, 16)
                        refill(sp, S_HY, S_OUT0, proj, HC)

                    @block.tensor
                    def _(pe):
                        for i in range(STEPS):
                            c, ct = divmod(i, HC)
                            if ct == 0:
                                chunk_wait(pe, S_HY + c)
                            if i >= 4:
                                pe.wait_ge(padded, i - 3)
                            for half in range(2):
                                for k in range(KD):
                                    last = nc.tensor.matmul(psum[:, 2 * (i % 4) + half, :],
                                                            wide(S_HY + c)[:, k, ct * P:(ct + 1) * P],
                                                            xnT[:, k, half * 512:(half + 1) * 512],
                                                            start=(k == 0), stop=(k == KD - 1))
                            last.then_inc(proj, 1)

                    @block.scalar
                    def _(act):
                        for i in range(STEPS):
                            act.wait_ge(proj, i + 1)
                            if i >= 2:
                                act.wait_ge(convolved, i - 1)
                            nc.scalar.copy(up[:, i % 2, 1:T + 1],
                                           psum[:, 2 * (i % 4):2 * (i % 4) + 2, :].rearrange("p a b -> p (a b)")
                                           ).then_inc(padded, 1)

                    @block.vector
                    def _(dve):
                        did = Tally(chain)
                        nc.vector.memset(up[:, :, 0:1], 0.0).then_inc(edges, 1)
                        nc.vector.memset(up[:, :, T + 1:T + 2], 0.0).then_inc(edges, 1)
                        dve.wait_ge(edges, 2)
                        dve.wait_ge(weights_in, 32)
                        for i in range(STEPS):
                            c, ct = divmod(i, HC)
                            n = (2 - c) * HC + ct
                            a, u = acc[:, i % 2, :], up[:, i % 2, :]
                            dve.wait_ge(padded, i + 1)
                            m = did(nc.vector.tensor_scalar(a, u[:, 0:T], cw[:, n, 0:1], cb[:, n:n + 1],
                                                            ALU.mult, ALU.add))
                            dve.wait_ge(chain, m)
                            m = did(nc.vector.scalar_tensor_tensor(out=a, in0=u[:, 1:T + 1], scalar=cw[:, n, 1:2],
                                                                   in1=a, op0=ALU.mult, op1=ALU.add))
                            dve.wait_ge(chain, m)
                            dst = (z[:, ct, :], a, yT[:, 4 + ct, :])[c]
                            nc.vector.scalar_tensor_tensor(out=dst, in0=u[:, 2:T + 2], scalar=cw[:, n, 2:3],
                                                           in1=a, op0=ALU.mult, op1=ALU.add).then_inc(convolved, 1)
                            if c == 1:
                                dve.wait_ge(convolved, i + 1)
                                nc.vector.tensor_tensor(z[:, ct, :], z[:, ct, :], a, ALU.mult).then_inc(chain, 1)
                                did.n += 1
                end_phase()

        @phase
        def hyena_filter(z, zT, hs, hd, hinv):
            (tab_in, lin, argued, waved, filt, decayed, mixed, normed, turned, moved, skipped, chain,
             row_ok, summed, patched) = take(15)
            with ExitStack() as st:
                zp = sb(st, "hy_positions", [EMB, T])
                w1 = sb(st, "hy_w1", [EMB, FF])
                w2 = sb(st, "hy_w2", [FF, FF])
                w3 = sb(st, "hy_w3", [FF, 2 * 512])
                fb = sb(st, "hy_fb", [FF, 3])
                tneg = sb(st, "hy_tneg", [P, NT])
                delta = sb(st, "hy_delta", [P, 512])
                skip = sb(st, "hy_skip", [P, HC])
                arg = sb(st, "hy_arg", [FF, T])
                turns = sb(st, "hy_turns", [FF, T])
                hdn = sb(st, "hy_hidden", [FF, T])
                dec = sb(st, "hy_decay", [P, 2, 512])
                hf = sb(st, "hy_fwd", [P, 2, 512])
                hb = sb(st, "hy_bwd", [P, 2, 512])
                ab = sb(st, "hy_abs", [P, 2, 2, 512])
                row = sb(st, "hy_row", [1, 512])
                TWO_PI = 2 * np.pi
                HI = 6.28125
                LO = TWO_PI - HI
                MAGIC = 1.5 * 2.0 ** 23
                with nc.Block() as block:
                    @block.sync
                    def _(sp):
                        for t, src in ((zp[:], I["c_positions"]), (w1[:], I["hy_w1"]), (w2[:], I["hy_w2"]),
                                       (w3[:], I["hy_w3"]), (fb[:], I["hy_fb"]), (tneg[:], I["c_tneg"]),
                                       (delta[:], I["c_delta"].partition_broadcast(P)), (skip[:], I["hy_skip"])):
                            sp.dma_start(t, src).then_inc(tab_in, 16)

                    @block.tensor
                    def _(pe):
                        def layer(w, x):
                            for half in range(2):
                                last = nc.tensor.matmul(psum[0:FF, half, :], w[:], x[:, half * 512:(half + 1) * 512],
                                                        start=True, stop=True)
                            last.then_inc(lin, 1)

                        def turn(n):
                            par, mt = divmod(n, NF)
                            if n >= 4:
                                pe.wait_ge(moved, n - 3)
                            for ct in range(HC):
                                t0 = par + 2 * mt * P
                                last = nc.tensor.transpose(psum[:, 4 + n % 4, ct * P:(ct + 1) * P],
                                                           z[:, ct, t0:t0 + 2 * P - 1:2], ident[:])
                            last.then_inc(turned, 1)

                        pe.wait_ge(tab_in, 16 * 8)
                        layer(w1, zp)
                        for n in range(4):
                            turn(n)
                        pe.wait_ge(waved, 1)
                        layer(w2, hdn)
                        for n in range(4, NT):
                            turn(n)
                        pe.wait_ge(waved, 2)
                        pe.wait_ge(moved, NT)

                        def norm_sum(n):
                            pe.wait_ge(mixed, n + 2)
                            for d in range(2):
                                last = nc.tensor.matmul(psum[0:1, 4, :], ones[:, 0:1], ab[:, n % 2, d, :],
                                                        start=(n == 0 and d == 0), stop=(n == NT - 1 and d == 1))
                            last.then_inc(normed, 1)

                        for n in range(NT):
                            par, mt = divmod(n, NF)
                            t0 = par + 2 * mt * P
                            if n >= 2:
                                pe.wait_ge(summed, n - 1)
                            for half in range(2):
                                last = nc.tensor.matmul(psum[:, 2 * (n % 2) + half, :], hdn[:, t0:t0 + 2 * P - 1:2],
                                                        w3[:, half * 512:(half + 1) * 512], start=True, stop=True)
                            last.then_inc(filt, 1)
                            if n:
                                norm_sum(n - 1)
                        norm_sum(NT - 1)
                        pe.wait_ge(row_ok, 1)
                        for ct in range(HC):
                            last = nc.tensor.matmul(psum[:, 5, ct:ct + 1], row[0:1, ct * P:(ct + 1) * P],
                                                    ones[0:1, 0:1], start=True, stop=True)
                        last.then_inc(normed, 1)

                    @block.gpsimd
                    def _(pool_e):
                        pool_e.wait_ge(patched, 2)
                        nc.gpsimd.memset(ab[0:1, 0, 1, :], 0.0).then_inc(mixed, 1)

                    @block.scalar
                    def _(act):
                        def size(n):
                            b = n % 2
                            act.wait_ge(summed, n + 1)
                            if n >= 2:
                                act.wait_ge(normed, n - 1)
                            for d, h in ((0, hf), (1, hb)):
                                ins = nc.scalar.activation(ab[:, b, d, :], h[:, b, :], ACT.Abs)
                                if n == 0:
                                    ins.then_inc(patched, 1)
                            if n:
                                ins.then_inc(mixed, 1)
                            else:
                                act.wait_ge(patched, 2)
                                act.wait_ge(mixed, 1)
                                nc.scalar.activation(ab[0:1, 0, 0, :], hs[0:1, 0, :], ACT.Abs).then_inc(mixed, 1)

                        act.wait_ge(tab_in, 16 * 8)
                        for k in range(2):
                            act.wait_ge(argued, k + 1)
                            nc.scalar.activation(hdn[:], arg[:], ACT.Sin).then_inc(waved, 1)
                            for n in range(4 * k, 4 * k + 4):
                                act.wait_ge(turned, n + 1)
                                nc.scalar.copy(zT[:, n, :], psum[:, 4 + n % 4, :]).then_inc(moved, 1)
                        for ct in range(HC):
                            act.wait_ge(turned, NT)
                            nc.scalar.activation(z[:, ct, :], z[:, ct, :], ACT.Copy, scale=skip[:, ct:ct + 1]
                                                 ).then_inc(skipped, 1)
                        for n in range(NT):
                            if n >= 2:
                                act.wait_ge(summed, n - 1)
                            nc.scalar.activation(dec[:, n % 2, :], delta[:], ACT.Exp, scale=tneg[:, n:n + 1]
                                                 ).then_inc(decayed, 1)
                            if n:
                                size(n - 1)
                        size(NT - 1)

                    @block.vector
                    def _(dve):
                        did = Tally(chain)

                        def step(ins):
                            dve.wait_ge(chain, did(ins))

                        dve.wait_ge(tab_in, 16 * 8)
                        for k in range(2):
                            dve.wait_ge(lin, k + 1)
                            if k:
                                dve.wait_ge(waved, 1)
                            step(nc.vector.tensor_scalar(
                                arg[:], psum[0:FF, 0:2, :].rearrange("p a b -> p (a b)"),
                                fb[:, 2 * k:2 * k + 1], fb[:, 1:2], ALU.add, ALU.mult))
                            step(nc.vector.tensor_scalar(turns[:], arg[:], 1 / TWO_PI, MAGIC, ALU.mult, ALU.add))
                            step(nc.vector.tensor_scalar(turns[:], turns[:], -MAGIC, None, ALU.add))
                            step(nc.vector.scalar_tensor_tensor(out=arg[:], in0=turns[:], scalar=-HI, in1=arg[:],
                                                                op0=ALU.mult, op1=ALU.add))
                            step(nc.vector.scalar_tensor_tensor(out=arg[:], in0=turns[:], scalar=-LO, in1=arg[:],
                                                                op0=ALU.mult, op1=ALU.add))
                            nc.vector.tensor_scalar(arg[:], arg[:], 3.1415925, -3.1415925, ALU.min, ALU.max
                                                    ).then_inc(argued, 1)
                        for n in range(NT):
                            b = n % 2
                            dve.wait_ge(filt, n + 1)
                            dve.wait_ge(decayed, n + 1)
                            if n >= 2:
                                dve.wait_ge(mixed, n)
                            did(nc.vector.tensor_tensor(hf[:, b, :], psum[:, 2 * b, :], dec[:, b, :], ALU.mult))
                            step(nc.vector.tensor_tensor(hb[:, b, :], psum[:, 2 * b + 1, :], dec[:, b, :], ALU.mult))
                            step(nc.vector.tensor_tensor(hs[:, n, :], hf[:, b, :], hb[:, b, :], ALU.add))
                            nc.vector.tensor_tensor(hd[:, n, :], hf[:, b, :], hb[:, b, :], ALU.subtract).then_inc(summed, 1)
                        dve.wait_ge(normed, NT)
                        nc.vector.tensor_scalar(row[:], psum[0:1, 4, :], EPS, None, ALU.add).then_inc(row_ok, 1)
                        dve.wait_ge(normed, NT + 1)
                        nc.vector.reciprocal(hinv[:], psum[:, 5, 0:HC]).then_inc(row_ok, 1)
                end_phase()

        @phase
        def hyena_forward(zT, hs, hd, Z):
            (piece_in, zed, keyed, edged, copied, mixed, used, chain) = take(8)
            BUFS = 4
            piece_ins = pool[8:8 + BUFS]
            with ExitStack() as st:
                tab = sb(st, "dft_tables", [P, BUFS, NF, P])
                acc = sb(st, "freq_acc", [P, 4, 512])
                tmp = sb(st, "freq_tmp", [P, 4, 512])
                PIECES = NF * 4
                with nc.Block() as block:
                    @block.sync
                    def _(sp):
                        for n in range(PIECES):
                            if n >= BUFS:
                                sp.wait_ge(used, n - BUFS + 1)
                            sp.dma_start(tab[:, n % BUFS, :, :], I["c_dft"][n // 4, :, n % 4, :, :]
                                         ).then_inc(piece_ins[n % BUFS], 16)

                    @block.tensor
                    def _(pe):
                        for kt in range(NF):
                            for t in range(4):
                                n = kt * 4 + t
                                par = t % 2
                                pe.wait_ge(piece_ins[n % BUFS], 16 * (n // BUFS + 1))
                                if kt:
                                    pe.wait_ge(copied, 4 * (kt - 1) + t + 1)
                                if n == 4:
                                    pe.wait_ge(mixed, 1)
                                for m in range(NF):
                                    last = nc.tensor.matmul(psum[:, t, :], tab[:, n % BUFS, m, :],
                                                            zT[:, par * NF + m, :], start=(m == 0), stop=(m == NF - 1))
                                last.then_inc(zed, 1)
                                if kt:
                                    pe.wait_ge(mixed, kt)
                                h = hs if t < 2 else hd
                                for m in range(NF):
                                    last = nc.tensor.matmul(psum[:, 4 + t, :], tab[:, n % BUFS, m, :],
                                                            h[:, par * NF + m, :], start=(m == 0), stop=(m == NF - 1))
                                if n == 2:
                                    last.then_inc(keyed, 1)
                                    pe.wait_ge(copied, 1)
                                    for m in range(NF):
                                        last = nc.tensor.matmul(psum[0:1, 0, :], tab[:, n % BUFS, m, 0:1],
                                                                hs[:, m, :], start=(m == 0), stop=(m == NF - 1))
                                last.then_inc(used, 1)

                    @block.scalar
                    def _(act):
                        for n in range(PIECES):
                            act.wait_ge(zed, n + 1)
                            nc.scalar.copy(Z[:, n % 4, n // 4, :], psum[:, n % 4, :]).then_inc(copied, 1)

                    @block.vector
                    def _(dve):
                        did = Tally(chain)
                        terms = [
                            [(0, 0, 1), (1, 1, 1), (2, 2, -1), (3, 3, -1)],
                            [(0, 1, 1), (1, 0, 1), (2, 3, -1), (3, 2, -1)],
                            [(0, 2, 1), (1, 3, 1), (2, 0, 1), (3, 1, 1)],
                            [(0, 3, 1), (1, 2, 1), (2, 1, 1), (3, 0, 1)],
                        ]
                        for kt in range(NF):
                            dve.wait_ge(copied, 4 * kt + 4)
                            dve.wait_ge(used, 4 * kt + 4)
                            q, lo = psum[0:1, 0, :], psum[0:1, 7, :]
                            se, so = Z[0:1, 2, kt, :], Z[0:1, 3, kt, :]
                            for s in range(4):
                                dst = acc if s == 0 else tmp
                                for o in range(4):
                                    zi, ki, _s = terms[o][s]
                                    n = did(nc.vector.tensor_tensor(dst[:, o, :], Z[:, zi, kt, :], psum[:, 4 + ki, :],
                                                                    ALU.mult))
                                dve.wait_ge(chain, n)
                                if kt == 0:
                                    zero = (2, 3) if s < 2 else (0, 1)
                                    for o in zero:
                                        n = did(nc.vector.memset(dst[0:1, o, :], 0.0))
                                    if s == 2:
                                        did(nc.vector.tensor_tensor(tmp[0:1, 2, :], se, q, ALU.mult))
                                        n = did(nc.vector.tensor_tensor(tmp[0:1, 3, :], se, lo, ALU.mult))
                                    if s == 3:
                                        did(nc.vector.scalar_tensor_tensor(out=tmp[0:1, 2, :], in0=so, scalar=-1.0,
                                                                           in1=lo, op0=ALU.mult, op1=ALU.mult))
                                        n = did(nc.vector.tensor_tensor(tmp[0:1, 3, :], so, q, ALU.mult))
                                    dve.wait_ge(chain, n)
                                if s:
                                    for o in range(4):
                                        op = ALU.add if terms[o][s][2] > 0 else ALU.subtract
                                        into = Z[:, o, kt, :] if s == 3 else acc[:, o, :]
                                        ins = nc.vector.tensor_tensor(into, acc[:, o, :], tmp[:, o, :], op)
                                        if s == 3 and o == 3:
                                            ins.then_inc(mixed, 1)
                                        else:
                                            n = did(ins)
                                    dve.wait_ge(chain, n)
                end_phase()

        @phase
        def hyena_inverse(z, Z, hinv, yT):
            (tab_a, tab_b, back, added, gated) = take(5)
            with ExitStack() as st:
                y = sb(st, "hy_y", [P, 2, 512])
                itab = xnT[:].rearrange("p k t -> p (k t)").rearrange("p (s k m) -> p s k m", s=4, k=NF)
                with nc.Block() as block:
                    @block.sync
                    def _(sp):
                        for par, got in ((0, tab_a), (1, tab_b)):
                            for s in (par, 2 + par):
                                sp.dma_start(itab[:, s, :, :], I["c_idft"][s]).then_inc(got, 16)

                    @block.tensor
                    def _(pe):
                        for i in range(2 * HC):
                            par, ct = divmod(i, HC)
                            pe.wait_ge(tab_b if par else tab_a, 32)
                            for n, (s, kt) in enumerate([(s, kt) for s in (par, 2 + par) for kt in range(NF)]):
                                last = nc.tensor.matmul(psum[:, i, :], Z[:, s, kt, ct * P:(ct + 1) * P],
                                                        itab[:, s, kt, :], start=(n == 0), stop=(n == 2 * NF - 1))
                            last.then_inc(back, 1)

                    @block.vector
                    def _(dve):
                        for i in range(2 * HC):
                            par, ct = divmod(i, HC)
                            dve.wait_ge(back, i + 1)
                            nc.vector.scalar_tensor_tensor(out=y[:, i % 2, :], in0=psum[:, i, :],
                                                           scalar=hinv[:, ct:ct + 1], in1=z[:, ct, par:T:2],
                                                           op0=ALU.mult, op1=ALU.add).then_inc(added, 1)
                            dve.wait_ge(added, i + 1)
                            g = yT[:, 4 + ct, par:T:2]
                            nc.vector.tensor_tensor(g, g, y[:, i % 2, :], ALU.mult).then_inc(gated, 1)
                end_phase()

        @phase
        def router(layer, row_of, gates, slots, ctrl):
            (tab_in, logit_ok, shifted, expd, picked, placed, marked, listed, chain) = take(9)
            with ExitStack() as st:
                name = str(layer)

                def t(n, shape, dt=F32):
                    return sb(st, f"r{name}_{n}", shape, dt)

                wr = t("w", [P, KD, NG + NE])
                br = t("b", [P, NG + NE])
                cst = t("cst", [P, NG + EG + NE + 7 + P + NBLKP + 16])
                tok = t("tok", [P, NT])
                at = [0]

                def piece(n):
                    at[0] += n
                    return cst[:, at[0] - n:at[0]]

                desc4, desc8, e32, thr, s128, b48, i16 = (piece(n) for n in (NG, EG, NE, 7, P, NBLKP, 16))
                L = t("logits", [P, NT, NG + NE])
                g, el = L[:, :, 0:NG], L[:, :, NG:NG + NE]
                gm = t("gm", [P, NT])
                gi = t("gi", [P, NT, NG])
                ohg = t("ohg", [P, NT, NG])
                m = t("m", [P, NT])
                ex = t("ex", [P, NT, NG + 1])
                gw = t("gw", [P, NT])
                sel = t("sel", [P, NT, NG, EG])
                se = t("se", [P, 2, NT, EG])
                mm = t("mm", [P, 2, NT])
                idx = t("idx", [P, NT, EG])
                oh = t("oh", [P, 2, NT, EG])
                M = t("M", [P, 3, NT, NG, EG])
                pos = t("pos", [P, NT, NE])
                tot = t("tot", [P, NT, NE])
                off = t("off", [P, NT + 1, NE])
                cmp = t("cmp", [P, NE, 16])
                sel3 = t("sel3", [P, NE, 16])
                nov = t("nov", [P, NE])
                incl = t("incl", [P, NE])
                base = t("base", [P, NE])
                big = t("big", [P, NT, NE])
                F = t("F", [P, 3, 2, NT])
                hi = t("hi", [P, 16])
                over = t("over", [P, 16])
                alt = t("alt", [P, 16])
                blk = t("blk", [P, 16])
                r = t("r", [P, 16])
                cmp2 = t("cmp2", [P, 16, 7])
                A = t("A", [P, 16, P])
                B = t("B", [P, 16, NBLKP])
                eov = t("eov", [P, 16])
                with nc.Block() as block:
                    @block.sync
                    def _(sp):
                        for dst, src in ((wr, I["r_w"][layer]), (br, I["r_b"][layer].partition_broadcast(P)),
                                         (cst, I["c_router"].partition_broadcast(P)), (tok, I["c_tok"])):
                            sp.dma_start(dst[:], src).then_inc(tab_in, 16)
                        sp.wait_ge(y_filled, 16 * (OVER * P // 640))

                    @block.tensor
                    def _(pe):
                        pe.wait_ge(tab_in, 64)
                        for j in range(NT):
                            for k in range(KD):
                                last = nc.tensor.matmul(psum[:, 0, j * 36:(j + 1) * 36], xnT[:, k, j * P:(j + 1) * P],
                                                        wr[:, k, :], start=(k == 0), stop=(k == KD - 1))
                        last.then_inc(logit_ok, 1)
                        pe.wait_ge(picked, 1)
                        both = M[:, 2, :, :, :].rearrange("p j g e -> p (j g e)")
                        nc.tensor.matmul(psum[:, 1, 0:NT * NE], upper[:], both, start=True, stop=True)
                        nc.tensor.matmul(psum[:, 2, 0:NT * NE], ones[:], both, start=True, stop=True
                                         ).then_inc(placed, 1)
                        pe.wait_ge(marked, 1)
                        for n in range(16):
                            last = nc.tensor.matmul(psum[:, 3, 0:NBLKP], A[:, n, :], B[:, n, :],
                                                    start=(n == 0), stop=(n == 15))
                        last.then_inc(listed, 1)

                    @block.scalar
                    def _(act):
                        act.wait_ge(shifted, 1)
                        nc.scalar.activation(ex[:], ex[:], ACT.Exp).then_inc(expd, 1)

                    @block.vector
                    def _(dve):
                        did = Tally(chain)
                        V = nc.vector

                        def step(ins):
                            dve.wait_ge(chain, did(ins))

                        def rows(a, n):
                            return a.unsqueeze(1).broadcast_to([P, NT, n])

                        def cols(a, n):
                            return a.unsqueeze(2).broadcast_to([P, NT, n])

                        dve.wait_ge(tab_in, 64)
                        dve.wait_ge(logit_ok, 1)
                        step(V.tensor_tensor(L[:], psum[:, 0, 0:NT * 36].rearrange("p (j c) -> p j c", j=NT),
                                             rows(br[:], 36), ALU.add))
                        step(V.tensor_reduce(gm[:], g, AX, ALU.max))

                        def first_max(out, vals, top, desc, scratch, n):
                            step(V.tensor_tensor(scratch, vals, cols(top, n), ALU.is_equal))
                            step(V.tensor_tensor(scratch, scratch, rows(desc, n), ALU.mult))
                            step(V.tensor_reduce(m[:], scratch, AX, ALU.max))
                            step(V.tensor_tensor(out, scratch, cols(m[:], n), ALU.is_equal))

                        first_max(ohg[:], g, gm[:], desc4, gi[:], NG)
                        step(V.tensor_tensor(ex[:, :, 0:NG], g, cols(gm[:], NG), ALU.subtract))
                        ohg8 = ohg[:].unsqueeze(3).broadcast_to([P, NT, NG, EG])
                        step(V.tensor_tensor(sel[:], el.rearrange("p j (g e) -> p j g e", g=NG), ohg8, ALU.mult))
                        step(V.tensor_reduce(se[:, 0, :, :], sel[:].rearrange("p j g e -> p j e g"), AX, ALU.add))
                        step(V.tensor_reduce(mm[:, 0, :], se[:, 0, :, :], AX, ALU.max))
                        first_max(oh[:, 0, :, :], se[:, 0, :, :], mm[:, 0, :], desc8, idx[:], EG)
                        step(V.scalar_tensor_tensor(out=se[:, 1, :, :], in0=oh[:, 0, :, :], scalar=-3e38,
                                                    in1=se[:, 0, :, :], op0=ALU.mult, op1=ALU.add))
                        step(V.tensor_reduce(mm[:, 1, :], se[:, 1, :, :], AX, ALU.max))
                        V.tensor_tensor(ex[:, :, NG:NG + 1], mm[:, 1, :].unsqueeze(2), mm[:, 0, :].unsqueeze(2),
                                        ALU.subtract).then_inc(shifted, 1)
                        first_max(oh[:, 1, :, :], se[:, 1, :, :], mm[:, 1, :], desc8, idx[:], EG)
                        for k in range(2):
                            did(V.tensor_tensor(M[:, k, :, :, :], ohg8,
                                                oh[:, k, :, :].unsqueeze(2).broadcast_to([P, NT, NG, EG]), ALU.mult))
                        dve.wait_ge(chain, did.n)
                        V.tensor_tensor(M[:, 2, :, :, :], M[:, 0, :, :, :], M[:, 1, :, :, :], ALU.add
                                        ).then_inc(picked, 1)
                        dve.wait_ge(expd, 1)
                        step(V.tensor_reduce(gw[:], ex[:, :, 0:NG], AX, ALU.add))
                        e2 = ex[:, :, NG:NG + 1].rearrange("p j a -> p (j a)")
                        step(V.tensor_scalar(m[:], e2, 1.0, None, ALU.add))
                        step(V.tensor_tensor(gw[:], gw[:], m[:], ALU.mult))
                        step(V.reciprocal(gates[:, 0:NT], gw[:]))
                        step(V.tensor_tensor(gates[:, NT:2 * NT], gates[:, 0:NT], e2, ALU.mult))
                        dve.wait_ge(placed, 1)
                        flat = "p (j e) -> p j e"
                        did(V.memset(off[:, 0, :], 0.0))
                        step(V.tensor_copy(tot[:], psum[:, 2, 0:NT * NE].rearrange(flat, j=NT)))
                        for j in range(NT):
                            step(V.tensor_tensor(off[:, j + 1, :], off[:, j, :], tot[:, j, :], ALU.add))
                        step(V.tensor_tensor(pos[:], psum[:, 1, 0:NT * NE].rearrange(flat, j=NT), off[:, 0:NT, :],
                                             ALU.add))
                        counts = off[:, NT, :]
                        step(V.tensor_tensor(cmp[:, :, 0:7], counts.unsqueeze(2).broadcast_to([P, NE, 7]),
                                             thr.unsqueeze(1).broadcast_to([P, NE, 7]), ALU.is_gt))
                        step(V.tensor_reduce(nov[:], cmp[:, :, 0:7], AX, ALU.add))
                        step(V.tensor_tensor_scan(incl[:], ones[:, 0:NE], nov[:], 0.0, ALU.mult, ALU.add))
                        step(V.tensor_tensor(base[:], incl[:], nov[:], ALU.subtract))
                        for f, field in enumerate((pos[:], rows(e32, NE), rows(base[:], NE))):
                            for k in range(2):
                                step(V.tensor_tensor(big[:], M[:, k, :, :, :].rearrange("p j g e -> p j (g e)"), field,
                                                     ALU.mult))
                                step(V.tensor_reduce(F[:, f, k, :], big[:], AX, ALU.add))
                        ps, e, ov = (F[:, f, :, :].rearrange("p k j -> p (k j)") for f in range(3))
                        step(V.tensor_tensor(cmp2[:], ps.unsqueeze(2).broadcast_to([P, 16, 7]),
                                             thr.unsqueeze(1).broadcast_to([P, 16, 7]), ALU.is_ge))
                        step(V.tensor_reduce(hi[:], cmp2[:], AX, ALU.add))
                        step(V.scalar_tensor_tensor(out=r[:], in0=hi[:], scalar=-float(P), in1=ps,
                                                    op0=ALU.mult, op1=ALU.add))
                        step(V.tensor_scalar(over[:], hi[:], 1.0, None, ALU.min))
                        step(V.scalar_tensor_tensor(out=alt[:], in0=ov, scalar=float(NE - 1), in1=hi[:],
                                                    op0=ALU.add, op1=ALU.add))
                        step(V.tensor_tensor(alt[:], alt[:], e, ALU.subtract))
                        step(V.tensor_tensor(alt[:], alt[:], over[:], ALU.mult))
                        step(V.tensor_tensor(blk[:], alt[:], e, ALU.add))
                        step(V.scalar_tensor_tensor(out=alt[:], in0=blk[:], scalar=float(P), in1=r[:],
                                                    op0=ALU.mult, op1=ALU.add))
                        did(V.tensor_copy(row_of[:], alt[:]))
                        did(V.tensor_tensor(A[:], r[:].unsqueeze(2).broadcast_to([P, 16, P]),
                                            s128.unsqueeze(1).broadcast_to([P, 16, P]), ALU.is_equal))
                        step(V.tensor_tensor(B[:], blk[:].unsqueeze(2).broadcast_to([P, 16, NBLKP]),
                                             b48.unsqueeze(1).broadcast_to([P, 16, NBLKP]), ALU.is_equal))
                        for k in range(2):
                            did(V.tensor_tensor(B[:, 8 * k:8 * k + 8, :], B[:, 8 * k:8 * k + 8, :],
                                                tok[:].unsqueeze(2).broadcast_to([P, NT, NBLKP]), ALU.mult))
                        dve.wait_ge(chain, did.n)
                        i3, b3, n3 = (i16.unsqueeze(1).broadcast_to([P, NE, 16]),
                                      base[:].unsqueeze(2).broadcast_to([P, NE, 16]),
                                      incl[:].unsqueeze(2).broadcast_to([P, NE, 16]))
                        V.tensor_tensor(cmp[:], i3, b3, ALU.is_ge).then_inc(marked, 1)
                        dve.wait_ge(marked, 1)
                        step(V.tensor_tensor(sel3[:], i3, n3, ALU.is_lt))
                        step(V.tensor_tensor(cmp[:], cmp[:], sel3[:], ALU.mult))
                        step(V.tensor_tensor(cmp[:], cmp[:], e32.unsqueeze(2).broadcast_to([P, NE, 16]), ALU.mult))
                        step(V.tensor_reduce(eov[:], cmp[:].rearrange("p e i -> p i e"), AX, ALU.add))
                        did(V.tensor_copy(ctrl[:, 1:17], eov[:]))
                        did(V.tensor_copy(ctrl[:, 0:1], incl[:, NE - 1:NE]))
                        dve.wait_ge(listed, 1)
                        V.tensor_copy(slots[:], psum[:, 3, 0:NBLKP]).then_inc(chain, 1)
                end_phase()

        @phase
        def experts(layer, slots):
            (idx_ok, x_lo, x_hi, xh_ok, xl_ok, w_high, w_rest, h1, h3, silu_ok, hid_ok, h_turned, hh_ok, hl_ok,
             y_lo, y_hi, ye_lo, ye_hi, st0, st1, met) = take(21)
            got, put = gather_in, (st0, st1)
            got_base = list(gathered)
            s0 = S_MOE1 if layer else S_MOE0
            with ExitStack() as st:
                nm = str(layer)
                idx = sb(st, "gidx" + nm, [P, 2], I32)
                xg = sb(st, "xg" + nm, [P, 2, D])
                xgH = sb(st, "xgH" + nm, [P, KD, P], F32R)
                xgL = sb(st, "xgL" + nm, [P, KD, P], F32R)
                act_h = sb(st, "act_h" + nm, [P, DE])
                hid = sb(st, "hid" + nm, [P, DE])
                hidH = sb(st, "hidH" + nm, [P, 4, P], F32R)
                hidL = sb(st, "hidL" + nm, [P, 4, P], F32R)
                y = sb(st, "y" + nm, [P, 2, D])
                wH = sb(st, "wH" + nm, [P, 2, 4096], F32R)
                wL = sb(st, "wL" + nm, [P, 2, 4096], F32R)
                LAST = NE - 1

                def run(eng, one):
                    one(0, 0, 0, True, False)
                    one(0, 1, 1, True, False)
                    with eng.Fori(1, NE // 2 - 1) as i:
                        one(i, 0, 2 * i, False, False)
                        one(i, 1, 2 * i + 1, False, False)
                    one(NE // 2 - 1, 0, LAST - 1, False, False)
                    one(NE // 2 - 1, 1, LAST, False, True)

                def part(w, c, b, half):
                    return w[:, (b + c) % 2, 2048 * half:2048 * (half + 1)]

                def raw(c, half):
                    return ring[:, (s0 + c) % RING, 2048 * half:2048 * (half + 1)]

                with nc.Block() as block:
                    @block.sync
                    def _(sp):
                        def one(i, b, e, first, last):
                            for c in range(3):
                                sp.wait_ge(w_rest, 6 * e + 2 * c + 2)
                                slot = (s0 + c) % RING
                                if last:
                                    if s0 + 3 * NE + c < S_END:
                                        load_chunk(sp, s0 + 3 * NE + c)
                                else:
                                    src = expert_src(layer, e + 1, c)
                                    sp.dma_start(chunk_dst(slot, src), src).then_inc(chunk_in[slot], 16)

                        run(sp, one)
                        sp.wait_ge(st0, 16 * NE // 2)
                        sp.wait_ge(st1, 16 * NE // 2)

                    @block.gpsimd
                    def _(pool_e):
                        def one(i, b, e, first, last):
                            if not first:
                                pool_e.wait_ge(x_hi, e - 1)
                            nc.gpsimd.tensor_copy(idx[:, b:b + 1], slots[:, bass.ds(e, 1)]).then_inc(idx_ok, 1)
                            pool_e.wait_ge(idx_ok, e + 1)
                            pool_e.sem_inc(met, 1)
                            pool_e.indirect_dma_start(
                                out=xg[:, b, :], out_offset=None, in_=xn_d[:, :],
                                in_offset=bass.IndirectOffsetOnAxis(ap=idx[:, b:b + 1], axis=0)
                            ).then_inc(got[b], 16)

                        run(pool_e, one)

                    @block.tensor
                    def _(pe):
                        def product(bank, xh, xl, c, b, e, half, ks, cols, start, stop):
                            pe.wait_ge(w_high, 6 * e + 2 * c + half + 1)
                            width = cols[1] - cols[0]

                            def rows(w, k):
                                w3 = part(w, c, b, half).rearrange("p (k c) -> p k c", k=len(ks))
                                return w3[:, k, cols[0]:cols[1]]

                            for n, k in enumerate(ks):
                                nc.tensor.matmul(psum[:, bank, 0:width], xh[:, k, :], rows(wH, n),
                                                 start=(start and n == 0), stop=False)
                                nc.tensor.matmul(psum[:, bank, 0:width], xl[:, k, :], rows(wH, n),
                                                 start=False, stop=False)
                            pe.wait_ge(w_rest, 6 * e + 2 * c + half + 1)
                            for n, k in enumerate(ks):
                                ins = nc.tensor.matmul(psum[:, bank, 0:width], xh[:, k, :], rows(wL, n),
                                                       start=False, stop=(stop and n == len(ks) - 1))
                            return ins

                        def turn_x(i, b, e, first):
                            pe.wait_ge(got[b], 16 * (i + 1) + got_base[b])
                            if not first:
                                pe.wait_ge(xl_ok, e)
                            for k in range(KD):
                                last = nc.tensor.transpose(psum[:, k // 4, (k % 4) * P:(k % 4 + 1) * P],
                                                           xg[:, b, k * P:(k + 1) * P], ident[:])
                                if k == 3:
                                    last.then_inc(x_lo, 1)
                            last.then_inc(x_hi, 1)

                        def one(i, b, e, first, last):
                            pe.wait_ge(xl_ok, e + 1)
                            for c, bank, done, read in ((0, 2, h1, silu_ok), (1, 3, h3, hid_ok)):
                                if not (first and b == 0):
                                    pe.wait_ge(read, e)
                                for half in range(2):
                                    ins = product(bank, xgH, xgL, c, b, e, half, range(4 * half, 4 * half + 4),
                                                  (0, DE), half == 0, half == 1)
                                ins.then_inc(done, 1)
                            if not last:
                                turn_x(i + b, 1 - b, e + 1, False)
                            pe.wait_ge(hid_ok, e + 1)
                            for k in range(4):
                                ins = nc.tensor.transpose(psum[:, 4, k * P:(k + 1) * P],
                                                          hid[:, k * P:(k + 1) * P], ident[:])
                            ins.then_inc(h_turned, 1)
                            pe.wait_ge(hl_ok, e + 1)
                            if not (first and b == 0):
                                pe.wait_ge(ye_lo, e)
                                pe.wait_ge(ye_hi, e)
                            for half in range(2):
                                for out_half, done in ((0, y_lo), (1, y_hi)):
                                    ins = product(5 + out_half, hidH, hidL, 2, b, e, half,
                                                  range(2 * half, 2 * half + 2),
                                                  (512 * out_half, 512 * out_half + 512), half == 0, half == 1)
                                    if half == 1:
                                        ins.then_inc(done, 1)

                        turn_x(0, 0, 0, True)
                        run(pe, one)

                    def quarter(bank):
                        return psum[:, bank, :].rearrange("p (k t) -> p k t", k=4)

                    @block.scalar
                    def _(act):
                        def split(c, b, e, half, first):
                            if half == 0:
                                act.wait_ge(chunk_in[(s0 + c) % RING], 16 * ((s0 + c) // RING + 1 + e))
                                if c == 2:
                                    act.wait_ge(h1, e + 1)
                                elif not (first and b == 0):
                                    act.wait_ge((h3, y_hi)[c], e)
                            nc.scalar.copy(part(wH, c, b, half), raw(c, half)).then_inc(w_high, 1)

                        def move_x(e):
                            for half, turned in ((0, x_lo), (1, x_hi)):
                                act.wait_ge(turned, e + 1)
                                nc.scalar.copy(xgH[:, 4 * half:4 * half + 4, :], quarter(half)).then_inc(xh_ok, 1)

                        def store_y(i, b, e, first):
                            act.wait_ge(y_lo, e + 1)
                            if not first:
                                act.wait_ge(put[b], 16 * i)
                            nc.scalar.copy(y[:, b, 0:512], psum[:, 5, :]).then_inc(ye_lo, 1)

                        def send_y(b, e):
                            act.wait_ge(ye_lo, e + 1)
                            act.wait_ge(ye_hi, e + 1)
                            act.dma_start(y_d[bass.ds(e * P, P), :], y[:, b, :]).then_inc(put[b], 16)

                        def one(i, b, e, first, last):
                            split(0, b, e, 0, first)
                            split(0, b, e, 1, first)
                            if not (first and b == 0):
                                store_y(i - (1 - b), 1 - b, e - 1, first)
                            split(1, b, e, 0, first)
                            split(1, b, e, 1, first)
                            if not (first and b == 0):
                                send_y(1 - b, e - 1)
                            act.wait_ge(h1, e + 1)
                            if not (first and b == 0):
                                act.wait_ge(hid_ok, e)
                            nc.scalar.activation(act_h[:], psum[:, 2, :], ACT.Silu).then_inc(silu_ok, 1)
                            split(2, b, e, 0, first)
                            split(2, b, e, 1, first)
                            if not last:
                                move_x(e + 1)
                            act.wait_ge(h_turned, e + 1)
                            nc.scalar.copy(hidH[:], quarter(4)).then_inc(hh_ok, 1)
                            if last:
                                store_y(i, b, e, first)
                                send_y(b, e)

                        move_x(0)
                        run(act, one)

                    @block.vector
                    def _(dve):
                        def rest(out, whole, high):
                            return nc.vector.tensor_tensor(out, whole, high.bitcast(F32), ALU.subtract)

                        def split(c, b, e, half):
                            dve.wait_ge(w_high, 6 * e + 2 * c + half + 1)
                            rest(part(wL, c, b, half), raw(c, half), part(wH, c, b, half)).then_inc(w_rest, 1)

                        def move_x(e):
                            for half in range(2):
                                dve.wait_ge(xh_ok, 2 * e + half + 1)
                                ks = slice(4 * half, 4 * half + 4)
                                ins = rest(xgL[:, ks, :], quarter(half), xgH[:, ks, :])
                            ins.then_inc(xl_ok, 1)

                        def store_y(i, b, e, first):
                            dve.wait_ge(y_hi, e + 1)
                            if not first:
                                dve.wait_ge(put[b], 16 * i)
                            nc.vector.tensor_copy(y[:, b, 512:1024], psum[:, 6, :]).then_inc(ye_hi, 1)

                        def one(i, b, e, first, last):
                            split(0, b, e, 0)
                            split(0, b, e, 1)
                            if not (first and b == 0):
                                store_y(i - (1 - b), 1 - b, e - 1, first)
                            split(1, b, e, 0)
                            split(1, b, e, 1)
                            split(2, b, e, 0)
                            dve.wait_ge(silu_ok, e + 1)
                            dve.wait_ge(h3, e + 1)
                            nc.vector.tensor_tensor(hid[:], act_h[:], psum[:, 3, :], ALU.mult).then_inc(hid_ok, 1)
                            split(2, b, e, 1)
                            dve.wait_ge(hh_ok, e + 1)
                            rest(hidL[:], quarter(4), hidH[:]).then_inc(hl_ok, 1)
                            if not last:
                                move_x(e + 1)
                            if last:
                                store_y(i, b, e, first)

                        move_x(0)
                        run(dve, one)
                for b in range(2):
                    gathered[b] += 16 * (NE // 2)
                for c in range(3):
                    issued[(s0 + c) % RING] = (s0 + 3 * (NE - 1) + c) // RING + 1 + (s0 + 3 * NE + c < S_END)
                end_phase()

        @phase
        def overflow(layer, slots, ctrl):
            (idx_ok, w_in, x_turned, xt_lo, xt_hi, h_ok, silu_ok, hid_ok, h_turned, h_moved, y_ok, ye_lo, ye_hi,
             put, met) = take(15)
            got = over_in[layer]
            with ExitStack() as st:
                nm = str(layer)
                idx = sb(st, "oidx" + nm, [P, 1], I32)
                xg = sb(st, "oxg" + nm, [P, D])
                xgT = sb(st, "oxgT" + nm, [P, KD, P])
                act_h = sb(st, "oact_h" + nm, [P, DE])
                hid = sb(st, "ohid" + nm, [P, DE])
                hidT = sb(st, "ohidT" + nm, [P, 4, P])
                y = sb(st, "oy" + nm, [P, D])
                w = sb(st, "ow" + nm, [P, 3, 4096])

                def run(eng, one):
                    n = eng.value_load(ctrl[0:1, 0:1], min_val=0, max_val=OVER)
                    with eng.If(n > 0):
                        with eng.Fori(0, n) as i:
                            one(i)
                            eng.wait_ge(put, 16 * (i + 1))
                            eng.sem_inc(met, 1)

                def quarter(bank):
                    return psum[:, bank, :].rearrange("p (k t) -> p k t", k=4)

                with nc.Block() as block:
                    @block.sync
                    def _(sp):
                        def one(i):
                            e = sp.value_load(ctrl[0:1, bass.ds(i + 1, 1)], min_val=0, max_val=NE - 1)
                            for c in range(3):
                                src = expert_src(layer, e, c)
                                sp.dma_start(w[:, c, :].rearrange("p (k c) -> p k c", k=src.shape[1]), src
                                             ).then_inc(w_in, 16)
                            sp.wait_ge(ye_lo, i + 1)
                            sp.wait_ge(ye_hi, i + 1)
                            sp.dma_start(y_d[bass.ds((i + NE) * P, P), :], y[:]).then_inc(put, 16)

                        run(sp, one)

                    @block.gpsimd
                    def _(pool_e):
                        def one(i):
                            nc.gpsimd.tensor_copy(idx[:], slots[:, bass.ds(i + NE, 1)]).then_inc(idx_ok, 1)
                            pool_e.wait_ge(idx_ok, i + 1)
                            pool_e.sem_inc(met, 1)
                            pool_e.indirect_dma_start(
                                out=xg[:], out_offset=None, in_=xn_d[:, :],
                                in_offset=bass.IndirectOffsetOnAxis(ap=idx[:], axis=0)
                            ).then_inc(got, 16)

                        run(pool_e, one)

                    @block.tensor
                    def _(pe):
                        def one(i):
                            pe.wait_ge(got, 16 * (i + 1))
                            for k in range(KD):
                                ins = nc.tensor.transpose(psum[:, k // 4, (k % 4) * P:(k % 4 + 1) * P],
                                                          xg[:, k * P:(k + 1) * P], ident[:])
                            ins.then_inc(x_turned, 1)
                            pe.wait_ge(xt_lo, i + 1)
                            pe.wait_ge(xt_hi, i + 1)
                            pe.wait_ge(w_in, 48 * (i + 1))
                            for c in range(2):
                                wc = w[:, c, :].rearrange("p (k c) -> p k c", k=8)
                                for k in range(KD):
                                    ins = nc.tensor.matmul(psum[:, 2 + c, :], xgT[:, k, :], wc[:, k, :],
                                                           start=(k == 0), stop=(k == KD - 1))
                            ins.then_inc(h_ok, 1)
                            pe.wait_ge(hid_ok, i + 1)
                            for k in range(4):
                                ins = nc.tensor.transpose(psum[:, 4, k * P:(k + 1) * P], hid[:, k * P:(k + 1) * P],
                                                          ident[:])
                            ins.then_inc(h_turned, 1)
                            pe.wait_ge(h_moved, i + 1)
                            wc = w[:, 2, :].rearrange("p (k c) -> p k c", k=4)
                            for half in range(2):
                                for k in range(4):
                                    ins = nc.tensor.matmul(psum[:, 5 + half, :], hidT[:, k, :],
                                                           wc[:, k, half * 512:(half + 1) * 512],
                                                           start=(k == 0), stop=(k == 3))
                            ins.then_inc(y_ok, 1)

                        run(pe, one)

                    @block.scalar
                    def _(act):
                        def one(i):
                            act.wait_ge(x_turned, i + 1)
                            nc.scalar.copy(xgT[:, 0:4, :], quarter(0)).then_inc(xt_lo, 1)
                            act.wait_ge(h_ok, i + 1)
                            nc.scalar.activation(act_h[:], psum[:, 2, :], ACT.Silu).then_inc(silu_ok, 1)
                            act.wait_ge(y_ok, i + 1)
                            nc.scalar.copy(y[:, 0:512], psum[:, 5, :]).then_inc(ye_lo, 1)

                        run(act, one)

                    @block.vector
                    def _(dve):
                        def one(i):
                            dve.wait_ge(x_turned, i + 1)
                            nc.vector.tensor_copy(xgT[:, 4:8, :], quarter(1)).then_inc(xt_hi, 1)
                            dve.wait_ge(silu_ok, i + 1)
                            nc.vector.tensor_tensor(hid[:], act_h[:], psum[:, 3, :], ALU.mult).then_inc(hid_ok, 1)
                            dve.wait_ge(h_turned, i + 1)
                            nc.vector.tensor_copy(hidT[:], quarter(4)).then_inc(h_moved, 1)
                            dve.wait_ge(y_ok, i + 1)
                            nc.vector.tensor_copy(y[:, 512:1024], psum[:, 6, :]).then_inc(ye_hi, 1)

                        run(dve, one)
                end_phase()

        @phase
        def combine(layer, row_of, gates, dst):
            (x_in, first_ok, done, stored) = take(4)
            got, got_base = gather_in, list(gathered)
            with ExitStack() as st:
                nm = str(layer)
                x_all = sb(st, "xc" + nm, [P, NT, D])
                yk = sb(st, "yk" + nm, [P, 2, 2, D])
                rows = xs.rearrange("(j p) d -> p j d", p=P)
                drows = dst.rearrange("(j p) d -> p j d", p=P)
                with nc.Block() as block:
                    @block.sync
                    def _(sp):
                        sp.dma_start(x_all[:], rows).then_inc(x_in, 16)
                        for j in range(NT):
                            sp.wait_ge(done, j + 1)
                            sp.dma_start(drows[:, j, :], x_all[:, j, :]).then_inc(stored, 16)
                        sp.wait_ge(stored, 16 * NT)

                    @block.gpsimd
                    def _(pool_e):
                        for j in range(NT):
                            if j >= 2:
                                pool_e.wait_ge(done, j - 1)
                            for k in range(2):
                                n = k * NT + j
                                pool_e.indirect_dma_start(
                                    out=yk[:, j % 2, k, :], out_offset=None, in_=y_d[:, :],
                                    in_offset=bass.IndirectOffsetOnAxis(ap=row_of[:, n:n + 1], axis=0)
                                ).then_inc(got[j % 2], 16)

                    @block.vector
                    def _(dve):
                        dve.wait_ge(x_in, 16)
                        for j in range(NT):
                            dve.wait_ge(got[j % 2], 32 * (j // 2 + 1) + got_base[j % 2])
                            for k, ok in ((0, first_ok), (1, done)):
                                nc.vector.scalar_tensor_tensor(out=x_all[:, j, :], in0=yk[:, j % 2, k, :],
                                                               scalar=gates[:, k * NT + j:k * NT + j + 1],
                                                               in1=x_all[:, j, :], op0=ALU.mult, op1=ALU.add
                                                               ).then_inc(ok, 1)
                                if k == 0:
                                    dve.wait_ge(first_ok, j + 1)
                for b in range(2):
                    gathered[b] += 32 * (NT // 2)
                end_phase()

        def moe(layer, dst):
            with ExitStack() as m:
                nm = str(layer)
                row_of = sb(m, "row_of" + nm, [P, 16], I32)
                gates = sb(m, "gates" + nm, [P, 16])
                slots = sb(m, "slots" + nm, [P, NBLKP], I32)
                ctrl = sb(m, "ctrl" + nm, [P, 17], I32)
                norm_phase("f" + nm, xs, I["ffn_norm"][layer, :], xn_d)
                router(layer, row_of, gates, slots, ctrl)
                experts(layer, slots)
                overflow(layer, slots, ctrl)
                combine(layer, row_of, gates, dst)

        @phase
        def ml_project(qkT, kn, vA, G):
            (proj, padded, convolved, silued, weights_in, edges, evac, staged0, staged1, k_turned, k_moved,
             chain) = take(12)
            staged = (staged0, staged1)
            with ExitStack() as st:
                up = sb(st, "ml_u_padded", [P, 2, T + 2])
                acc = sb(st, "ml_conv_acc", [P, 2, T])
                so = sb(st, "ml_sigmoid_o", [P, 2, 512])
                cw = sb(st, "ml_conv_w", [P, 8, 3])
                cb = sb(st, "ml_conv_b", [P, 8])
                gw = sb(st, "ml_gate_w", [P, KD, 4 * GROWS])
                CONV = 8
                V0, O0, G0, END = 0, 2 * NT, 4 * NT, 5 * NT
                with nc.Block() as block:
                    @block.sync
                    def _(sp):
                        sp.dma_start(cw[:], I["ml_conv_w"]).then_inc(weights_in, 16)
                        sp.dma_start(cb[:], I["ml_conv_b"]).then_inc(weights_in, 16)
                        sp.dma_start(gw[:], I["ml_gate_w"]).then_inc(weights_in, 16)
                        for c in range(6):
                            sp.wait_ge(proj, 4 * (c + 1) if c < 2 else 8 * c)
                            load_chunk(sp, S_ML + c + RING)

                    @block.tensor
                    def _(pe):
                        for i in range(CONV):
                            c, ct = divmod(i, 4)
                            if ct == 0:
                                chunk_wait(pe, S_ML + c)
                            if i >= 4:
                                pe.wait_ge(padded, i - 3)
                            for half in range(2):
                                for k in range(KD):
                                    last = nc.tensor.matmul(psum[:, 2 * (i % 4) + half, :],
                                                            wide(S_ML + c)[:, k, ct * P:(ct + 1) * P],
                                                            xnT[:, k, half * 512:(half + 1) * 512],
                                                            start=(k == 0), stop=(k == KD - 1))
                            last.then_inc(proj, 1)
                        pe.wait_ge(padded, CONV)
                        pe.wait_ge(weights_in, 48)
                        for s in range(END):
                            c, j = divmod(s, NT)
                            if j == 0 and s < G0:
                                chunk_wait(pe, S_ML + 2 + c)
                            if s >= 8:
                                pe.wait_ge(evac, s - 7)
                            n = 512 if s < G0 else 4 * GROWS
                            for k in range(KD):
                                rhs = wide(S_ML + 2 + c)[:, k, :] if s < G0 else gw[:, k, :]
                                last = nc.tensor.matmul(psum[:, s % 8, 0:n], xnT[:, k, j * P:(j + 1) * P], rhs,
                                                        start=(k == 0), stop=(k == KD - 1))
                            last.then_inc(proj, 1)
                        pe.wait_ge(silued, CONV)
                        for j in range(NT):
                            pe.wait_ge(evac, END - 7 + j)
                            for h in range(MH):
                                last = nc.tensor.transpose(psum[:, j, h * P:(h + 1) * P],
                                                           qkT[:, 4 + h, j * P:(j + 1) * P], ident[:])
                            last.then_inc(k_turned, 1)

                    @block.scalar
                    def _(act):
                        def silu(i):
                            act.wait_ge(convolved, i + 1)
                            nc.scalar.activation(qkT[:, i, :], acc[:, i % 2, :], ACT.Silu).then_inc(silued, 1)

                        for i in range(CONV):
                            act.wait_ge(proj, i + 1)
                            if i >= 2:
                                act.wait_ge(convolved, i - 1)
                            nc.scalar.copy(up[:, i % 2, 1:T + 1],
                                           psum[:, 2 * (i % 4):2 * (i % 4) + 2, :].rearrange("p a b -> p (a b)")
                                           ).then_inc(padded, 1)
                            if i:
                                silu(i - 1)
                        silu(CONV - 1)
                        for s in range(END):
                            c, j = divmod(s, NT)
                            act.wait_ge(proj, CONV + s + 1)
                            bank = psum[:, s % 8, :]
                            if s < O0:
                                nc.scalar.copy(vA[:, j, 2 * c:2 * c + 2, 0:MV], bank.rearrange("p (h e) -> p h e", h=2)
                                               ).then_inc(evac, 1)
                            elif s < G0:
                                b = s % 2
                                if s - O0 >= 2:
                                    act.wait_ge(staged[b], 16 * ((s - O0) // 2))
                                nc.scalar.activation(so[:, b, :], bank, ACT.Sigmoid).then_inc(evac, 1)
                                act.wait_ge(evac, s + 1)
                                act.dma_start(so_d[j * P:(j + 1) * P, (c - 2) * 512:(c - 1) * 512], so[:, b, :]
                                              ).then_inc(staged[b], 16)
                            else:
                                nc.scalar.copy(G[:, j, :], bank[:, 0:4 * GROWS]).then_inc(evac, 1)
                        for b in range(2):
                            act.wait_ge(staged[b], 16 * NT)

                    @block.vector
                    def _(dve):
                        did = Tally(chain)
                        nc.vector.memset(up[:, :, 0:1], 0.0).then_inc(edges, 1)
                        nc.vector.memset(up[:, :, T + 1:T + 2], 0.0).then_inc(edges, 1)
                        nc.vector.memset(vA[:, :, :, MV:MVA], 1.0).then_inc(edges, 1)
                        dve.wait_ge(edges, 3)
                        dve.wait_ge(weights_in, 48)
                        for i in range(CONV):
                            a, u = acc[:, i % 2, :], up[:, i % 2, :]
                            dve.wait_ge(padded, i + 1)
                            if i >= 2:
                                dve.wait_ge(silued, i - 1)
                            m = did(nc.vector.tensor_scalar(a, u[:, 0:T], cw[:, i, 0:1], cb[:, i:i + 1],
                                                            ALU.mult, ALU.add))
                            dve.wait_ge(chain, m)
                            m = did(nc.vector.scalar_tensor_tensor(out=a, in0=u[:, 1:T + 1], scalar=cw[:, i, 1:2],
                                                                   in1=a, op0=ALU.mult, op1=ALU.add))
                            dve.wait_ge(chain, m)
                            nc.vector.scalar_tensor_tensor(out=a, in0=u[:, 2:T + 2], scalar=cw[:, i, 2:3],
                                                           in1=a, op0=ALU.mult, op1=ALU.add).then_inc(convolved, 1)
                        for j in range(NT):
                            dve.wait_ge(k_turned, j + 1)
                            nc.vector.tensor_copy(kn[:, j, :], psum[:, j, :]).then_inc(k_moved, 1)
                end_phase()

        @phase
        def ml_gates(G, cols, colb, apr):
            (bias_in, rows_ok, shifted, sized, expd, logd, ready, powered, turned, moved, flipped, diag_ok,
             chain) = take(13)
            with ExitStack() as st:
                gb = sb(st, "gate_bias", [GROWS, 2])
                mst = sb(st, "carried_max", [GROWS, NT + 1])
                ap = sb(st, "decay_rows", [GROWS, NT])
                dg = sb(st, "decay_diag", [GROWS, NT, GROWS])
                R = [xnT[0:GROWS, n, :] for n in range(8)]
                XF, KW, LF, LI, BC, A, M, WI = R
                ENM, NEGM = XF, LF

                def chunked(row):
                    return row.rearrange("g (c t) -> g c t", c=NT)

                with nc.Block() as block:
                    @block.sync
                    def _(sp):
                        sp.dma_start(gb[:], I["ml_gate_b"]).then_inc(bias_in, 16)

                    @block.tensor
                    def _(pe):
                        for gate in range(2):
                            for c in range(NT):
                                dst = psum[0:GROWS, 2 * gate + c // 4, (c % 4) * P:(c % 4 + 1) * P]
                                o = 2 * GROWS * gate
                                nc.tensor.matmul(dst, G[:, c, o:o + GROWS], ident[:], start=True, stop=False)
                                last = nc.tensor.matmul(dst, G[:, NT - 1 - c, o + GROWS:o + 2 * GROWS], flip[:],
                                                        start=False, stop=True)
                        last.then_inc(rows_ok, 1)
                        pe.wait_ge(powered, 3)
                        pe.wait_ge(ready, 1)
                        for n in range(5 * NT):
                            q, c = divmod(n, NT)
                            row = (A, WI, ENM, KW, NEGM)[q]
                            last = nc.tensor.matmul(psum[:, 4 + n // 14, (n % 14) * GROWS:(n % 14 + 1) * GROWS],
                                                    row[:, c * P:(c + 1) * P], ident[0:GROWS, 0:GROWS],
                                                    start=True, stop=True)
                        last.then_inc(turned, 1)
                        pe.wait_ge(moved, 3)
                        nc.tensor.matmul(psum[:, 7, 0:160], flip[:], cols[:, :, :, 32:36],
                                         start=True, stop=True).then_inc(flipped, 1)
                        pe.wait_ge(diag_ok, 1)
                        nc.tensor.matmul(psum[:, 4, 0:NT * GROWS], ones[0:GROWS, :],
                                         dg[:].rearrange("g c h -> g (c h)"), start=True, stop=True
                                         ).then_inc(flipped, 1)

                    @block.scalar
                    def _(act):
                        act.wait_ge(shifted, 1)
                        nc.scalar.activation(KW, XF, ACT.Abs).then_inc(sized, 1)
                        act.wait_ge(sized, 1)
                        nc.scalar.activation(KW, KW, ACT.Exp, scale=-1.0).then_inc(expd, 1)
                        act.wait_ge(expd, 1)
                        nc.scalar.activation(KW, KW, ACT.Ln, bias=1.0).then_inc(logd, 1)
                        act.wait_ge(shifted, 2)
                        nc.scalar.activation(ap[:], ap[:], ACT.Exp).then_inc(expd, 1)
                        nc.scalar.activation(WI, WI, ACT.Exp).then_inc(powered, 1)
                        nc.scalar.activation(ENM, ENM, ACT.Exp, scale=-1.0).then_inc(powered, 1)
                        nc.scalar.activation(KW, KW, ACT.Exp).then_inc(powered, 1)

                    @block.vector
                    def _(dve):
                        V = nc.vector
                        did = Tally(chain)

                        def step(ins):
                            dve.wait_ge(chain, did(ins))

                        def two(b):
                            return psum[0:GROWS, b:b + 2, :].rearrange("p a b -> p (a b)")

                        dve.wait_ge(bias_in, 16)
                        dve.wait_ge(rows_ok, 1)
                        V.tensor_scalar(XF, two(2), gb[:, 1:2], None, ALU.add).then_inc(shifted, 1)
                        did(V.tensor_scalar(LI, two(0), gb[:, 0:1], None, ALU.add))
                        did(V.memset(mst[:, 0:1], 0.0))
                        dve.wait_ge(chain, did.n)
                        dve.wait_ge(logd, 1)
                        step(V.scalar_tensor_tensor(out=LF, in0=XF, scalar=0.0, in1=KW, op0=ALU.min,
                                                    op1=ALU.subtract))
                        for c in range(NT):
                            t = slice(c * P, (c + 1) * P)
                            did(V.tensor_tensor_scan(BC[:, t], ones[0:GROWS, :], LF[:, t], 0.0, ALU.mult, ALU.add))
                        dve.wait_ge(chain, did.n)
                        step(V.tensor_tensor(A, LI, BC, ALU.subtract))
                        for c in range(NT):
                            t, end = slice(c * P, (c + 1) * P), slice((c + 1) * P - 1, (c + 1) * P)
                            step(V.tensor_tensor_scan(M[:, t], A[:, t], A[:, t], mst[:, c:c + 1], ALU.max, ALU.max))
                            step(V.tensor_tensor(mst[:, c + 1:c + 2], BC[:, end], M[:, end], ALU.add))
                        last = chunked(M)[:, :, P - 1:P]
                        did(V.tensor_tensor(chunked(WI), mst[:, 0:NT].unsqueeze(2).broadcast_to([GROWS, NT, P]),
                                            chunked(M), ALU.subtract))
                        did(V.tensor_tensor(ENM, BC, M, ALU.add))
                        did(V.tensor_tensor(chunked(KW), chunked(A), last.broadcast_to([GROWS, NT, P]), ALU.subtract))
                        dve.wait_ge(chain, did.n)
                        V.tensor_tensor(ap[:].unsqueeze(2), mst[:, 0:NT].unsqueeze(2), last, ALU.subtract
                                        ).then_inc(shifted, 1)
                        V.tensor_scalar(NEGM, M, -1.0, None, ALU.mult).then_inc(ready, 1)
                        dve.wait_ge(expd, 2)
                        V.tensor_tensor(dg[:], ap[:].unsqueeze(2).broadcast_to([GROWS, NT, GROWS]),
                                        ident[0:GROWS, 0:GROWS].unsqueeze(1).broadcast_to([GROWS, NT, GROWS]),
                                        ALU.mult).then_inc(diag_ok, 1)
                        dve.wait_ge(turned, 1)
                        flat = cols[:].rearrange("p q c g -> p (q c g)")
                        for b in range(3):
                            n = min(14, 5 * NT - 14 * b) * GROWS
                            V.tensor_copy(flat[:, b * 14 * GROWS:b * 14 * GROWS + n], psum[:, 4 + b, 0:n]
                                          ).then_inc(moved, 1)
                        dve.wait_ge(flipped, 1)
                        dve.wait_ge(moved, 3)
                        step(V.tensor_copy(colb[:], psum[:, 7, 0:160].rearrange("p (q c h) -> p q c h", q=5, c=NT)))
                        did(V.tensor_scalar(cols[:, 1, :, :], cols[:, 1, :, :], KSCALE, None, ALU.mult))
                        did(V.tensor_scalar(colb[:, 1, :, :], colb[:, 1, :, :], KSCALE, None, ALU.mult))
                        dve.wait_ge(flipped, 2)
                        did(V.tensor_copy(apr[:], psum[:, 4, 0:NT * GROWS].rearrange("p (c g) -> p c g", c=NT)))
                end_phase()

        @phase
        def ml_scan(qkT, kn, vA, cols, colb, apr, hs):
            (s_ok, qc_ok, v_ok, cc_ok, e_ok, w_ok, scw_ok, t_ok, num_ok, h_ok, c_ok, kw_ok, den_ok,
             chain) = take(14)
            with ExitStack() as st:
                C = sb(st, "ml_state", [P, 2 * MH, MVA])
                e0 = sb(st, "ml_exponent", [P, 2, P])
                wT = sb(st, "ml_weight", [P, 2, P])
                scw = sb(st, "ml_scores", [P, 2, P])
                kw = sb(st, "ml_kw", [P, 2, P])
                t1 = sb(st, "ml_inter", [P, 2, MVA])
                num = sb(st, "ml_num", [P, 2, MVA])
                den = sb(st, "ml_den", [P, 2, 2])
                UNITS = NT * 2 * MH
                STATED = UNITS - 2 * MH

                def unit(u):
                    c, gi = divmod(u, 2 * MH)
                    d, h = divmod(gi, MH)
                    n = NT - 1 - c if d else c
                    col = (lambda q: colb[:, q, c, h:h + 1]) if d else (lambda q: cols[:, q, c, h:h + 1])
                    return c, d, h, gi, n, col

                with nc.Block() as block:
                    @block.tensor
                    def _(pe):
                        def scores(u):
                            c, d, h, gi, n, col = unit(u)
                            b = u % 2
                            t = slice(n * P, (n + 1) * P)
                            if u >= 2:
                                pe.wait_ge(scw_ok, u - 1)
                            nc.tensor.matmul(psum[:, b, 0:P], qkT[:, 4 + h, t], qkT[:, h, t], start=True, stop=True)
                            nc.tensor.matmul(psum[:, b, P:2 * P], col(4).broadcast_to([P, P]), ident[:],
                                             start=True, stop=True).then_inc(s_ok, 1)
                            if c:
                                pe.wait_ge(c_ok, u - 2 * MH + 1)
                                if u - 2 * MH >= 2:
                                    pe.wait_ge(t_ok, u - 2 * MH - 1)
                                nc.tensor.matmul(psum[:, 2 + b, 0:MVA], qkT[:, h, t], C[:, gi, :],
                                                 start=True, stop=True).then_inc(qc_ok, 1)

                        def values(u):
                            c, d, h, gi, n, col = unit(u)
                            b = u % 2
                            pe.wait_ge(scw_ok, u + 1)
                            if u >= 2:
                                pe.wait_ge(num_ok, u - 1)
                            nc.tensor.matmul(psum[:, 4 + b, 0:MVA], scw[:, b, :], vA[:, n, h, :],
                                             start=True, stop=True).then_inc(v_ok, 1)
                            if u < STATED:
                                pe.wait_ge(kw_ok, u + 1)
                                if u >= 2:
                                    pe.wait_ge(c_ok, u - 1)
                                nc.tensor.matmul(psum[:, 6 + b, 0:MVA], kw[:, b, :], vA[:, n, h, :],
                                                 start=True, stop=True).then_inc(cc_ok, 1)

                        scores(0)
                        for u in range(UNITS):
                            if u + 1 < UNITS:
                                scores(u + 1)
                            values(u)

                    @block.scalar
                    def _(act):
                        def inter(u):
                            c, d, h, gi, n, col = unit(u)
                            if c:
                                act.wait_ge(qc_ok, u - 2 * MH + 1)
                                if u - 2 * MH >= 2:
                                    act.wait_ge(num_ok, u - 1)
                                nc.scalar.activation(t1[:, u % 2, :], psum[:, 2 + u % 2, 0:MVA], ACT.Copy,
                                                     scale=col(1)).then_inc(t_ok, 1)

                        for u in range(UNITS):
                            act.wait_ge(e_ok, u + 1)
                            if u >= 2:
                                act.wait_ge(scw_ok, u - 1)
                            nc.scalar.activation(wT[:, u % 2, :], e0[:, u % 2, :], ACT.Exp).then_inc(w_ok, 1)
                            inter(u)

                    @block.gpsimd
                    def _(pool_e):
                        for u in range(STATED):
                            c, d, h, gi, n, col = unit(u)
                            if u >= 2:
                                pool_e.wait_ge(cc_ok, u - 1)
                            nc.gpsimd.tensor_scalar(kw[:, u % 2, :], kn[:, n, h * P:(h + 1) * P], col(3), None,
                                                    ALU.mult).then_inc(kw_ok, 1)

                    @block.vector
                    def _(dve):
                        V = nc.vector
                        did = Tally(chain)

                        def exponent(u):
                            c, d, h, gi, n, col = unit(u)
                            dve.wait_ge(s_ok, u + 1)
                            if u >= 2:
                                dve.wait_ge(w_ok, u - 1)
                            V.scalar_tensor_tensor(out=e0[:, u % 2, :], in0=psum[:, u % 2, P:2 * P], scalar=col(0),
                                                   in1=(cap_b if d else cap_f)[:], op0=ALU.add, op1=ALU.min
                                                   ).then_inc(e_ok, 1)

                        def weigh(u):
                            dve.wait_ge(w_ok, u + 1)
                            if u >= 2:
                                dve.wait_ge(v_ok, u - 1)
                            V.scalar_tensor_tensor(out=scw[:, u % 2, :], in0=psum[:, u % 2, 0:P], scalar=KSCALE,
                                                   in1=wT[:, u % 2, :], op0=ALU.mult, op1=ALU.mult
                                                   ).then_inc(scw_ok, 1)

                        def finish(u):
                            c, d, h, gi, n, col = unit(u)
                            b = u % 2
                            dve.wait_ge(v_ok, u + 1)
                            if c:
                                dve.wait_ge(t_ok, u - 2 * MH + 1)
                                V.tensor_tensor(num[:, b, :], t1[:, b, :], psum[:, 4 + b, 0:MVA], ALU.add
                                                ).then_inc(num_ok, 1)
                            else:
                                V.tensor_copy(num[:, b, :], psum[:, 4 + b, 0:MVA]).then_inc(num_ok, 1)
                            if u < STATED:
                                dve.wait_ge(cc_ok, u + 1)
                                if c:
                                    V.scalar_tensor_tensor(out=C[:, gi, :], in0=C[:, gi, :],
                                                           scalar=apr[:, c, 32 * d + h:32 * d + h + 1],
                                                           in1=psum[:, 6 + b, 0:MVA], op0=ALU.mult, op1=ALU.add
                                                           ).then_inc(c_ok, 1)
                                else:
                                    V.tensor_copy(C[:, gi, :], psum[:, 6 + b, 0:MVA]).then_inc(c_ok, 1)
                            dve.wait_ge(num_ok, u + 1)
                            q = num[:, b, MV:MVA]
                            V.scalar_tensor_tensor(out=den[:, b, 0:1], in0=q, scalar=-1.0, in1=q, op0=ALU.mult,
                                                   op1=ALU.max).then_inc(den_ok, 1)
                            dve.wait_ge(den_ok, u + 1)
                            dve.wait_ge(chain, did(V.tensor_scalar(den[:, b, 0:1], den[:, b, 0:1], col(2), None,
                                                                   ALU.max)))
                            dve.wait_ge(chain, did(V.reciprocal(den[:, b, 1:2], den[:, b, 0:1])))
                            dst = hs[:, n, h * MV:(h + 1) * MV]
                            if c < NT // 2:
                                V.tensor_scalar(dst, num[:, b, 0:MV], den[:, b, 1:2], None, ALU.mult
                                                ).then_inc(h_ok, 1)
                            else:
                                first = (NT - 1 - c) * 2 * MH + (1 - d) * MH + h
                                dve.wait_ge(h_ok, first + 1)
                                V.scalar_tensor_tensor(out=dst, in0=num[:, b, 0:MV], scalar=den[:, b, 1:2],
                                                       in1=dst, op0=ALU.mult, op1=ALU.add).then_inc(h_ok, 1)

                        exponent(0)
                        for u in range(UNITS):
                            if u + 1 < UNITS:
                                exponent(u + 1)
                            weigh(u)
                            if u:
                                finish(u - 1)
                        finish(UNITS - 1)
                end_phase()

        start_phase()
        norm_phase("0", I["x"], I["mix_norm"][0, :], None)
        with ExitStack() as mixer:
            yT = sb(mixer, "yT", [P, KD, T])
            with ExitStack() as att:
                qkT = sb(att, "qkT", [P, 2, AH, T])
                v = sb(att, "v_att", [P, NT, 512])
                attention_project(qkT, v)
                o = yT[:, 4:8, :].rearrange("p k t -> p (k t)").rearrange("p (j c) -> p j c", j=NT)
                attention(qkT, v, o)
                head_norm("att", o, AH, DV, I["ev_subln"], 1.0 - (0.8 - 0.6), None, yT)
            with ExitStack() as hy:
                z = sb(hy, "z", [P, HC, T])
                hinv = sb(hy, "hinv", [P, HC])
                hyena_project(z, yT)
                zT = sb(hy, "zT", [P, NT, 512])
                both = xnT[:].rearrange("p k t -> p (k t)").rearrange("p (n c) -> p n c", c=512)
                hs, hd = both[:, 0:NT, :], both[:, NT:2 * NT, :]
                hyena_filter(z, zT, hs, hd, hinv)
                Z = sb(hy, "Z", [P, 4, NF, 512])
                hyena_forward(zT, hs, hd, Z)
                hyena_inverse(z, Z, hinv, yT)
            out_phase("0", yT, S_OUT0, I["x"], xs)
        moe(0, xs)
        norm_phase("1", xs, I["mix_norm"][1, :], None)
        hs = xnT[:].rearrange("p k t -> p (k t)").rearrange("p (j c) -> p j c", j=NT)
        with ExitStack() as ml:
            qkT = sb(ml, "ml_qkT", [P, 8, T])
            kn = sb(ml, "ml_k", [P, NT, 512])
            vA = sb(ml, "ml_v", [P, NT, MH, MVA])
            G = sb(ml, "ml_G", [P, NT, 4 * GROWS])
            ml_project(qkT, kn, vA, G)
            cols = sb(ml, "ml_cols", [P, 5, NT, GROWS])
            colb = sb(ml, "ml_colb", [P, 5, NT, MH])
            apr = sb(ml, "ml_decay", [P, NT, GROWS])
            ml_gates(G, cols, colb, apr)
            ml_scan(qkT, kn, vA, cols, colb, apr, hs)
        with ExitStack() as ml:
            yT = sb(ml, "yT1", [P, KD, T])
            head_norm("ml", hs, MH, MV, I["od_out_norm"], 1.0, so_d, yT)
            out_phase("1", yT, S_OUT1, xs, xs)
        moe(1, out)
        if phases[0] >= LAST_PHASE[0]:
            with nc.Block() as block:
                @block.sync
                def _(sp):
                    for n in range(RING):
                        sp.wait_ge(chunk_in[n], 16 * issued[n])


def constants():
    f = np.float32
    i = np.arange(P)
    c = {
        "c_ident": np.eye(P, dtype=f),
        "c_flip": np.ascontiguousarray(np.eye(P, dtype=f)[::-1]),
        "c_ones": np.ones((P, P), f),
        "c_upper": (i[:, None] < i[None, :]).astype(f),
        "c_cap_f": np.where(i[:, None] <= i[None, :], 0.0, NEG).astype(f),
        "c_cap_b": np.where(i[:, None] >= i[None, :], 0.0, NEG).astype(f),
    }
    inv = (1.0 / (500000.0 ** (np.arange(0, ROPE, 2, dtype=np.float64) / ROPE))).astype(f)
    ang = (np.arange(T, dtype=f)[:, None] * inv[None, :]).astype(np.float64)
    cos, sin = np.cos(ang), np.sin(ang)
    def tiles(a):
        return np.ascontiguousarray(a.reshape(NT, P, -1).transpose(1, 0, 2)).astype(f)
    c["c_cos2"] = tiles(np.concatenate([cos, cos], 1))
    c["c_sin2"] = tiles(np.concatenate([-sin, sin], 1))
    t = np.linspace(0.0, 1.0, T, dtype=f)
    bands = np.linspace(1e-4, 15, 16, dtype=f)
    ang = (f(2.0 * np.pi / T) * np.arange(T, dtype=f)[:, None] * bands[None, :]).astype(np.float64)
    c["c_positions"] = np.ascontiguousarray(
        np.concatenate([t[:, None].astype(np.float64), np.cos(ang), -np.sin(ang)], 1).T).astype(f)
    c["c_delta"] = np.abs(np.linspace(np.log(1e-2) / 1.5, np.log(1e-2) / 0.3, 512, dtype=f))
    c["c_tneg"] = np.ascontiguousarray(-t.reshape(NF, P, 2).transpose(1, 2, 0).reshape(P, NT))
    k = np.arange(512)[:, None]
    m = np.arange(512)[None, :]
    tabs = []
    for par in range(2):
        theta = 2 * np.pi * ((k * (2 * m + par)) % 2048) / 2048
        tabs.append((np.cos(theta), np.sin(theta)))
    sign = (-1.0) ** np.arange(512)
    cs = [tabs[0][0], tabs[1][0], tabs[0][1].copy(), tabs[1][1].copy()]
    for s in (2, 3):
        cs[s][0, :] = sign
    fwd = np.stack([a.T for a in cs])
    c["c_dft"] = np.ascontiguousarray(
        fwd.reshape(4, NF, P, NF, P).transpose(3, 2, 0, 1, 4)).astype(f)
    inv = np.stack(cs) * (4.0 / 2048)
    inv[:, 0, :] /= 2
    c["c_idft"] = np.ascontiguousarray(inv.reshape(4, NF, P, 512).transpose(0, 2, 1, 3)).astype(f)
    c["c_router"] = np.concatenate([
        np.arange(NG, 0, -1), np.arange(EG, 0, -1), np.arange(NE), P * np.arange(1, 8), np.arange(P),
        np.arange(NBLKP), np.arange(16)]).astype(f)
    c["c_tok"] = np.ascontiguousarray(np.arange(T).reshape(NT, P).T).astype(f)
    return c


def layouts(a):
    r = {
        "x": a["x"].reshape(T, D),
        "mix_norm": a["mix_norm"], "ffn_norm": a["ffn_norm"],
        "ev_w_in": a["ev_w_in"][0], "ev_w_out": a["ev_w_out"][0],
        "od_w_in": a["od_w_in"][0], "od_w_out": a["od_w_out"][0],
        "ev_q_norm": a["ev_q_norm"][0], "ev_k_norm": a["ev_k_norm"][0],
        "ev_lam_q1": a["ev_lam_q1"][0], "ev_lam_k1": a["ev_lam_k1"][0],
        "ev_lam_q2": a["ev_lam_q2"][0], "ev_lam_k2": a["ev_lam_k2"][0],
        "ev_subln": np.tile(a["ev_subln"], (AH, 1)).reshape(AH * DV),
        "moe_w1": a["moe_w1"].reshape(2 * NE * D, DE),
        "moe_w3": a["moe_w3"].reshape(2 * NE * D, DE),
        "moe_w2": a["moe_w2"].reshape(2 * NE * DE, D),
    }
    w = a["ev_hy_conv_w"][0]
    r["hy_conv_w"] = w.reshape(3, 3 * HC, P).transpose(2, 1, 0)
    r["hy_conv_b"] = a["ev_hy_conv_b"][0].reshape(3 * HC, P).T
    r["hy_w1"], r["hy_w2"], r["hy_w3"] = a["ev_hy_f_w1"][0], a["ev_hy_f_w2"][0], a["ev_hy_f_w3"][0]
    r["hy_fb"] = np.stack([a["ev_hy_f_b1"][0], a["ev_hy_f_freq"][0], a["ev_hy_f_b2"][0]], 1)
    r["hy_skip"] = a["ev_hy_skip"][0].reshape(HC, P).T
    r["r_w"] = np.concatenate([a["moe_wg"], a["moe_we"]], 2).reshape(2, KD, P, NG + NE).transpose(0, 2, 1, 3)
    r["r_b"] = np.concatenate([a["moe_bg"], a["moe_be"]], 1)
    r["ml_conv_w"] = a["od_conv_w"][0].reshape(3, 8, P).transpose(2, 1, 0)
    r["ml_conv_b"] = a["od_conv_b"][0].reshape(8, P).T
    r["od_out_norm"] = a["od_out_norm"][0]
    gate = a["od_w_in"][0][:, 3072:]
    gw = np.zeros((D, 4, GROWS), np.float32)
    gb = np.zeros((GROWS, 2), np.float32)
    for n, (src, at) in enumerate(((0, 0), (8, 32), (4, 0), (12, 32))):
        gw[:, n, at:at + 4] = gate[:, src:src + 4]
        gb[at:at + 4, n // 2] = a["od_gate_b"][0][src:src + 4]
    r["ml_gate_w"] = gw.reshape(KD, P, 4 * GROWS).transpose(1, 0, 2)
    r["ml_gate_b"] = gb
    return r


def kernel(**inputs):
    import concourse.bacc as bacc
    from concourse.bass_utils import run_bass_kernel_spmd

    arrays = layouts({k: np.asarray(v) for k, v in inputs.items()})
    arrays.update(constants())
    nc = bacc.Bacc("TRN2", target_bir_lowering=False, num_devices=1)
    feeds, aps = {}, {}
    for name, a in arrays.items():
        a = np.ascontiguousarray(a)
        feeds[f"in_{name}"] = a
        aps[name] = nc.dram_tensor(f"in_{name}", a.shape, mybir.dt.from_np(a.dtype), kind="ExternalInput").ap()
    out = nc.dram_tensor("out_0", (T, D), F32, kind="ExternalOutput").ap()
    build(nc, aps, out)
    r = run_bass_kernel_spmd(nc, [feeds], core_ids=[0])
    return r.results[0]["out_0"].reshape(1, T, D)
```

```python
from contextlib import ExitStack

import numpy as np

import concourse.bass as bass
from concourse import mybir

F32 = mybir.dt.float32
F32R = mybir.dt.float32r
I32 = mybir.dt.int32
ALU = mybir.AluOpType
ACT = mybir.ActivationFunctionType
AX = mybir.AxisListType.X

P = 128
D = 1024
T = 1024
NT = T // P
KD = D // P
HALF = 512
EPS = 1e-6

AH = 4
DK = 64
DV = 128
ROPE = 16
NC = 2 * AH
HC = 512 // P
FF = 64
EMB = 33
NF = 4

MH = 4
MV = 256
MVA = MV + 1
GROWS = 36
NEG = -1e30
KSCALE = 128 ** -0.5

NG = 4
EG = 8
NE = NG * EG
DE = 512
OVER = 15
NBLK = NE + OVER
NBLKP = 48

RING = 3
S_ATT, S_HY, S_OUT0, S_MOE0 = 0, 3, 6, 8
S_ML, S_OUT1, S_MOE1, S_END = 104, 110, 112, 208

LAST_PHASE = [99]


class Tally:

    def __init__(self, sem):
        self.sem = sem
        self.n = 0

    def __call__(self, ins):
        ins.then_inc(self.sem, 1)
        self.n += 1
        return self.n


def build(nc, I, out):
    ctx = ExitStack()
    with ctx:
        POOL = 28
        pool = [nc.alloc_semaphore(f"phase_sem{i}") for i in range(POOL)]
        pool_range = range(pool[0].num, pool[0].num + POOL)
        chunk_in = [nc.alloc_semaphore(f"chunk_in{i}") for i in range(RING)]
        consts_in = nc.alloc_semaphore("consts_in")
        rest_in = nc.alloc_semaphore("rest_of_consts_in")
        y_filled = nc.alloc_semaphore("y_filled")
        gather_in = [nc.alloc_semaphore(f"gather_in{i}") for i in range(2)]
        gathered = [0, 0]
        over_in = [nc.alloc_semaphore(f"over_in{i}") for i in range(2)]
        phases = [0]
        issued = [0] * RING

        def take(n):
            assert n <= POOL, n
            return pool[:n]

        def phase(program):
            def run(*a):
                if phases[0] < LAST_PHASE[0]:
                    program(*a)
            return run

        def end_phase():
            nc.all_engine_barrier(sems_to_clear=pool_range)
            phases[0] += 1

        def sb(stack, name, shape, dt=F32, side=None):
            return stack.enter_context(nc.sbuf_tensor(name, shape, dt, side=side))

        xs = nc.dram_tensor("x_scratch", (T, D), F32).ap()
        xn_d = nc.dram_tensor("xn_scratch", (T, D), F32).ap()
        so_d = nc.dram_tensor("sigmoid_o_scratch", (T, D), F32).ap()
        y_d = nc.dram_tensor("y_scratch", (NBLK * P, D), F32).ap()

        def sb_pair(stack, name, shape):
            at = -(-nc.sbuf_base // 32) * 32
            t = sb(stack, name, shape)
            return t, nc.alloc_sbuf_tensor_at(name + "_rest", shape, F32R, offset=at)

        ring, ring_rest = sb_pair(ctx, "ring", [P, RING, 4096])
        ident = sb(ctx, "ident", [P, P])
        flip = sb(ctx, "flip", [P, P])
        ones = sb(ctx, "ones", [P, P])
        upper = sb(ctx, "upper", [P, P])
        cap_f = sb(ctx, "cap_f", [P, P])
        cap_b = sb(ctx, "cap_b", [P, P])
        xnT, xnL = sb_pair(ctx, "xnT", [P, KD, T])
        psum = ctx.enter_context(nc.psum_tensor("psum", [P, 8, 512], F32))

        def half_chunk(w, c0):
            return w[:, c0:c0 + HALF].rearrange("(k p) c -> p k c", p=P)

        def chunk_src(n):
            if n < S_HY:
                return half_chunk(I["ev_w_in"], 512 * (n - S_ATT))
            if n < S_OUT0:
                return half_chunk(I["ev_w_in"], 1536 + 512 * (2 - (n - S_HY)))
            if n < S_MOE0:
                return half_chunk(I["ev_w_out"], 512 * (n - S_OUT0))
            if S_ML <= n < S_OUT1:
                return half_chunk(I["od_w_in"], 512 * (n - S_ML))
            if S_OUT1 <= n < S_MOE1:
                return half_chunk(I["od_w_out"], 512 * (n - S_OUT1))
            layer, m = (0, n - S_MOE0) if n < S_ML else (1, n - S_MOE1)
            return expert_src(layer, m // 3, m % 3)

        def expert_src(layer, e, c):
            w = I[("moe_w1", "moe_w3", "moe_w2")[c]]
            rows = 1024 if c < 2 else 512
            r0 = (e + layer * NE) * rows
            return w[bass.ds(r0, rows), :].rearrange("(k p) c -> p k c", p=P)

        def chunk_dst(slot, src):
            k = src.shape[1]
            return ring[:, slot, :].rearrange("p (k c) -> p k c", k=k)

        def load_chunk(sp, n):
            src = chunk_src(n)
            sp.dma_start(chunk_dst(n % RING, src), src).then_inc(chunk_in[n % RING], 16)
            issued[n % RING] = n // RING + 1

        def refill(sp, first, last, done, each):
            for n in range(first, last):
                if n + RING < S_END:
                    sp.wait_ge(done, each * (n - first + 1))
                    load_chunk(sp, n + RING)

        def chunk_wait(pe, n):
            pe.wait_ge(chunk_in[n % RING], 16 * (n // RING + 1))

        def wide(n):
            return ring[:, n % RING, :].rearrange("p (k c) -> p k c", k=8)

        def wide_rest(n):
            return ring_rest[:, n % RING, :].rearrange("p (k c) -> p k c", k=8)

        def rest_of(out, whole, high):
            return nc.vector.tensor_tensor(out, whole, high.bitcast(F32), ALU.subtract)

        def split_product(dst, lhs, rhs, start, stop):
            nc.tensor.matmul(dst, lhs[0], rhs[0], start=start, stop=False)
            nc.tensor.matmul(dst, lhs[0], rhs[1], start=False, stop=False)
            return nc.tensor.matmul(dst, lhs[1], rhs[0], start=False, stop=stop)

        @phase
        def first_norm(src, gain):
            (gain_in, squared, mean_ok, root_ok, recip_ok, xn_ok, tr_lo, tr_hi, copied_lo, copied_hi) = take(10)
            x_in = pool[10:10 + NT // 2]
            with ExitStack() as st:
                x_all = sb(st, f"x_all0", [P, NT, D])
                g_bc = sb(st, f"g_bc0", [P, D])
                sq = sb(st, f"sq0", [P, D])
                ss = sb(st, f"ss0", [P, NT])
                ms = sb(st, f"ms0", [P, NT])
                sd = sb(st, f"sd0", [P, NT])
                rs = sb(st, f"rs0", [P, NT])
                rows = src.rearrange("(j p) d -> p j d", p=P)
                with nc.Block() as block:
                    @block.sync
                    def _(sp):
                        for n in range(NT // 2):
                            sp.dma_start(x_all[:, 2 * n:2 * n + 2, :], rows[:, 2 * n:2 * n + 2, :]
                                         ).then_inc(x_in[n], 16)
                        sp.dma_start(ident[:], I["c_ident"]).then_inc(consts_in, 16)
                        sp.dma_start(g_bc[:], gain.partition_broadcast(P)).then_inc(gain_in, 16)
                        for n in range(RING):
                            load_chunk(sp, n)
                        for t, c_name in ((flip, "c_flip"), (ones, "c_ones"), (upper, "c_upper"),
                                          (cap_f, "c_cap_f"), (cap_b, "c_cap_b")):
                            sp.dma_start(t[:], I[c_name]).then_inc(rest_in, 16)
                        sp.wait_ge(rest_in, 5 * 16)

                    @block.scalar
                    def _(act):
                        for j in range(NT):
                            act.wait_ge(x_in[j // 2], 16)
                            if j:
                                act.wait_ge(squared, j)
                            nc.scalar.activation(sq[:], x_all[:, j, :], ACT.Square,
                                                 accum_out=ss[:, j:j + 1]).then_inc(squared, 1)
                        act.wait_ge(mean_ok, 1)
                        nc.scalar.activation(sd[:], ms[:], ACT.Sqrt).then_inc(root_ok, 1)
                        for j in range(NT):
                            act.wait_ge(tr_lo, j + 1)
                            nc.scalar.copy(xnT[:, 0:4, j * P:(j + 1) * P],
                                           psum[:, 2 * (j % 4), :].rearrange("p (k t) -> p k t", k=4)
                                           ).then_inc(copied_lo, 1)

                    @block.vector
                    def _(dve):
                        def move(j):
                            dve.wait_ge(tr_hi, j + 1)
                            nc.vector.tensor_copy(xnT[:, 4:8, j * P:(j + 1) * P],
                                                  psum[:, 2 * (j % 4) + 1, :].rearrange("p (k t) -> p k t", k=4)
                                                  ).then_inc(copied_hi, 1)

                        dve.wait_ge(squared, NT)
                        nc.vector.tensor_scalar(ms[:], ss[:], 1.0 / D, EPS, ALU.mult, ALU.add).then_inc(mean_ok, 1)
                        dve.wait_ge(root_ok, 1)
                        nc.vector.reciprocal(rs[:], sd[:]).then_inc(recip_ok, 1)
                        dve.wait_ge(recip_ok, 1)
                        dve.wait_ge(gain_in, 16)
                        for j in range(NT):
                            nc.vector.scalar_tensor_tensor(out=x_all[:, j, :], in0=x_all[:, j, :],
                                                           scalar=rs[:, j:j + 1], in1=g_bc[:], op0=ALU.mult,
                                                           op1=ALU.mult).then_inc(xn_ok, 1)
                            if j:
                                move(j - 1)
                        move(NT - 1)

                    @block.tensor
                    def _(pe):
                        pe.wait_ge(consts_in, 16)
                        for j in range(NT):
                            pe.wait_ge(xn_ok, j + 1)
                            if j >= 4:
                                pe.wait_ge(copied_lo, j - 3)
                                pe.wait_ge(copied_hi, j - 3)
                            for k in range(KD):
                                last = nc.tensor.transpose(
                                    psum[:, 2 * (j % 4) + k // 4, (k % 4) * P:(k % 4 + 1) * P],
                                    x_all[:, j, k * P:(k + 1) * P], ident[:])
                                if k == 3:
                                    last.then_inc(tr_lo, 1)
                            last.then_inc(tr_hi, 1)
                end_phase()

        @phase
        def attention_project(qkT, v):
            (proj, qk_read, squared, summed, mean_ok, root_ok, normed, turned, qk_moved, v_copied, tab_in,
             chain, x_high, x_rest, w_high, w_rest) = take(16)
            with ExitStack() as st:
                sq = sb(st, "sq_qk", [P, 2, 512])
                stat = sb(st, "stat_qk", [P, 3, 2, NC])
                qn = sb(st, "qn", [P, 3, 512])
                rot = sb(st, "rot", [P, NC, ROPE])
                gains = sb(st, "qk_gains", [P, 2, DK])
                cos2 = sb(st, "cos2", [P, NT, ROPE])
                sin2 = sb(st, "sin2", [P, NT, ROPE])
                wH = sb(st, "w_high_qk", [P, 2, 8, HALF], F32R)
                xH = sb(st, "x_high_qk", [P, 2, KD, P], F32R)
                xL = sb(st, "x_rest_qk", [P, 2, KD, P], F32R)
                STEPS = 2 * NT

                def tile(j):
                    return xnT[:, :, j * P:(j + 1) * P]

                with nc.Block() as block:
                    @block.sync
                    def _(sp):
                        sp.dma_start(gains[:, 0, :], I["ev_q_norm"].partition_broadcast(P)).then_inc(tab_in, 16)
                        sp.dma_start(gains[:, 1, :], I["ev_k_norm"].partition_broadcast(P)).then_inc(tab_in, 16)
                        sp.dma_start(cos2[:], I["c_cos2"]).then_inc(tab_in, 16)
                        sp.dma_start(sin2[:], I["c_sin2"]).then_inc(tab_in, 16)
                        refill(sp, S_ATT, S_HY, proj, NT)

                    @block.tensor
                    def _(pe):
                        def turn(i):
                            pe.wait_ge(normed, i + 1)
                            if i >= 2:
                                pe.wait_ge(qk_moved, i - 1)
                            for h in range(AH):
                                last = nc.tensor.transpose(psum[:, 4 + i % 2, h * P:(h + 1) * P],
                                                           qn[:, i % 3, h * P:(h + 1) * P], ident[:])
                            last.then_inc(turned, 1)

                        for i in range(3 * NT):
                            c, j = divmod(i, NT)
                            pe.wait_ge(x_rest, i + 1)
                            if i >= 4:
                                if i - 4 < STEPS:
                                    pe.wait_ge(qk_read, i - 3)
                                else:
                                    pe.wait_ge(v_copied, i - 3 - STEPS)
                            for k in range(KD):
                                if j == 0 and k % 4 == 0:
                                    pe.wait_ge(w_rest, 2 * c + k // 4 + 1)
                                last = split_product(psum[:, i % 4, :], (xH[:, i % 2, k, :], xL[:, i % 2, k, :]),
                                                     (wH[:, c % 2, k, :], wide_rest(S_ATT + c)[:, k, :]),
                                                     k == 0, k == KD - 1)
                            last.then_inc(proj, 1)
                            if 2 <= i <= STEPS + 1:
                                turn(i - 2)

                    @block.scalar
                    def _(act):
                        def split_w(c):
                            chunk_wait(act, S_ATT + c)
                            for half in range(2):
                                ks = slice(4 * half, 4 * half + 4)
                                nc.scalar.copy(wH[:, c % 2, ks, :], wide(S_ATT + c)[:, ks, :]).then_inc(w_high, 1)

                        def split_x(i):
                            if i < 3 * NT:
                                if i >= 2:
                                    act.wait_ge(proj, i - 1)
                                nc.scalar.copy(xH[:, i % 2, :, :], tile(i % NT)).then_inc(x_high, 1)

                        def move(i):
                            act.wait_ge(turned, i + 1)
                            c, j = divmod(i, NT)
                            nc.scalar.copy(qkT[:, c, :, j * P:(j + 1) * P],
                                           psum[:, 4 + i % 2, :].rearrange("p (h t) -> p h t", h=AH)
                                           ).then_inc(qk_moved, 1)

                        split_x(0)
                        split_w(0)
                        split_x(1)
                        split_w(1)
                        for i in range(STEPS):
                            act.wait_ge(proj, i + 1)
                            if i >= 2:
                                act.wait_ge(summed, i - 1)
                            nc.scalar.activation(sq[:, i % 2, :], psum[:, i % 4, :], ACT.Square).then_inc(squared, 1)
                            split_x(i + 2)
                            act.wait_ge(mean_ok, i + 1)
                            nc.scalar.activation(stat[:, 1, i % 2, :], stat[:, 0, i % 2, :], ACT.Sqrt,
                                                 scale=(64.0 if i < NT else 1.0)).then_inc(root_ok, 1)
                            if i >= 3:
                                move(i - 3)
                            if i == NT:
                                split_w(2)
                        move(STEPS - 3)
                        for j in range(NT):
                            act.wait_ge(proj, STEPS + j + 1)
                            nc.scalar.copy(v[:, j, :], psum[:, (STEPS + j) % 4, :]).then_inc(v_copied, 1)
                            split_x(STEPS + j + 2)
                            if j < 2:
                                move(STEPS - 2 + j)

                    @block.vector
                    def _(dve):
                        did = Tally(chain)

                        def split_w(c):
                            for half in range(2):
                                ks = slice(4 * half, 4 * half + 4)
                                dve.wait_ge(w_high, 2 * c + half + 1)
                                rest_of(wide_rest(S_ATT + c)[:, ks, :], wide(S_ATT + c)[:, ks, :], wH[:, c % 2, ks, :]
                                        ).then_inc(w_rest, 1)

                        def split_x(i):
                            if i < 3 * NT:
                                dve.wait_ge(x_high, i + 1)
                                rest_of(xL[:, i % 2, :, :], tile(i % NT), xH[:, i % 2, :, :]).then_inc(x_rest, 1)

                        def normalise(i):
                            c, j = divmod(i, NT)
                            q = qn[:, i % 3, :].rearrange("p (n d) -> p n d", d=DK)
                            dve.wait_ge(root_ok, i + 1)
                            n = did(nc.vector.reciprocal(stat[:, 2, i % 2, :], stat[:, 1, i % 2, :]))
                            dve.wait_ge(chain, n)
                            if i >= 3:
                                dve.wait_ge(turned, i - 2)
                            nc.vector.tensor_tensor(
                                q, psum[:, i % 4, :].rearrange("p (n d) -> p n d", d=DK),
                                stat[:, 2, i % 2, :].unsqueeze(2).broadcast_to([P, NC, DK]), ALU.mult
                            ).then_inc(qk_read, 1)
                            dve.wait_ge(qk_read, i + 1)
                            n = did(nc.vector.tensor_tensor(
                                q, q, gains[:, c, :].unsqueeze(1).broadcast_to([P, NC, DK]), ALU.mult))
                            dve.wait_ge(chain, n)
                            h = ROPE // 2
                            s = sin2[:, j, :].unsqueeze(1)
                            did(nc.vector.tensor_tensor(rot[:, :, 0:h], q[:, :, h:ROPE],
                                                        s[:, :, 0:h].broadcast_to([P, NC, h]), ALU.mult))
                            n = did(nc.vector.tensor_tensor(rot[:, :, h:ROPE], q[:, :, 0:h],
                                                            s[:, :, h:ROPE].broadcast_to([P, NC, h]), ALU.mult))
                            dve.wait_ge(chain, n)
                            n = did(nc.vector.tensor_tensor(
                                q[:, :, 0:ROPE], q[:, :, 0:ROPE],
                                cos2[:, j, :].unsqueeze(1).broadcast_to([P, NC, ROPE]), ALU.mult))
                            dve.wait_ge(chain, n)
                            nc.vector.tensor_tensor(q[:, :, 0:ROPE], q[:, :, 0:ROPE], rot[:], ALU.add
                                                    ).then_inc(normed, 1)

                        split_x(0)
                        split_w(0)
                        split_x(1)
                        split_w(1)
                        dve.wait_ge(tab_in, 64)
                        for i in range(STEPS):
                            dve.wait_ge(squared, i + 1)
                            nc.vector.tensor_reduce(
                                stat[:, 2, i % 2, :], sq[:, i % 2, :].rearrange("p (n d) -> p n d", d=DK), AX, ALU.add
                            ).then_inc(summed, 1)
                            dve.wait_ge(summed, i + 1)
                            nc.vector.tensor_scalar(stat[:, 0, i % 2, :], stat[:, 2, i % 2, :], 1.0 / DK, EPS,
                                                    ALU.mult, ALU.add).then_inc(mean_ok, 1)
                            split_x(i + 2)
                            if i:
                                normalise(i - 1)
                            if i == NT:
                                split_w(2)
                        normalise(STEPS - 1)
                        for j in range(NT):
                            split_x(STEPS + j + 2)
                end_phase()

        @phase
        def attention(qkT, v, o):
            (scored, max_neg, expd, comb, turned_lo, turned_hi, wt_lo, wt_hi, summed, o_copied, lam_in, lam_ok,
             chain) = take(13)
            with ExitStack() as st:
                pr = sb(st, "probs", [P, 2, 2, T])
                w = sb(st, "attn_w", [P, 2, T])
                wT = sb(st, "attn_wT", [P, 2, NT, P])
                nmx = sb(st, "neg_max", [P, 2, 2])
                l = sb(st, "row_sum", [P, 2, 2])
                r = sb(st, "row_recip", [P, 2, 2])
                lam = sb(st, "lam", [P, 4, DK])
                lp = sb(st, "lam_prod", [P, 2, DK])
                ls = sb(st, "lam_sum", [P, 4])
                STEPS = AH * NT
                LAG = 2
                TB, OB = 6, 7

                def pair(u):
                    b = 2 * (u % 3)
                    return psum[:, b:b + 2, :].rearrange("p a b -> p (a b)")

                with nc.Block() as block:
                    @block.sync
                    def _(sp):
                        for n, name in enumerate(("ev_lam_q1", "ev_lam_q2", "ev_lam_k1", "ev_lam_k2")):
                            sp.dma_start(lam[:, n, :], I[name].partition_broadcast(P)).then_inc(lam_in, 16)
                        for n in range(OVER * P // 640):
                            sp.dma_start(y_d[NE * P + 640 * n:NE * P + 640 * (n + 1), :], I["x"][0:640, :]
                                         ).then_inc(y_filled, 16)

                    @block.tensor
                    def _(pe):
                        def scores(u):
                            i, c = divmod(u, 2)
                            h, j = divmod(i, NT)
                            if u >= 3:
                                pe.wait_ge(expd, u - 2)
                            rows = slice(c * DK, (c + 1) * DK)
                            for half in range(2):
                                last = nc.tensor.matmul(psum[:, 2 * (u % 3) + half, :],
                                                        qkT[rows, 0, h, j * P:(j + 1) * P],
                                                        qkT[rows, 1, h, half * 512:(half + 1) * 512],
                                                        start=True, stop=True)
                            last.then_inc(scored, 1)

                        def turn(i, half):
                            if half == 0:
                                pe.wait_ge(comb, i + 1)
                                if i:
                                    pe.wait_ge(wt_hi, i)
                            else:
                                pe.wait_ge(wt_lo, i + 1)
                            for k in range(4):
                                last = nc.tensor.transpose(psum[:, TB, k * P:(k + 1) * P],
                                                           w[:, i % 2, (4 * half + k) * P:(4 * half + k + 1) * P],
                                                           ident[:])
                            last.then_inc(turned_hi if half else turned_lo, 1)

                        def values(i):
                            h, j = divmod(i, NT)
                            pe.wait_ge(wt_hi, i + 1)
                            if i:
                                pe.wait_ge(o_copied, i)
                            for k in range(NT):
                                last = nc.tensor.matmul(psum[:, OB, (i % 2) * DV:(i % 2 + 1) * DV], wT[:, i % 2, k, :],
                                                        v[:, k, h * DV:(h + 1) * DV], start=(k == 0), stop=(k == NT - 1))
                            last.then_inc(summed, 1)

                        for i in range(STEPS + LAG):
                            late = i - LAG
                            if late >= 0:
                                turn(late, 0)
                            if i < STEPS:
                                scores(2 * i)
                            if late >= 0:
                                turn(late, 1)
                            if i < STEPS:
                                scores(2 * i + 1)
                            if late >= 0:
                                values(late)

                    @block.vector
                    def _(dve):
                        did = Tally(chain)
                        dve.wait_ge(lam_in, 64)
                        n = did(nc.vector.tensor_tensor(lp[:], lam[:, 0:2, :], lam[:, 2:4, :], ALU.mult))
                        dve.wait_ge(chain, n)
                        nc.vector.tensor_reduce(ls[:, 0:2], lp[:], AX, ALU.add).then_inc(lam_ok, 1)
                        dve.wait_ge(lam_ok, 2)
                        n = did(nc.vector.tensor_tensor(ls[:, 0:1], ls[:, 3:4], ls[:, 2:3], ALU.subtract))
                        dve.wait_ge(chain, n)
                        lam_init = 0.8 - 0.6
                        n = did(nc.vector.tensor_scalar(ls[:, 1:2], ls[:, 0:1], -lam_init, None, ALU.add))
                        dve.wait_ge(chain, n)

                        def row_max(u):
                            i, c = divmod(u, 2)
                            dve.wait_ge(scored, u + 1)
                            if u >= 4:
                                dve.wait_ge(expd, u - 3)
                            nc.vector.tensor_reduce(nmx[:, i % 2, c:c + 1], pair(u), AX, ALU.max, negate=True
                                                    ).then_inc(max_neg, 1)

                        def combine(i):
                            b = i % 2
                            dve.wait_ge(expd, 2 * i + 2)
                            n = did(nc.vector.reciprocal(r[:, b, :], l[:, b, :]))
                            dve.wait_ge(chain, n)
                            n = did(nc.vector.tensor_tensor(r[:, b, 1:2], r[:, b, 1:2], ls[:, 1:2], ALU.mult))
                            dve.wait_ge(chain, n)
                            n = did(nc.vector.tensor_scalar(pr[:, b, 1, :], pr[:, b, 1, :], r[:, b, 1:2], None, ALU.mult))
                            dve.wait_ge(chain, n)
                            if i >= 2:
                                dve.wait_ge(turned_hi, i - 1)
                            nc.vector.scalar_tensor_tensor(out=w[:, b, :], in0=pr[:, b, 0, :], scalar=r[:, b, 0:1],
                                                           in1=pr[:, b, 1, :], op0=ALU.mult, op1=ALU.add
                                                           ).then_inc(comb, 1)

                        def move(i):
                            dve.wait_ge(turned_hi, i + 1)
                            if i >= 2:
                                dve.wait_ge(summed, i - 1)
                            nc.vector.tensor_copy(wT[:, i % 2, 4:8, :].rearrange("p k t -> p (k t)"), psum[:, TB, :]
                                                  ).then_inc(wt_hi, 1)

                        for i in range(STEPS + LAG):
                            if i < STEPS:
                                row_max(2 * i)
                            if i >= LAG:
                                move(i - LAG)
                            if 1 <= i <= STEPS:
                                combine(i - 1)
                            if i < STEPS:
                                row_max(2 * i + 1)

                    @block.scalar
                    def _(act):
                        act.wait_ge(lam_ok, 1)
                        nc.scalar.activation(ls[:, 2:4], ls[:, 0:2], ACT.Exp).then_inc(lam_ok, 1)

                        def expo(u):
                            i, c = divmod(u, 2)
                            act.wait_ge(max_neg, u + 1)
                            if i >= 2:
                                act.wait_ge(comb, i - 1)
                            nc.scalar.activation(pr[:, i % 2, c, :], pair(u), ACT.Exp, bias=nmx[:, i % 2, c:c + 1],
                                                 accum_out=l[:, i % 2, c:c + 1]).then_inc(expd, 1)

                        def move(i):
                            act.wait_ge(turned_lo, i + 1)
                            if i >= 2:
                                act.wait_ge(summed, i - 1)
                            nc.scalar.copy(wT[:, i % 2, 0:4, :].rearrange("p k t -> p (k t)"), psum[:, TB, :]
                                           ).then_inc(wt_lo, 1)

                        def keep(i):
                            h, j = divmod(i, NT)
                            act.wait_ge(summed, i + 1)
                            nc.scalar.copy(o[:, j, h * DV:(h + 1) * DV], psum[:, OB, (i % 2) * DV:(i % 2 + 1) * DV]
                                           ).then_inc(o_copied, 1)

                        for i in range(STEPS + LAG):
                            if i >= LAG:
                                move(i - LAG)
                            if i < STEPS:
                                expo(2 * i)
                            if i >= LAG + 1:
                                keep(i - LAG - 1)
                            if i < STEPS:
                                expo(2 * i + 1)
                        keep(STEPS - 1)
                end_phase()

        @phase
        def head_norm(name, o, heads, width, gain, post, gate, yT):
            (gain_in, gate_in0, gate_in1, squared, gated, mean_ok, root_ok, scaled, turned, copied,
             chain) = take(11)
            gate_in = (gate_in0, gate_in1)
            W = heads * width
            banks = W // 512
            with ExitStack() as st:
                sq = sb(st, f"sq_{name}", [P, 2, W])
                ss = sb(st, f"ss_{name}", [P, NT, heads])
                ms, sd, rs = (sb(st, f"{n}_{name}", [P, NT, heads]) for n in ("ms", "sd", "rs"))
                g_bc = sb(st, f"g_{name}", [P, W])
                gt = sb(st, f"gate_{name}", [P, 2, W]) if gate is not None else None
                with nc.Block() as block:
                    @block.sync
                    def _(sp):
                        sp.dma_start(g_bc[:].rearrange("p (h w) -> p h w", w=gain.shape[-1]),
                                     gain.partition_broadcast(P)).then_inc(gain_in, 16)
                        if gate is not None:
                            for j in range(NT):
                                if j >= 2:
                                    sp.wait_ge(gated, j - 1)
                                sp.dma_start(gt[:, j % 2, :], gate[j * P:(j + 1) * P, :]
                                             ).then_inc(gate_in[j % 2], 16)

                    @block.scalar
                    def _(act):
                        def squares(j):
                            if j >= 2:
                                act.wait_ge(squared, j - 1)
                            for h in range(heads):
                                cols = slice(h * width, (h + 1) * width)
                                ins = nc.scalar.activation(sq[:, j % 2, cols], o[:, j, cols], ACT.Square,
                                                           accum_out=ss[:, j, h:h + 1])
                            ins.then_inc(squared, 1)

                        def move(j):
                            for b in range(banks):
                                act.wait_ge(turned, j * banks + b + 1)
                                nc.scalar.copy(yT[:, 4 * b:4 * b + 4, j * P:(j + 1) * P],
                                               psum[:, (j * banks + b) % 4, :].rearrange("p (k t) -> p k t", k=4)
                                               ).then_inc(copied, 1)

                        squares(0)
                        for j in range(NT):
                            if j + 1 < NT:
                                squares(j + 1)
                            act.wait_ge(mean_ok, j + 1)
                            nc.scalar.activation(sd[:, j, :], ms[:, j, :], ACT.Sqrt).then_inc(root_ok, 1)
                            if j >= 2:
                                move(j - 2)
                        move(NT - 2)
                        move(NT - 1)

                    @block.vector
                    def _(dve):
                        did = Tally(chain)

                        def mean(j):
                            dve.wait_ge(squared, j + 1)
                            nc.vector.tensor_scalar(ms[:, j, :], ss[:, j, :], 1.0 / width, EPS, ALU.mult, ALU.add
                                                    ).then_inc(mean_ok, 1)

                        dve.wait_ge(gain_in, 16)
                        if post != 1.0:
                            n = did(nc.vector.tensor_scalar(g_bc[:], g_bc[:], post, None, ALU.mult))
                            dve.wait_ge(chain, n)
                        mean(0)
                        for j in range(NT):
                            if j + 1 < NT:
                                mean(j + 1)
                            dve.wait_ge(root_ok, j + 1)
                            n = did(nc.vector.reciprocal(rs[:, j, :], sd[:, j, :]))
                            dve.wait_ge(chain, n)
                            for h in range(heads):
                                cols = slice(h * width, (h + 1) * width)
                                ins = nc.vector.scalar_tensor_tensor(out=o[:, j, cols], in0=o[:, j, cols],
                                                                     scalar=rs[:, j, h:h + 1], in1=g_bc[:, cols],
                                                                     op0=ALU.mult, op1=ALU.mult)
                            ins.then_inc(scaled, 1)

                    if gate is not None:
                        @block.gpsimd
                        def _(pool_e):
                            for j in range(NT):
                                pool_e.wait_ge(scaled, j + 1)
                                pool_e.wait_ge(gate_in[j % 2], 16 * (j // 2 + 1))
                                nc.gpsimd.tensor_tensor(o[:, j, :], o[:, j, :], gt[:, j % 2, :], ALU.mult
                                                        ).then_inc(gated, 1)

                    @block.tensor
                    def _(pe):
                        for j in range(NT):
                            pe.wait_ge(scaled if gate is None else gated, j + 1)
                            for b in range(banks):
                                n = j * banks + b
                                if n >= 4:
                                    pe.wait_ge(copied, n - 3)
                                for k in range(4):
                                    last = nc.tensor.transpose(psum[:, n % 4, k * P:(k + 1) * P],
                                                               o[:, j, (4 * b + k) * P:(4 * b + k + 1) * P], ident[:])
                                last.then_inc(turned, 1)
                end_phase()

        @phase
        def out_phase(name, yT, yL, s0, xsrc, gain):
            (x_in, gain_in, proj, added, stored, y_high, y_rest, w_high, w_rest, squared, mean_ok, root_ok, recip_ok,
             xn_ok, tr_lo, tr_hi, copied_lo, copied_hi, xn_out0, xn_out1) = take(20)
            xn_out = (xn_out0, xn_out1)
            with ExitStack() as st:
                x_all = sb(st, f"x_res{name}", [P, NT, D])
                wH = sb(st, f"w_high{name}", [P, 2, 8, HALF], F32R)
                g_bc = sb(st, f"ffn_gain{name}", [P, D])
                sq = sb(st, f"sq_out{name}", [P, D])
                xn = sb(st, f"xn_out{name}", [P, 2, D])
                ss, ms, sd, rs = (sb(st, f"{n}_out{name}", [P, NT]) for n in ("ss", "ms", "sd", "rs"))
                yH = xnL
                TURN = 6
                rows = xsrc.rearrange("(j p) d -> p j d", p=P)
                dst = xs.rearrange("(j p) d -> p j d", p=P)
                STEPS = 2 * NT
                with nc.Block() as block:
                    @block.sync
                    def _(sp):
                        sp.dma_start(x_all[:], rows).then_inc(x_in, 16)
                        sp.dma_start(g_bc[:], gain.partition_broadcast(P)).then_inc(gain_in, 16)
                        refill(sp, s0, s0 + 1, proj, NT)
                        for j in range(NT):
                            sp.wait_ge(added, NT + j + 1)
                            sp.dma_start(dst[:, j, :], x_all[:, j, :]).then_inc(stored, 16)
                            if j:
                                sp.wait_ge(xn_ok, j)
                                sp.dma_start(xn_d[(j - 1) * P:j * P, :], xn[:, (j - 1) % 2, :]
                                             ).then_inc(xn_out[(j - 1) % 2], 16)
                        sp.wait_ge(proj, STEPS)
                        if s0 + 1 + RING < S_END:
                            load_chunk(sp, s0 + 1 + RING)
                        sp.wait_ge(xn_ok, NT)
                        sp.dma_start(xn_d[(NT - 1) * P:NT * P, :], xn[:, (NT - 1) % 2, :]
                                     ).then_inc(xn_out[(NT - 1) % 2], 16)
                        sp.wait_ge(stored, 16 * NT)
                        for b in range(2):
                            sp.wait_ge(xn_out[b], 16 * (NT // 2))

                    @block.scalar
                    def _(act):
                        def split_w(c):
                            chunk_wait(act, s0 + c)
                            for half in range(2):
                                ks = slice(4 * half, 4 * half + 4)
                                nc.scalar.copy(wH[:, c, ks, :], wide(s0 + c)[:, ks, :]).then_inc(w_high, 1)

                        for j in range(NT):
                            js = slice(j * P, (j + 1) * P)
                            nc.scalar.copy(yH[:, :, js], yT[:, :, js]).then_inc(y_high, 1)
                            if j == 0:
                                split_w(0)
                        split_w(1)

                        def move(j):
                            act.wait_ge(tr_lo, j + 1)
                            nc.scalar.copy(xnT[:, 0:4, j * P:(j + 1) * P],
                                           psum[:, TURN, :].rearrange("p (k t) -> p k t", k=4)).then_inc(copied_lo, 1)

                        for j in range(NT):
                            act.wait_ge(added, NT + j + 1)
                            if j:
                                act.wait_ge(squared, j)
                            nc.scalar.activation(sq[:], x_all[:, j, :], ACT.Square,
                                                 accum_out=ss[:, j:j + 1]).then_inc(squared, 1)
                            act.wait_ge(mean_ok, j + 1)
                            nc.scalar.activation(sd[:, j:j + 1], ms[:, j:j + 1], ACT.Sqrt).then_inc(root_ok, 1)
                            if j >= 2:
                                move(j - 2)
                        move(NT - 2)
                        move(NT - 1)

                    @block.tensor
                    def _(pe):
                        def turn(j):
                            pe.wait_ge(xn_ok, j + 1)
                            if j:
                                pe.wait_ge(copied_lo, j)
                                pe.wait_ge(copied_hi, j)
                            for k in range(KD):
                                last = nc.tensor.transpose(psum[:, TURN + k // 4, (k % 4) * P:(k % 4 + 1) * P],
                                                           xn[:, j % 2, k * P:(k + 1) * P], ident[:])
                                if k == 3:
                                    last.then_inc(tr_lo, 1)
                            last.then_inc(tr_hi, 1)

                        for i in range(STEPS):
                            c, j = divmod(i, NT)
                            js = slice(j * P, (j + 1) * P)
                            if c == 0:
                                pe.wait_ge(y_rest, j + 1)
                            if i >= 6:
                                pe.wait_ge(added, i - 5)
                            for k in range(KD):
                                if j == 0 and k % 4 == 0:
                                    pe.wait_ge(w_rest, 2 * c + k // 4 + 1)
                                last = split_product(psum[:, i % 6, :], (yH[:, k, js], yL[:, k, js]),
                                                     (wH[:, c, k, :], wide_rest(s0 + c)[:, k, :]), k == 0, k == KD - 1)
                            last.then_inc(proj, 1)
                            if i >= NT + 2:
                                turn(i - NT - 2)
                        turn(NT - 2)
                        turn(NT - 1)

                    @block.vector
                    def _(dve):
                        def split_w(c):
                            for half in range(2):
                                ks = slice(4 * half, 4 * half + 4)
                                dve.wait_ge(w_high, 2 * c + half + 1)
                                rest_of(wide_rest(s0 + c)[:, ks, :], wide(s0 + c)[:, ks, :], wH[:, c, ks, :]
                                        ).then_inc(w_rest, 1)

                        for j in range(NT):
                            js = slice(j * P, (j + 1) * P)
                            dve.wait_ge(y_high, j + 1)
                            rest_of(yL[:, :, js], yT[:, :, js], yH[:, :, js]).then_inc(y_rest, 1)
                            if j == 0:
                                split_w(0)
                        split_w(1)
                        dve.wait_ge(x_in, 16)
                        dve.wait_ge(gain_in, 16)

                        def move(j):
                            dve.wait_ge(tr_hi, j + 1)
                            nc.vector.tensor_copy(xnT[:, 4:8, j * P:(j + 1) * P],
                                                  psum[:, TURN + 1, :].rearrange("p (k t) -> p k t", k=4)
                                                  ).then_inc(copied_hi, 1)

                        for i in range(STEPS):
                            c, j = divmod(i, NT)
                            dve.wait_ge(proj, i + 1)
                            xp = x_all[:, j, c * 512:(c + 1) * 512]
                            nc.vector.tensor_tensor(xp, xp, psum[:, i % 6, :], ALU.add).then_inc(added, 1)
                            if c == 0:
                                continue
                            one = slice(j, j + 1)
                            dve.wait_ge(squared, j + 1)
                            nc.vector.tensor_scalar(ms[:, one], ss[:, one], 1.0 / D, EPS, ALU.mult, ALU.add
                                                    ).then_inc(mean_ok, 1)
                            dve.wait_ge(root_ok, j + 1)
                            nc.vector.reciprocal(rs[:, one], sd[:, one]).then_inc(recip_ok, 1)
                            dve.wait_ge(recip_ok, j + 1)
                            if j >= 2:
                                dve.wait_ge(xn_out[j % 2], 16 * (j // 2))
                                dve.wait_ge(tr_hi, j - 1)
                            nc.vector.scalar_tensor_tensor(out=xn[:, j % 2, :], in0=x_all[:, j, :], scalar=rs[:, one],
                                                           in1=g_bc[:], op0=ALU.mult, op1=ALU.mult).then_inc(xn_ok, 1)
                            if j >= 2:
                                move(j - 2)
                        move(NT - 2)
                        move(NT - 1)
                end_phase()

        @phase
        def hyena_project(z, yT, xnH):
            (proj, padded, convolved, weights_in, edges, chain, x_high, x_rest, w_high, w_rest) = take(10)
            with ExitStack() as st:
                up = sb(st, "u_padded", [P, 2, T + 2])
                acc = sb(st, "conv_acc", [P, 2, T])
                cw = sb(st, "hy_conv_w", [P, 3 * HC, 3])
                cb = sb(st, "hy_conv_b", [P, 3 * HC])
                wH = sb(st, "w_high_hy", [P, 2, KD, P], F32R)
                STEPS = 3 * HC

                def block_of(w, i):
                    c, ct = divmod(i, HC)
                    return w(S_HY + c)[:, :, ct * P:(ct + 1) * P]

                def x_piece(n):
                    half, quad = divmod(n, 2)
                    return (slice(None), slice(4 * quad, 4 * quad + 4), slice(half * 512, (half + 1) * 512))

                with nc.Block() as block:
                    @block.sync
                    def _(sp):
                        sp.dma_start(cw[:], I["hy_conv_w"]).then_inc(weights_in, 16)
                        sp.dma_start(cb[:], I["hy_conv_b"]).then_inc(weights_in, 16)
                        refill(sp, S_HY, S_OUT0, proj, HC)

                    @block.tensor
                    def _(pe):
                        for i in range(STEPS):
                            pe.wait_ge(w_rest, i + 1)
                            if i >= 4:
                                pe.wait_ge(padded, i - 3)
                            for half in range(2):
                                ts = slice(half * 512, (half + 1) * 512)
                                for k in range(KD):
                                    if i == 0 and k % 4 == 0:
                                        pe.wait_ge(x_rest, 2 * half + k // 4 + 1)
                                    last = split_product(psum[:, 2 * (i % 4) + half, :],
                                                         (wH[:, i % 2, k, :], block_of(wide_rest, i)[:, k, :]),
                                                         (xnH[:, k, ts], xnL[:, k, ts]), k == 0, k == KD - 1)
                            last.then_inc(proj, 1)

                    @block.scalar
                    def _(act):
                        def split_w(i):
                            if i < STEPS:
                                if i % HC == 0:
                                    chunk_wait(act, S_HY + i // HC)
                                if i >= 2:
                                    act.wait_ge(proj, i - 1)
                                nc.scalar.copy(wH[:, i % 2, :, :], block_of(wide, i)).then_inc(w_high, 1)

                        split_w(0)
                        for n in range(4):
                            nc.scalar.copy(xnH[x_piece(n)], xnT[x_piece(n)]).then_inc(x_high, 1)
                        split_w(1)
                        for i in range(STEPS):
                            act.wait_ge(proj, i + 1)
                            if i >= 2:
                                act.wait_ge(convolved, i - 1)
                            nc.scalar.copy(up[:, i % 2, 1:T + 1],
                                           psum[:, 2 * (i % 4):2 * (i % 4) + 2, :].rearrange("p a b -> p (a b)")
                                           ).then_inc(padded, 1)
                            split_w(i + 2)

                    @block.vector
                    def _(dve):
                        did = Tally(chain)

                        def split_w(i):
                            if i < STEPS:
                                dve.wait_ge(w_high, i + 1)
                                rest_of(block_of(wide_rest, i), block_of(wide, i), wH[:, i % 2, :, :]
                                        ).then_inc(w_rest, 1)

                        split_w(0)
                        for n in range(4):
                            dve.wait_ge(x_high, n + 1)
                            rest_of(xnL[x_piece(n)], xnT[x_piece(n)], xnH[x_piece(n)]).then_inc(x_rest, 1)
                        split_w(1)
                        nc.vector.memset(up[:, :, 0:1], 0.0).then_inc(edges, 1)
                        nc.vector.memset(up[:, :, T + 1:T + 2], 0.0).then_inc(edges, 1)
                        dve.wait_ge(edges, 2)
                        dve.wait_ge(weights_in, 32)
                        for i in range(STEPS):
                            split_w(i + 2)
                            c, ct = divmod(i, HC)
                            n = (2 - c) * HC + ct
                            a, u = acc[:, i % 2, :], up[:, i % 2, :]
                            dve.wait_ge(padded, i + 1)
                            m = did(nc.vector.tensor_scalar(a, u[:, 0:T], cw[:, n, 0:1], cb[:, n:n + 1],
                                                            ALU.mult, ALU.add))
                            dve.wait_ge(chain, m)
                            m = did(nc.vector.scalar_tensor_tensor(out=a, in0=u[:, 1:T + 1], scalar=cw[:, n, 1:2],
                                                                   in1=a, op0=ALU.mult, op1=ALU.add))
                            dve.wait_ge(chain, m)
                            dst = (z[:, ct, :], a, yT[:, 4 + ct, :])[c]
                            nc.vector.scalar_tensor_tensor(out=dst, in0=u[:, 2:T + 2], scalar=cw[:, n, 2:3],
                                                           in1=a, op0=ALU.mult, op1=ALU.add).then_inc(convolved, 1)
                            if c == 1:
                                dve.wait_ge(convolved, i + 1)
                                nc.vector.tensor_tensor(z[:, ct, :], z[:, ct, :], a, ALU.mult).then_inc(chain, 1)
                                did.n += 1
                end_phase()

        @phase
        def hyena_filter(z, zT, hs, hd, hinv):
            (tab_in, lin, argued, waved, filt, decayed, mixed, normed, turned, moved, skipped, chain,
             row_ok, summed, patched) = take(15)
            with ExitStack() as st:
                zp = sb(st, "hy_positions", [EMB, T])
                w1 = sb(st, "hy_w1", [EMB, FF])
                w2 = sb(st, "hy_w2", [FF, FF])
                w3 = sb(st, "hy_w3", [FF, 2 * 512])
                fb = sb(st, "hy_fb", [FF, 3])
                tneg = sb(st, "hy_tneg", [P, NT])
                delta = sb(st, "hy_delta", [P, 512])
                skip = sb(st, "hy_skip", [P, HC])
                arg = sb(st, "hy_arg", [FF, T])
                turns = sb(st, "hy_turns", [FF, T])
                hdn = sb(st, "hy_hidden", [FF, T])
                dec = sb(st, "hy_decay", [P, 2, 512])
                hf = sb(st, "hy_fwd", [P, 2, 512])
                hb = sb(st, "hy_bwd", [P, 2, 512])
                ab = sb(st, "hy_abs", [P, 2, 2, 512])
                row = sb(st, "hy_row", [1, 512])
                TWO_PI = 2 * np.pi
                HI = 6.28125
                LO = TWO_PI - HI
                MAGIC = 1.5 * 2.0 ** 23
                with nc.Block() as block:
                    @block.sync
                    def _(sp):
                        for t, src in ((zp[:], I["c_positions"]), (w1[:], I["hy_w1"]), (w2[:], I["hy_w2"]),
                                       (w3[:], I["hy_w3"]), (fb[:], I["hy_fb"]), (tneg[:], I["c_tneg"]),
                                       (delta[:], I["c_delta"].partition_broadcast(P)), (skip[:], I["hy_skip"])):
                            sp.dma_start(t, src).then_inc(tab_in, 16)

                    @block.tensor
                    def _(pe):
                        def layer(w, x):
                            for half in range(2):
                                last = nc.tensor.matmul(psum[0:FF, half, :], w[:], x[:, half * 512:(half + 1) * 512],
                                                        start=True, stop=True)
                            last.then_inc(lin, 1)

                        def turn(n):
                            par, mt = divmod(n, NF)
                            if n >= 4:
                                pe.wait_ge(moved, n - 3)
                            for ct in range(HC):
                                t0 = par + 2 * mt * P
                                last = nc.tensor.transpose(psum[:, 4 + n % 4, ct * P:(ct + 1) * P],
                                                           z[:, ct, t0:t0 + 2 * P - 1:2], ident[:])
                            last.then_inc(turned, 1)

                        pe.wait_ge(tab_in, 16 * 8)
                        layer(w1, zp)
                        for n in range(4):
                            turn(n)
                        pe.wait_ge(waved, 1)
                        layer(w2, hdn)
                        for n in range(4, NT):
                            turn(n)
                        pe.wait_ge(waved, 2)
                        pe.wait_ge(moved, NT)

                        def norm_sum(n):
                            pe.wait_ge(mixed, n + 2)
                            for d in range(2):
                                last = nc.tensor.matmul(psum[0:1, 4, :], ones[:, 0:1], ab[:, n % 2, d, :],
                                                        start=(n == 0 and d == 0), stop=(n == NT - 1 and d == 1))
                            last.then_inc(normed, 1)

                        for n in range(NT):
                            par, mt = divmod(n, NF)
                            t0 = par + 2 * mt * P
                            if n >= 2:
                                pe.wait_ge(summed, n - 1)
                            for half in range(2):
                                last = nc.tensor.matmul(psum[:, 2 * (n % 2) + half, :], hdn[:, t0:t0 + 2 * P - 1:2],
                                                        w3[:, half * 512:(half + 1) * 512], start=True, stop=True)
                            last.then_inc(filt, 1)
                            if n:
                                norm_sum(n - 1)
                        norm_sum(NT - 1)
                        pe.wait_ge(row_ok, 1)
                        for ct in range(HC):
                            last = nc.tensor.matmul(psum[:, 5, ct:ct + 1], row[0:1, ct * P:(ct + 1) * P],
                                                    ones[0:1, 0:1], start=True, stop=True)
                        last.then_inc(normed, 1)

                    @block.gpsimd
                    def _(pool_e):
                        pool_e.wait_ge(patched, 2)
                        nc.gpsimd.memset(ab[0:1, 0, 1, :], 0.0).then_inc(mixed, 1)

                    @block.scalar
                    def _(act):
                        def size(n):
                            b = n % 2
                            act.wait_ge(summed, n + 1)
                            if n >= 2:
                                act.wait_ge(normed, n - 1)
                            for d, h in ((0, hf), (1, hb)):
                                ins = nc.scalar.activation(ab[:, b, d, :], h[:, b, :], ACT.Abs)
                                if n == 0:
                                    ins.then_inc(patched, 1)
                            if n:
                                ins.then_inc(mixed, 1)
                            else:
                                act.wait_ge(patched, 2)
                                act.wait_ge(mixed, 1)
                                nc.scalar.activation(ab[0:1, 0, 0, :], hs[0:1, 0, :], ACT.Abs).then_inc(mixed, 1)

                        act.wait_ge(tab_in, 16 * 8)
                        for k in range(2):
                            act.wait_ge(argued, k + 1)
                            nc.scalar.activation(hdn[:], arg[:], ACT.Sin).then_inc(waved, 1)
                            for n in range(4 * k, 4 * k + 4):
                                act.wait_ge(turned, n + 1)
                                nc.scalar.copy(zT[:, n, :], psum[:, 4 + n % 4, :]).then_inc(moved, 1)
                        for n in range(NT):
                            if n >= 2:
                                act.wait_ge(summed, n - 1)
                            nc.scalar.activation(dec[:, n % 2, :], delta[:], ACT.Exp, scale=tneg[:, n:n + 1]
                                                 ).then_inc(decayed, 1)
                            if n:
                                size(n - 1)
                        size(NT - 1)
                        for ct in range(HC):
                            act.wait_ge(turned, NT)
                            nc.scalar.activation(z[:, ct, :], z[:, ct, :], ACT.Copy, scale=skip[:, ct:ct + 1]
                                                 ).then_inc(skipped, 1)

                    @block.vector
                    def _(dve):
                        did = Tally(chain)

                        def step(ins):
                            dve.wait_ge(chain, did(ins))

                        dve.wait_ge(tab_in, 16 * 8)
                        for k in range(2):
                            dve.wait_ge(lin, k + 1)
                            if k:
                                dve.wait_ge(waved, 1)
                            step(nc.vector.tensor_scalar(
                                arg[:], psum[0:FF, 0:2, :].rearrange("p a b -> p (a b)"),
                                fb[:, 2 * k:2 * k + 1], fb[:, 1:2], ALU.add, ALU.mult))
                            step(nc.vector.tensor_scalar(turns[:], arg[:], 1 / TWO_PI, MAGIC, ALU.mult, ALU.add))
                            step(nc.vector.tensor_scalar(turns[:], turns[:], -MAGIC, None, ALU.add))
                            step(nc.vector.scalar_tensor_tensor(out=arg[:], in0=turns[:], scalar=-HI, in1=arg[:],
                                                                op0=ALU.mult, op1=ALU.add))
                            step(nc.vector.scalar_tensor_tensor(out=arg[:], in0=turns[:], scalar=-LO, in1=arg[:],
                                                                op0=ALU.mult, op1=ALU.add))
                            nc.vector.tensor_scalar(arg[:], arg[:], 3.1415925, -3.1415925, ALU.min, ALU.max
                                                    ).then_inc(argued, 1)
                        for n in range(NT):
                            b = n % 2
                            dve.wait_ge(filt, n + 1)
                            dve.wait_ge(decayed, n + 1)
                            if n >= 2:
                                dve.wait_ge(mixed, n)
                            did(nc.vector.tensor_tensor(hf[:, b, :], psum[:, 2 * b, :], dec[:, b, :], ALU.mult))
                            step(nc.vector.tensor_tensor(hb[:, b, :], psum[:, 2 * b + 1, :], dec[:, b, :], ALU.mult))
                            step(nc.vector.tensor_tensor(hs[:, n, :], hf[:, b, :], hb[:, b, :], ALU.add))
                            nc.vector.tensor_tensor(hd[:, n, :], hf[:, b, :], hb[:, b, :], ALU.subtract).then_inc(summed, 1)
                        dve.wait_ge(normed, NT)
                        nc.vector.tensor_scalar(row[:], psum[0:1, 4, :], EPS, None, ALU.add).then_inc(row_ok, 1)
                        dve.wait_ge(normed, NT + 1)
                        nc.vector.reciprocal(hinv[:], psum[:, 5, 0:HC]).then_inc(row_ok, 1)
                end_phase()

        def even_tables(zT):
            both = zT[:].rearrange("p n c -> p (n c)").rearrange("p (s k m) -> p s k m", s=2, k=NF)
            return both[:, 0, :, :], both[:, 1, :, :]

        @phase
        def hyena_forward(zT, hs, hd, Z):
            (copied, row_moved, mixed, used, chain, early) = take(6)
            BUFS = 4
            piece_ins = pool[8:8 + BUFS]
            with ExitStack() as st:
                tab = sb(st, "dft_tables", [P, BUFS, NF, P])
                acc = sb(st, "freq_acc", [P, 4, 512])
                tmp = sb(st, "freq_tmp", [P, 4, 512])
                mid = sb(st, "filter_at_512", [1, 512])
                PIECES = NF * 4
                with nc.Block() as block:
                    @block.sync
                    def _(sp):
                        for n in range(2 * PIECES):
                            if n >= BUFS:
                                sp.wait_ge(used, n - BUFS + 1)
                            kt, t = divmod(n % PIECES, 4)
                            sp.dma_start(tab[:, n % BUFS, :, :], I["c_dft"][kt, :, t, :, :]
                                         ).then_inc(piece_ins[n % BUFS], 16)
                        for n, tables in enumerate(even_tables(zT)):
                            sp.dma_start(tables, I["c_idft"][2 * n]).then_inc(early, 16)
                        sp.wait_ge(early, 32)

                    @block.tensor
                    def _(pe):
                        def transform(n, dst, src, cols=slice(None)):
                            par = n % 2
                            for m in range(NF):
                                last = nc.tensor.matmul(dst, tab[:, n % BUFS, m, cols], src[:, par * NF + m, :],
                                                        start=(m == 0), stop=(m == NF - 1))
                            return last

                        for n in range(PIECES):
                            pe.wait_ge(piece_ins[n % BUFS], 16 * (n // BUFS + 1))
                            if n >= 8:
                                pe.wait_ge(copied, n - 7)
                            transform(n, psum[:, n % 8, :], zT).then_inc(used, 1)
                        for q in range(PIECES):
                            n = PIECES + q
                            kt, t = divmod(q, 4)
                            pe.wait_ge(piece_ins[n % BUFS], 16 * (n // BUFS + 1))
                            if q < 8:
                                pe.wait_ge(copied, PIECES - 7 + q)
                            elif t == 0:
                                pe.wait_ge(mixed, kt - 1)
                            if q == 4:
                                pe.wait_ge(row_moved, 1)
                            last = transform(n, psum[:, 4 * (kt % 2) + t, :], hs if t < 2 else hd)
                            if q == 2:
                                pe.wait_ge(copied, PIECES)
                                last = transform(n, psum[0:1, 4, :], hs, slice(0, 1))
                            last.then_inc(used, 1)

                    @block.scalar
                    def _(act):
                        for n in range(PIECES):
                            act.wait_ge(used, n + 1)
                            nc.scalar.copy(Z[:, n % 4, n // 4, :], psum[:, n % 8, :]).then_inc(copied, 1)
                        act.wait_ge(used, PIECES + 3)
                        nc.scalar.copy(mid[:], psum[0:1, 4, :]).then_inc(row_moved, 1)

                    @block.vector
                    def _(dve):
                        did = Tally(chain)
                        terms = [
                            [(0, 0, 1), (1, 1, 1), (2, 2, -1), (3, 3, -1)],
                            [(0, 1, 1), (1, 0, 1), (2, 3, -1), (3, 2, -1)],
                            [(0, 2, 1), (1, 3, 1), (2, 0, 1), (3, 1, 1)],
                            [(0, 3, 1), (1, 2, 1), (2, 1, 1), (3, 0, 1)],
                        ]
                        for kt in range(NF):
                            dve.wait_ge(copied, PIECES)
                            dve.wait_ge(row_moved, 1)
                            dve.wait_ge(used, PIECES + 4 * kt + 4)
                            if kt:
                                dve.wait_ge(mixed, kt)
                            q, lo = mid[:], psum[0:1, 3, :]
                            se, so = Z[0:1, 2, kt, :], Z[0:1, 3, kt, :]
                            for s in range(4):
                                dst = acc if s == 0 else tmp
                                for o in range(4):
                                    zi, ki, _s = terms[o][s]
                                    n = did(nc.vector.tensor_tensor(dst[:, o, :], Z[:, zi, kt, :],
                                                                    psum[:, 4 * (kt % 2) + ki, :],
                                                                    ALU.mult))
                                dve.wait_ge(chain, n)
                                if kt == 0:
                                    zero = (2, 3) if s < 2 else (0, 1)
                                    for o in zero:
                                        n = did(nc.vector.memset(dst[0:1, o, :], 0.0))
                                    if s == 2:
                                        did(nc.vector.tensor_tensor(tmp[0:1, 2, :], se, q, ALU.mult))
                                        n = did(nc.vector.tensor_tensor(tmp[0:1, 3, :], se, lo, ALU.mult))
                                    if s == 3:
                                        did(nc.vector.scalar_tensor_tensor(out=tmp[0:1, 2, :], in0=so, scalar=-1.0,
                                                                           in1=lo, op0=ALU.mult, op1=ALU.mult))
                                        n = did(nc.vector.tensor_tensor(tmp[0:1, 3, :], so, q, ALU.mult))
                                    dve.wait_ge(chain, n)
                                if s:
                                    for o in range(4):
                                        op = ALU.add if terms[o][s][2] > 0 else ALU.subtract
                                        into = Z[:, o, kt, :] if s == 3 else acc[:, o, :]
                                        ins = nc.vector.tensor_tensor(into, acc[:, o, :], tmp[:, o, :], op)
                                        if s == 3 and o == 3:
                                            ins.then_inc(mixed, 1)
                                        else:
                                            n = did(ins)
                                    dve.wait_ge(chain, n)
                end_phase()

        @phase
        def hyena_inverse(z, zT, Z, hinv, yT):
            (tab_in, back, added, gated) = take(4)
            with ExitStack() as st:
                y = sb(st, "hy_y", [P, 2, 512])
                itab = xnT[:].rearrange("p k t -> p (k t)").rearrange("p (s k m) -> p s k m", s=4, k=NF)
                even = even_tables(zT)
                with nc.Block() as block:
                    @block.sync
                    def _(sp):
                        for s in (1, 3):
                            sp.dma_start(itab[:, s, :, :], I["c_idft"][s]).then_inc(tab_in, 16)

                    @block.tensor
                    def _(pe):
                        for i in range(2 * HC):
                            par, ct = divmod(i, HC)
                            if i == HC:
                                pe.wait_ge(tab_in, 32)
                            for n, (s, kt) in enumerate([(s, kt) for s in (par, 2 + par) for kt in range(NF)]):
                                last = nc.tensor.matmul(psum[:, i, :], Z[:, s, kt, ct * P:(ct + 1) * P],
                                                        (itab[:, s] if par else even[s // 2])[:, kt, :], start=(n == 0), stop=(n == 2 * NF - 1))
                            last.then_inc(back, 1)

                    @block.vector
                    def _(dve):
                        for i in range(2 * HC):
                            par, ct = divmod(i, HC)
                            dve.wait_ge(back, i + 1)
                            nc.vector.scalar_tensor_tensor(out=y[:, i % 2, :], in0=psum[:, i, :],
                                                           scalar=hinv[:, ct:ct + 1], in1=z[:, ct, par:T:2],
                                                           op0=ALU.mult, op1=ALU.add).then_inc(added, 1)
                            dve.wait_ge(added, i + 1)
                            g = yT[:, 4 + ct, par:T:2]
                            nc.vector.tensor_tensor(g, g, y[:, i % 2, :], ALU.mult).then_inc(gated, 1)
                end_phase()

        @phase
        def router(layer, row_of, gates, slots, ctrl):
            (tab_in, logit_ok, shifted, expd, picked, placed, marked, listed, chain, moved) = take(10)
            with ExitStack() as st:
                name = str(layer)

                def t(n, shape, dt=F32):
                    return sb(st, f"r{name}_{n}", shape, dt)

                wr = t("w", [P, KD, NG + NE])
                br = t("b", [P, NG + NE])
                cst = t("cst", [P, NG + EG + NE + 7 + P + NBLKP + 16])
                tok = t("tok", [P, NT])
                at = [0]

                def piece(n):
                    at[0] += n
                    return cst[:, at[0] - n:at[0]]

                desc4, desc8, e32, thr, s128, b48, i16 = (piece(n) for n in (NG, EG, NE, 7, P, NBLKP, 16))
                L = t("logits", [P, NT, NG + NE])
                LT = sb(st, f"r{name}_logitsT", [NG + NE, T])
                g, el = L[:, :, 0:NG], L[:, :, NG:NG + NE]
                gm = t("gm", [P, NT])
                gi = t("gi", [P, NT, NG])
                ohg = t("ohg", [P, NT, NG])
                m = t("m", [P, NT])
                ex = t("ex", [P, NT, NG + 1])
                gw = t("gw", [P, NT])
                sel = t("sel", [P, NT, NG, EG])
                se = t("se", [P, 2, NT, EG])
                mm = t("mm", [P, 2, NT])
                idx = t("idx", [P, NT, EG])
                oh = t("oh", [P, 2, NT, EG])
                M = t("M", [P, 3, NT, NG, EG])
                pos = t("pos", [P, NT, NE])
                tot = t("tot", [P, NT, NE])
                off = t("off", [P, NT + 1, NE])
                cmp = t("cmp", [P, NE, 16])
                sel3 = t("sel3", [P, NE, 16])
                nov = t("nov", [P, NE])
                incl = t("incl", [P, NE])
                base = t("base", [P, NE])
                big = t("big", [P, NT, NE])
                F = t("F", [P, 3, 2, NT])
                hi = t("hi", [P, 16])
                over = t("over", [P, 16])
                alt = t("alt", [P, 16])
                blk = t("blk", [P, 16])
                r = t("r", [P, 16])
                cmp2 = t("cmp2", [P, 16, 7])
                A = t("A", [P, 16, P])
                B = t("B", [P, 16, NBLKP])
                eov = t("eov", [P, 16])
                with nc.Block() as block:
                    @block.sync
                    def _(sp):
                        for dst, src in ((wr, I["r_w"][layer]), (br, I["r_b"][layer].partition_broadcast(P)),
                                         (cst, I["c_router"].partition_broadcast(P)), (tok, I["c_tok"])):
                            sp.dma_start(dst[:], src).then_inc(tab_in, 16)
                        sp.wait_ge(y_filled, 16 * (OVER * P // 640))

                    @block.tensor
                    def _(pe):
                        pe.wait_ge(tab_in, 64)
                        for half in range(2):
                            for k in range(KD):
                                last = nc.tensor.matmul(psum[0:NG + NE, 4 + half, :], wr[:, k, :],
                                                        xnT[:, k, half * 512:(half + 1) * 512],
                                                        start=(k == 0), stop=(k == KD - 1))
                            last.then_inc(logit_ok, 1)
                        for j in range(NT):
                            if j % 4 == 0:
                                pe.wait_ge(moved, j // 4 + 1)
                            last = nc.tensor.transpose(psum[:, 0, j * 36:(j + 1) * 36], LT[:, j * P:(j + 1) * P],
                                                       ident[0:NG + NE, 0:NG + NE])
                        last.then_inc(logit_ok, 1)
                        pe.wait_ge(picked, 1)
                        both = M[:, 2, :, :, :].rearrange("p j g e -> p (j g e)")
                        nc.tensor.matmul(psum[:, 1, 0:NT * NE], upper[:], both, start=True, stop=True)
                        nc.tensor.matmul(psum[:, 2, 0:NT * NE], ones[:], both, start=True, stop=True
                                         ).then_inc(placed, 1)
                        pe.wait_ge(marked, 1)
                        for n in range(16):
                            last = nc.tensor.matmul(psum[:, 3, 0:NBLKP], A[:, n, :], B[:, n, :],
                                                    start=(n == 0), stop=(n == 15))
                        last.then_inc(listed, 1)

                    @block.scalar
                    def _(act):
                        for half in range(2):
                            act.wait_ge(logit_ok, half + 1)
                            nc.scalar.copy(LT[:, half * 512:(half + 1) * 512], psum[0:NG + NE, 4 + half, :]
                                           ).then_inc(moved, 1)
                        act.wait_ge(shifted, 1)
                        nc.scalar.activation(ex[:], ex[:], ACT.Exp).then_inc(expd, 1)

                    @block.vector
                    def _(dve):
                        did = Tally(chain)
                        V = nc.vector

                        def step(ins):
                            dve.wait_ge(chain, did(ins))

                        def rows(a, n):
                            return a.unsqueeze(1).broadcast_to([P, NT, n])

                        def cols(a, n):
                            return a.unsqueeze(2).broadcast_to([P, NT, n])

                        dve.wait_ge(tab_in, 64)
                        dve.wait_ge(logit_ok, 3)
                        step(V.tensor_tensor(L[:], psum[:, 0, 0:NT * 36].rearrange("p (j c) -> p j c", j=NT),
                                             rows(br[:], 36), ALU.add))
                        step(V.tensor_reduce(gm[:], g, AX, ALU.max))

                        def first_max(out, vals, top, desc, scratch, n):
                            step(V.tensor_tensor(scratch, vals, cols(top, n), ALU.is_equal))
                            step(V.tensor_tensor(scratch, scratch, rows(desc, n), ALU.mult))
                            step(V.tensor_reduce(m[:], scratch, AX, ALU.max))
                            step(V.tensor_tensor(out, scratch, cols(m[:], n), ALU.is_equal))

                        first_max(ohg[:], g, gm[:], desc4, gi[:], NG)
                        step(V.tensor_tensor(ex[:, :, 0:NG], g, cols(gm[:], NG), ALU.subtract))
                        ohg8 = ohg[:].unsqueeze(3).broadcast_to([P, NT, NG, EG])
                        step(V.tensor_tensor(sel[:], el.rearrange("p j (g e) -> p j g e", g=NG), ohg8, ALU.mult))
                        step(V.tensor_reduce(se[:, 0, :, :], sel[:].rearrange("p j g e -> p j e g"), AX, ALU.add))
                        step(V.tensor_reduce(mm[:, 0, :], se[:, 0, :, :], AX, ALU.max))
                        first_max(oh[:, 0, :, :], se[:, 0, :, :], mm[:, 0, :], desc8, idx[:], EG)
                        step(V.scalar_tensor_tensor(out=se[:, 1, :, :], in0=oh[:, 0, :, :], scalar=-3e38,
                                                    in1=se[:, 0, :, :], op0=ALU.mult, op1=ALU.add))
                        step(V.tensor_reduce(mm[:, 1, :], se[:, 1, :, :], AX, ALU.max))
                        V.tensor_tensor(ex[:, :, NG:NG + 1], mm[:, 1, :].unsqueeze(2), mm[:, 0, :].unsqueeze(2),
                                        ALU.subtract).then_inc(shifted, 1)
                        first_max(oh[:, 1, :, :], se[:, 1, :, :], mm[:, 1, :], desc8, idx[:], EG)
                        for k in range(2):
                            did(V.tensor_tensor(M[:, k, :, :, :], ohg8,
                                                oh[:, k, :, :].unsqueeze(2).broadcast_to([P, NT, NG, EG]), ALU.mult))
                        dve.wait_ge(chain, did.n)
                        V.tensor_tensor(M[:, 2, :, :, :], M[:, 0, :, :, :], M[:, 1, :, :, :], ALU.add
                                        ).then_inc(picked, 1)
                        dve.wait_ge(expd, 1)
                        step(V.tensor_reduce(gw[:], ex[:, :, 0:NG], AX, ALU.add))
                        e2 = ex[:, :, NG:NG + 1].rearrange("p j a -> p (j a)")
                        step(V.tensor_scalar(m[:], e2, 1.0, None, ALU.add))
                        step(V.tensor_tensor(gw[:], gw[:], m[:], ALU.mult))
                        step(V.reciprocal(gates[:, 0:NT], gw[:]))
                        step(V.tensor_tensor(gates[:, NT:2 * NT], gates[:, 0:NT], e2, ALU.mult))
                        dve.wait_ge(placed, 1)
                        flat = "p (j e) -> p j e"
                        did(V.memset(off[:, 0, :], 0.0))
                        step(V.tensor_copy(tot[:], psum[:, 2, 0:NT * NE].rearrange(flat, j=NT)))
                        for j in range(NT):
                            step(V.tensor_tensor(off[:, j + 1, :], off[:, j, :], tot[:, j, :], ALU.add))
                        step(V.tensor_tensor(pos[:], psum[:, 1, 0:NT * NE].rearrange(flat, j=NT), off[:, 0:NT, :],
                                             ALU.add))
                        counts = off[:, NT, :]
                        step(V.tensor_tensor(cmp[:, :, 0:7], counts.unsqueeze(2).broadcast_to([P, NE, 7]),
                                             thr.unsqueeze(1).broadcast_to([P, NE, 7]), ALU.is_gt))
                        step(V.tensor_reduce(nov[:], cmp[:, :, 0:7], AX, ALU.add))
                        step(V.tensor_tensor_scan(incl[:], ones[:, 0:NE], nov[:], 0.0, ALU.mult, ALU.add))
                        step(V.tensor_tensor(base[:], incl[:], nov[:], ALU.subtract))
                        for f, field in enumerate((pos[:], rows(e32, NE), rows(base[:], NE))):
                            for k in range(2):
                                step(V.tensor_tensor(big[:], M[:, k, :, :, :].rearrange("p j g e -> p j (g e)"), field,
                                                     ALU.mult))
                                step(V.tensor_reduce(F[:, f, k, :], big[:], AX, ALU.add))
                        ps, e, ov = (F[:, f, :, :].rearrange("p k j -> p (k j)") for f in range(3))
                        step(V.tensor_tensor(cmp2[:], ps.unsqueeze(2).broadcast_to([P, 16, 7]),
                                             thr.unsqueeze(1).broadcast_to([P, 16, 7]), ALU.is_ge))
                        step(V.tensor_reduce(hi[:], cmp2[:], AX, ALU.add))
                        step(V.scalar_tensor_tensor(out=r[:], in0=hi[:], scalar=-float(P), in1=ps,
                                                    op0=ALU.mult, op1=ALU.add))
                        step(V.tensor_scalar(over[:], hi[:], 1.0, None, ALU.min))
                        step(V.scalar_tensor_tensor(out=alt[:], in0=ov, scalar=float(NE - 1), in1=hi[:],
                                                    op0=ALU.add, op1=ALU.add))
                        step(V.tensor_tensor(alt[:], alt[:], e, ALU.subtract))
                        step(V.tensor_tensor(alt[:], alt[:], over[:], ALU.mult))
                        step(V.tensor_tensor(blk[:], alt[:], e, ALU.add))
                        step(V.scalar_tensor_tensor(out=alt[:], in0=blk[:], scalar=float(P), in1=r[:],
                                                    op0=ALU.mult, op1=ALU.add))
                        did(V.tensor_copy(row_of[:], alt[:]))
                        did(V.tensor_tensor(A[:], r[:].unsqueeze(2).broadcast_to([P, 16, P]),
                                            s128.unsqueeze(1).broadcast_to([P, 16, P]), ALU.is_equal))
                        step(V.tensor_tensor(B[:], blk[:].unsqueeze(2).broadcast_to([P, 16, NBLKP]),
                                             b48.unsqueeze(1).broadcast_to([P, 16, NBLKP]), ALU.is_equal))
                        for k in range(2):
                            did(V.tensor_tensor(B[:, 8 * k:8 * k + 8, :], B[:, 8 * k:8 * k + 8, :],
                                                tok[:].unsqueeze(2).broadcast_to([P, NT, NBLKP]), ALU.mult))
                        dve.wait_ge(chain, did.n)
                        i3, b3, n3 = (i16.unsqueeze(1).broadcast_to([P, NE, 16]),
                                      base[:].unsqueeze(2).broadcast_to([P, NE, 16]),
                                      incl[:].unsqueeze(2).broadcast_to([P, NE, 16]))
                        V.tensor_tensor(cmp[:], i3, b3, ALU.is_ge).then_inc(marked, 1)
                        dve.wait_ge(marked, 1)
                        step(V.tensor_tensor(sel3[:], i3, n3, ALU.is_lt))
                        step(V.tensor_tensor(cmp[:], cmp[:], sel3[:], ALU.mult))
                        step(V.tensor_tensor(cmp[:], cmp[:], e32.unsqueeze(2).broadcast_to([P, NE, 16]), ALU.mult))
                        step(V.tensor_reduce(eov[:], cmp[:].rearrange("p e i -> p i e"), AX, ALU.add))
                        did(V.tensor_copy(ctrl[:, 1:17], eov[:]))
                        did(V.tensor_copy(ctrl[:, 0:1], incl[:, NE - 1:NE]))
                        dve.wait_ge(listed, 1)
                        V.tensor_copy(slots[:], psum[:, 3, 0:NBLKP]).then_inc(chain, 1)
                end_phase()

        @phase
        def experts(layer, slots):
            (idx_ok, x_lo, x_hi, xh_ok, xl_ok, w_high, w_rest, h1, h3, silu_ok, hid_ok, h_turned, hh_ok, hl_ok,
             y_lo, y_hi, ye_lo, ye_hi, st0, st1, met) = take(21)
            got, put = gather_in, (st0, st1)
            got_base = list(gathered)
            s0 = S_MOE1 if layer else S_MOE0
            with ExitStack() as st:
                nm = str(layer)
                idx = sb(st, "gidx" + nm, [P, 2], I32)
                xg = sb(st, "xg" + nm, [P, 2, D])
                xgH = sb(st, "xgH" + nm, [P, KD, P], F32R)
                xgL = sb(st, "xgL" + nm, [P, KD, P], F32R)
                act_h = sb(st, "act_h" + nm, [P, DE])
                hid = sb(st, "hid" + nm, [P, DE])
                hidH = sb(st, "hidH" + nm, [P, 4, P], F32R)
                hidL = sb(st, "hidL" + nm, [P, 4, P], F32R)
                y = sb(st, "y" + nm, [P, 2, D])
                wH = sb(st, "wH" + nm, [P, 2, 4096], F32R)
                wL = sb(st, "wL" + nm, [P, 2, 4096], F32R)
                LAST = NE - 1

                def run(eng, one):
                    one(0, 0, 0, True, False)
                    one(0, 1, 1, True, False)
                    with eng.Fori(1, NE // 2 - 1) as i:
                        one(i, 0, 2 * i, False, False)
                        one(i, 1, 2 * i + 1, False, False)
                    one(NE // 2 - 1, 0, LAST - 1, False, False)
                    one(NE // 2 - 1, 1, LAST, False, True)

                def part(w, c, b, half):
                    return w[:, (b + c) % 2, 2048 * half:2048 * (half + 1)]

                def raw(c, half):
                    return ring[:, (s0 + c) % RING, 2048 * half:2048 * (half + 1)]

                with nc.Block() as block:
                    @block.sync
                    def _(sp):
                        def one(i, b, e, first, last):
                            for c in range(3):
                                sp.wait_ge(w_rest, 6 * e + 2 * c + 2)
                                slot = (s0 + c) % RING
                                if last:
                                    if s0 + 3 * NE + c < S_END:
                                        load_chunk(sp, s0 + 3 * NE + c)
                                else:
                                    src = expert_src(layer, e + 1, c)
                                    sp.dma_start(chunk_dst(slot, src), src).then_inc(chunk_in[slot], 16)

                        run(sp, one)
                        sp.wait_ge(st0, 16 * NE // 2)
                        sp.wait_ge(st1, 16 * NE // 2)

                    @block.gpsimd
                    def _(pool_e):
                        def one(i, b, e, first, last):
                            if not first:
                                pool_e.wait_ge(x_hi, e - 1)
                            nc.gpsimd.tensor_copy(idx[:, b:b + 1], slots[:, bass.ds(e, 1)]).then_inc(idx_ok, 1)
                            pool_e.wait_ge(idx_ok, e + 1)
                            pool_e.sem_inc(met, 1)
                            pool_e.indirect_dma_start(
                                out=xg[:, b, :], out_offset=None, in_=xn_d[:, :],
                                in_offset=bass.IndirectOffsetOnAxis(ap=idx[:, b:b + 1], axis=0)
                            ).then_inc(got[b], 16)

                        run(pool_e, one)

                    @block.tensor
                    def _(pe):
                        def product(bank, xh, xl, c, b, e, half, ks, cols, start, stop):
                            pe.wait_ge(w_high, 6 * e + 2 * c + half + 1)
                            width = cols[1] - cols[0]

                            def rows(w, k):
                                w3 = part(w, c, b, half).rearrange("p (k c) -> p k c", k=len(ks))
                                return w3[:, k, cols[0]:cols[1]]

                            for n, k in enumerate(ks):
                                nc.tensor.matmul(psum[:, bank, 0:width], xh[:, k, :], rows(wH, n),
                                                 start=(start and n == 0), stop=False)
                                nc.tensor.matmul(psum[:, bank, 0:width], xl[:, k, :], rows(wH, n),
                                                 start=False, stop=False)
                            pe.wait_ge(w_rest, 6 * e + 2 * c + half + 1)
                            for n, k in enumerate(ks):
                                ins = nc.tensor.matmul(psum[:, bank, 0:width], xh[:, k, :], rows(wL, n),
                                                       start=False, stop=(stop and n == len(ks) - 1))
                            return ins

                        def turn_x(i, b, e, first):
                            pe.wait_ge(got[b], 16 * (i + 1) + got_base[b])
                            if not first:
                                pe.wait_ge(xl_ok, e)
                            for k in range(KD):
                                last = nc.tensor.transpose(psum[:, k // 4, (k % 4) * P:(k % 4 + 1) * P],
                                                           xg[:, b, k * P:(k + 1) * P], ident[:])
                                if k == 3:
                                    last.then_inc(x_lo, 1)
                            last.then_inc(x_hi, 1)

                        def one(i, b, e, first, last):
                            pe.wait_ge(xl_ok, e + 1)
                            for c, bank, done, read in ((0, 2, h1, silu_ok), (1, 3, h3, hid_ok)):
                                if not (first and b == 0):
                                    pe.wait_ge(read, e)
                                for half in range(2):
                                    ins = product(bank, xgH, xgL, c, b, e, half, range(4 * half, 4 * half + 4),
                                                  (0, DE), half == 0, half == 1)
                                ins.then_inc(done, 1)
                            if not last:
                                turn_x(i + b, 1 - b, e + 1, False)
                            pe.wait_ge(hid_ok, e + 1)
                            for k in range(4):
                                ins = nc.tensor.transpose(psum[:, 4, k * P:(k + 1) * P],
                                                          hid[:, k * P:(k + 1) * P], ident[:])
                            ins.then_inc(h_turned, 1)
                            pe.wait_ge(hl_ok, e + 1)
                            if not (first and b == 0):
                                pe.wait_ge(ye_lo, e)
                                pe.wait_ge(ye_hi, e)
                            for half in range(2):
                                for out_half, done in ((0, y_lo), (1, y_hi)):
                                    ins = product(5 + out_half, hidH, hidL, 2, b, e, half,
                                                  range(2 * half, 2 * half + 2),
                                                  (512 * out_half, 512 * out_half + 512), half == 0, half == 1)
                                    if half == 1:
                                        ins.then_inc(done, 1)

                        turn_x(0, 0, 0, True)
                        run(pe, one)

                    def quarter(bank):
                        return psum[:, bank, :].rearrange("p (k t) -> p k t", k=4)

                    @block.scalar
                    def _(act):
                        def split(c, b, e, half, first):
                            if half == 0:
                                act.wait_ge(chunk_in[(s0 + c) % RING], 16 * ((s0 + c) // RING + 1 + e))
                                if c == 2:
                                    act.wait_ge(h1, e + 1)
                                elif not (first and b == 0):
                                    act.wait_ge((h3, y_hi)[c], e)
                            nc.scalar.copy(part(wH, c, b, half), raw(c, half)).then_inc(w_high, 1)

                        def move_x(e):
                            for half, turned in ((0, x_lo), (1, x_hi)):
                                act.wait_ge(turned, e + 1)
                                nc.scalar.copy(xgH[:, 4 * half:4 * half + 4, :], quarter(half)).then_inc(xh_ok, 1)

                        def store_y(i, b, e, first):
                            act.wait_ge(y_lo, e + 1)
                            if not first:
                                act.wait_ge(put[b], 16 * i)
                            nc.scalar.copy(y[:, b, 0:512], psum[:, 5, :]).then_inc(ye_lo, 1)

                        def send_y(b, e):
                            act.wait_ge(ye_lo, e + 1)
                            act.wait_ge(ye_hi, e + 1)
                            act.dma_start(y_d[bass.ds(e * P, P), :], y[:, b, :]).then_inc(put[b], 16)

                        def one(i, b, e, first, last):
                            split(0, b, e, 0, first)
                            split(0, b, e, 1, first)
                            if not (first and b == 0):
                                store_y(i - (1 - b), 1 - b, e - 1, first)
                            split(1, b, e, 0, first)
                            split(1, b, e, 1, first)
                            if not (first and b == 0):
                                send_y(1 - b, e - 1)
                            act.wait_ge(h1, e + 1)
                            if not (first and b == 0):
                                act.wait_ge(hid_ok, e)
                            nc.scalar.activation(act_h[:], psum[:, 2, :], ACT.Silu).then_inc(silu_ok, 1)
                            split(2, b, e, 0, first)
                            split(2, b, e, 1, first)
                            if not last:
                                move_x(e + 1)
                            act.wait_ge(h_turned, e + 1)
                            nc.scalar.copy(hidH[:], quarter(4)).then_inc(hh_ok, 1)
                            if last:
                                store_y(i, b, e, first)
                                send_y(b, e)

                        move_x(0)
                        run(act, one)

                    @block.vector
                    def _(dve):
                        def rest(out, whole, high):
                            return nc.vector.tensor_tensor(out, whole, high.bitcast(F32), ALU.subtract)

                        def split(c, b, e, half):
                            dve.wait_ge(w_high, 6 * e + 2 * c + half + 1)
                            rest(part(wL, c, b, half), raw(c, half), part(wH, c, b, half)).then_inc(w_rest, 1)

                        def move_x(e):
                            for half in range(2):
                                dve.wait_ge(xh_ok, 2 * e + half + 1)
                                ks = slice(4 * half, 4 * half + 4)
                                ins = rest(xgL[:, ks, :], quarter(half), xgH[:, ks, :])
                            ins.then_inc(xl_ok, 1)

                        def store_y(i, b, e, first):
                            dve.wait_ge(y_hi, e + 1)
                            if not first:
                                dve.wait_ge(put[b], 16 * i)
                            nc.vector.tensor_copy(y[:, b, 512:1024], psum[:, 6, :]).then_inc(ye_hi, 1)

                        def one(i, b, e, first, last):
                            split(0, b, e, 0)
                            split(0, b, e, 1)
                            if not (first and b == 0):
                                store_y(i - (1 - b), 1 - b, e - 1, first)
                            split(1, b, e, 0)
                            split(1, b, e, 1)
                            split(2, b, e, 0)
                            dve.wait_ge(silu_ok, e + 1)
                            dve.wait_ge(h3, e + 1)
                            nc.vector.tensor_tensor(hid[:], act_h[:], psum[:, 3, :], ALU.mult).then_inc(hid_ok, 1)
                            split(2, b, e, 1)
                            dve.wait_ge(hh_ok, e + 1)
                            rest(hidL[:], quarter(4), hidH[:]).then_inc(hl_ok, 1)
                            if not last:
                                move_x(e + 1)
                            if last:
                                store_y(i, b, e, first)

                        move_x(0)
                        run(dve, one)
                for b in range(2):
                    gathered[b] += 16 * (NE // 2)
                for c in range(3):
                    issued[(s0 + c) % RING] = (s0 + 3 * (NE - 1) + c) // RING + 1 + (s0 + 3 * NE + c < S_END)
                end_phase()

        @phase
        def overflow(layer, slots, ctrl):
            (idx_ok, w1_in, w3_in, w2_in, x_turned, xt_lo, xt_hi, h_ok, silu_ok, hid_ok, h_turned, h_moved, y_ok, ye_lo, ye_hi,
             put, met) = take(17)
            w_in = (w1_in, w3_in, w2_in)
            got = over_in[layer]
            with ExitStack() as st:
                nm = str(layer)
                idx = sb(st, "oidx" + nm, [P, 1], I32)
                xg = sb(st, "oxg" + nm, [P, D])
                xgT = sb(st, "oxgT" + nm, [P, KD, P])
                act_h = sb(st, "oact_h" + nm, [P, DE])
                hid = sb(st, "ohid" + nm, [P, DE])
                hidT = sb(st, "ohidT" + nm, [P, 4, P])
                y = sb(st, "oy" + nm, [P, D])
                w = sb(st, "ow" + nm, [P, 3, 4096])

                def run(eng, one):
                    n = eng.value_load(ctrl[0:1, 0:1], min_val=0, max_val=OVER)
                    with eng.If(n > 0):
                        with eng.Fori(0, n) as i:
                            one(i)
                            eng.wait_ge(put, 16 * (i + 1))
                            eng.sem_inc(met, 1)

                def quarter(bank):
                    return psum[:, bank, :].rearrange("p (k t) -> p k t", k=4)

                with nc.Block() as block:
                    @block.sync
                    def _(sp):
                        def one(i):
                            e = sp.value_load(ctrl[0:1, bass.ds(i + 1, 1)], min_val=0, max_val=NE - 1)
                            for c in range(3):
                                src = expert_src(layer, e, c)
                                sp.dma_start(w[:, c, :].rearrange("p (k c) -> p k c", k=src.shape[1]), src
                                             ).then_inc(w_in[c], 16)
                            sp.wait_ge(ye_lo, i + 1)
                            sp.wait_ge(ye_hi, i + 1)
                            sp.dma_start(y_d[bass.ds((i + NE) * P, P), :], y[:]).then_inc(put, 16)

                        run(sp, one)

                    @block.gpsimd
                    def _(pool_e):
                        def one(i):
                            nc.gpsimd.tensor_copy(idx[:], slots[:, bass.ds(i + NE, 1)]).then_inc(idx_ok, 1)
                            pool_e.wait_ge(idx_ok, i + 1)
                            pool_e.sem_inc(met, 1)
                            pool_e.indirect_dma_start(
                                out=xg[:], out_offset=None, in_=xn_d[:, :],
                                in_offset=bass.IndirectOffsetOnAxis(ap=idx[:], axis=0)
                            ).then_inc(got, 16)

                        run(pool_e, one)

                    @block.tensor
                    def _(pe):
                        def one(i):
                            pe.wait_ge(got, 16 * (i + 1))
                            for k in range(KD):
                                ins = nc.tensor.transpose(psum[:, k // 4, (k % 4) * P:(k % 4 + 1) * P],
                                                          xg[:, k * P:(k + 1) * P], ident[:])
                            ins.then_inc(x_turned, 1)
                            pe.wait_ge(xt_lo, i + 1)
                            pe.wait_ge(xt_hi, i + 1)
                            for c in range(2):
                                wc = w[:, c, :].rearrange("p (k c) -> p k c", k=8)
                                pe.wait_ge(w_in[c], 16 * (i + 1))
                                for k in range(KD):
                                    ins = nc.tensor.matmul(psum[:, 2 + c, :], xgT[:, k, :], wc[:, k, :],
                                                           start=(k == 0), stop=(k == KD - 1))
                            ins.then_inc(h_ok, 1)
                            pe.wait_ge(hid_ok, i + 1)
                            for k in range(4):
                                ins = nc.tensor.transpose(psum[:, 4, k * P:(k + 1) * P], hid[:, k * P:(k + 1) * P],
                                                          ident[:])
                            ins.then_inc(h_turned, 1)
                            pe.wait_ge(h_moved, i + 1)
                            wc = w[:, 2, :].rearrange("p (k c) -> p k c", k=4)
                            pe.wait_ge(w_in[2], 16 * (i + 1))
                            for half in range(2):
                                for k in range(4):
                                    ins = nc.tensor.matmul(psum[:, 5 + half, :], hidT[:, k, :],
                                                           wc[:, k, half * 512:(half + 1) * 512],
                                                           start=(k == 0), stop=(k == 3))
                            ins.then_inc(y_ok, 1)

                        run(pe, one)

                    @block.scalar
                    def _(act):
                        def one(i):
                            act.wait_ge(x_turned, i + 1)
                            nc.scalar.copy(xgT[:, 0:4, :], quarter(0)).then_inc(xt_lo, 1)
                            act.wait_ge(h_ok, i + 1)
                            nc.scalar.activation(act_h[:], psum[:, 2, :], ACT.Silu).then_inc(silu_ok, 1)
                            act.wait_ge(y_ok, i + 1)
                            nc.scalar.copy(y[:, 0:512], psum[:, 5, :]).then_inc(ye_lo, 1)

                        run(act, one)

                    @block.vector
                    def _(dve):
                        def one(i):
                            dve.wait_ge(x_turned, i + 1)
                            nc.vector.tensor_copy(xgT[:, 4:8, :], quarter(1)).then_inc(xt_hi, 1)
                            dve.wait_ge(silu_ok, i + 1)
                            nc.vector.tensor_tensor(hid[:], act_h[:], psum[:, 3, :], ALU.mult).then_inc(hid_ok, 1)
                            dve.wait_ge(h_turned, i + 1)
                            nc.vector.tensor_copy(hidT[:], quarter(4)).then_inc(h_moved, 1)
                            dve.wait_ge(y_ok, i + 1)
                            nc.vector.tensor_copy(y[:, 512:1024], psum[:, 6, :]).then_inc(ye_hi, 1)

                        run(dve, one)
                end_phase()

        @phase
        def combine(layer, row_of, gates, dst, gain):
            (x_in, gain_in, first_ok, done, stored, squared, mean_ok, root_ok, recip_ok, xn_ok, tr_lo, tr_hi,
             copied_lo, copied_hi) = take(14)
            got, got_base = gather_in, list(gathered)
            with ExitStack() as st:
                nm = str(layer)
                x_all = sb(st, "xc" + nm, [P, NT, D])
                yk = sb(st, "yk" + nm, [P, 2, 2, D])
                g_bc = sb(st, "next_gain" + nm, [P, D])
                sq = sb(st, "sq_c" + nm, [P, D])
                xn = sb(st, "xn_c" + nm, [P, 2, D])
                ss, ms, sd, rs = (sb(st, f"{n}_c{nm}", [P, NT]) for n in ("ss", "ms", "sd", "rs"))
                rows = xs.rearrange("(j p) d -> p j d", p=P)
                drows = dst.rearrange("(j p) d -> p j d", p=P)
                with nc.Block() as block:
                    @block.sync
                    def _(sp):
                        sp.dma_start(x_all[:], rows).then_inc(x_in, 16)
                        if gain is not None:
                            sp.dma_start(g_bc[:], gain.partition_broadcast(P)).then_inc(gain_in, 16)
                        for j in range(NT):
                            sp.wait_ge(done, j + 1)
                            sp.dma_start(drows[:, j, :], x_all[:, j, :]).then_inc(stored, 16)
                        sp.wait_ge(stored, 16 * NT)

                    @block.gpsimd
                    def _(pool_e):
                        for j in range(NT):
                            if j >= 2:
                                pool_e.wait_ge(done, j - 1)
                            for k in range(2):
                                n = k * NT + j
                                pool_e.indirect_dma_start(
                                    out=yk[:, j % 2, k, :], out_offset=None, in_=y_d[:, :],
                                    in_offset=bass.IndirectOffsetOnAxis(ap=row_of[:, n:n + 1], axis=0)
                                ).then_inc(got[j % 2], 16)

                    if gain is not None:
                        @block.scalar
                        def _(act):
                            def move(j):
                                act.wait_ge(tr_lo, j + 1)
                                nc.scalar.copy(xnT[:, 0:4, j * P:(j + 1) * P],
                                               psum[:, 2 * (j % 4), :].rearrange("p (k t) -> p k t", k=4)
                                               ).then_inc(copied_lo, 1)

                            for j in range(NT):
                                act.wait_ge(done, j + 1)
                                if j:
                                    act.wait_ge(squared, j)
                                nc.scalar.activation(sq[:], x_all[:, j, :], ACT.Square,
                                                     accum_out=ss[:, j:j + 1]).then_inc(squared, 1)
                                act.wait_ge(mean_ok, j + 1)
                                nc.scalar.activation(sd[:, j:j + 1], ms[:, j:j + 1], ACT.Sqrt).then_inc(root_ok, 1)
                                if j:
                                    move(j - 1)
                            move(NT - 1)

                        @block.tensor
                        def _(pe):
                            for j in range(NT):
                                pe.wait_ge(xn_ok, j + 1)
                                if j >= 4:
                                    pe.wait_ge(copied_lo, j - 3)
                                    pe.wait_ge(copied_hi, j - 3)
                                for k in range(KD):
                                    last = nc.tensor.transpose(
                                        psum[:, 2 * (j % 4) + k // 4, (k % 4) * P:(k % 4 + 1) * P],
                                        xn[:, j % 2, k * P:(k + 1) * P], ident[:])
                                    if k == 3:
                                        last.then_inc(tr_lo, 1)
                                last.then_inc(tr_hi, 1)

                    @block.vector
                    def _(dve):
                        def move(j):
                            dve.wait_ge(tr_hi, j + 1)
                            nc.vector.tensor_copy(xnT[:, 4:8, j * P:(j + 1) * P],
                                                  psum[:, 2 * (j % 4) + 1, :].rearrange("p (k t) -> p k t", k=4)
                                                  ).then_inc(copied_hi, 1)

                        def normalise(j):
                            one = slice(j, j + 1)
                            dve.wait_ge(squared, j + 1)
                            nc.vector.tensor_scalar(ms[:, one], ss[:, one], 1.0 / D, EPS, ALU.mult, ALU.add
                                                    ).then_inc(mean_ok, 1)
                            dve.wait_ge(root_ok, j + 1)
                            nc.vector.reciprocal(rs[:, one], sd[:, one]).then_inc(recip_ok, 1)
                            dve.wait_ge(recip_ok, j + 1)
                            if j == 0:
                                dve.wait_ge(gain_in, 16)
                            if j >= 2:
                                dve.wait_ge(tr_hi, j - 1)
                            nc.vector.scalar_tensor_tensor(out=xn[:, j % 2, :], in0=x_all[:, j, :], scalar=rs[:, one],
                                                           in1=g_bc[:], op0=ALU.mult, op1=ALU.mult).then_inc(xn_ok, 1)
                            if j:
                                move(j - 1)

                        dve.wait_ge(x_in, 16)
                        for j in range(NT):
                            dve.wait_ge(got[j % 2], 32 * (j // 2 + 1) + got_base[j % 2])
                            for k, ok in ((0, first_ok), (1, done)):
                                nc.vector.scalar_tensor_tensor(out=x_all[:, j, :], in0=yk[:, j % 2, k, :],
                                                               scalar=gates[:, k * NT + j:k * NT + j + 1],
                                                               in1=x_all[:, j, :], op0=ALU.mult, op1=ALU.add
                                                               ).then_inc(ok, 1)
                                if k == 0:
                                    dve.wait_ge(first_ok, j + 1)
                            if gain is not None and j:
                                normalise(j - 1)
                        if gain is not None:
                            normalise(NT - 1)
                            move(NT - 1)
                for b in range(2):
                    gathered[b] += 32 * (NT // 2)
                end_phase()

        def moe(layer, dst, gain):
            with ExitStack() as m:
                nm = str(layer)
                row_of = sb(m, "row_of" + nm, [P, 16], I32)
                gates = sb(m, "gates" + nm, [P, 16])
                slots = sb(m, "slots" + nm, [P, NBLKP], I32)
                ctrl = sb(m, "ctrl" + nm, [P, 17], I32)
                router(layer, row_of, gates, slots, ctrl)
                experts(layer, slots)
                overflow(layer, slots, ctrl)
                combine(layer, row_of, gates, dst, gain)

        @phase
        def ml_project_qk(qkT, G, xnH):
            (proj, padded, convolved, silued, weights_in, edges, evac, chain, x_high, x_rest, w_high, w_rest,
             gate_high, gate_rest) = take(14)
            with ExitStack() as st:
                up = sb(st, "ml_u_padded", [P, 2, T + 2])
                acc = sb(st, "ml_conv_acc", [P, 2, T])
                cw = sb(st, "ml_conv_w", [P, 8, 3])
                cb = sb(st, "ml_conv_b", [P, 8])
                gw = sb(st, "ml_gate_w", [P, KD, 4 * GROWS])
                gwH = sb(st, "ml_gate_w_high", [P, KD, 4 * GROWS], F32R)
                gwL = sb(st, "ml_gate_w_rest", [P, KD, 4 * GROWS], F32R)
                wH = sb(st, "w_high_ml", [P, 2, KD, P], F32R)
                CONV = 8

                def block_of(w, i):
                    c, ct = divmod(i, 4)
                    return w(S_ML + c)[:, :, ct * P:(ct + 1) * P]

                def x_piece(n):
                    half, quad = divmod(n, 2)
                    return (slice(None), slice(4 * quad, 4 * quad + 4), slice(half * 512, (half + 1) * 512))

                with nc.Block() as block:
                    @block.sync
                    def _(sp):
                        sp.dma_start(cw[:], I["ml_conv_w"]).then_inc(weights_in, 16)
                        sp.dma_start(cb[:], I["ml_conv_b"]).then_inc(weights_in, 16)
                        sp.dma_start(gw[:], I["ml_gate_w"]).then_inc(weights_in, 16)
                        refill(sp, S_ML, S_ML + 2, proj, 4)

                    @block.tensor
                    def _(pe):
                        for i in range(CONV):
                            pe.wait_ge(w_rest, i + 1)
                            if i >= 4:
                                pe.wait_ge(padded, i - 3)
                            for half in range(2):
                                ts = slice(half * 512, (half + 1) * 512)
                                for k in range(KD):
                                    if i == 0 and k % 4 == 0:
                                        pe.wait_ge(x_rest, 2 * half + k // 4 + 1)
                                    last = split_product(psum[:, 2 * (i % 4) + half, :],
                                                         (wH[:, i % 2, k, :], block_of(wide_rest, i)[:, k, :]),
                                                         (xnH[:, k, ts], xnL[:, k, ts]), k == 0, k == KD - 1)
                            last.then_inc(proj, 1)
                        pe.wait_ge(gate_rest, 1)
                        for j in range(NT):
                            js = slice(j * P, (j + 1) * P)
                            if j % 2 == 0:
                                pe.wait_ge(padded, j // 2 + 5)
                            for k in range(KD):
                                last = split_product(psum[:, j, 0:4 * GROWS], (xnH[:, k, js], xnL[:, k, js]),
                                                     (gwH[:, k, :], gwL[:, k, :]), k == 0, k == KD - 1)
                            last.then_inc(proj, 1)

                    @block.scalar
                    def _(act):
                        def split_w(i):
                            if i < CONV:
                                if i % 4 == 0:
                                    chunk_wait(act, S_ML + i // 4)
                                if i >= 2:
                                    act.wait_ge(proj, i - 1)
                                nc.scalar.copy(wH[:, i % 2, :, :], block_of(wide, i)).then_inc(w_high, 1)

                        def silu(i):
                            act.wait_ge(convolved, i + 1)
                            nc.scalar.activation(qkT[:, i, :], acc[:, i % 2, :], ACT.Silu).then_inc(silued, 1)

                        split_w(0)
                        for n in range(4):
                            nc.scalar.copy(xnH[x_piece(n)], xnT[x_piece(n)]).then_inc(x_high, 1)
                        split_w(1)
                        act.wait_ge(weights_in, 48)
                        nc.scalar.copy(gwH[:], gw[:]).then_inc(gate_high, 1)
                        for i in range(CONV):
                            act.wait_ge(proj, i + 1)
                            if i >= 2:
                                act.wait_ge(convolved, i - 1)
                            nc.scalar.copy(up[:, i % 2, 1:T + 1],
                                           psum[:, 2 * (i % 4):2 * (i % 4) + 2, :].rearrange("p a b -> p (a b)")
                                           ).then_inc(padded, 1)
                            split_w(i + 2)
                            if i:
                                silu(i - 1)
                        silu(CONV - 1)
                        for j in range(NT):
                            act.wait_ge(proj, CONV + j + 1)
                            nc.scalar.copy(G[:, j, :], psum[:, j, 0:4 * GROWS]).then_inc(evac, 1)

                    @block.vector
                    def _(dve):
                        did = Tally(chain)

                        def split_w(i):
                            if i < CONV:
                                dve.wait_ge(w_high, i + 1)
                                rest_of(block_of(wide_rest, i), block_of(wide, i), wH[:, i % 2, :, :]
                                        ).then_inc(w_rest, 1)

                        split_w(0)
                        for n in range(4):
                            dve.wait_ge(x_high, n + 1)
                            rest_of(xnL[x_piece(n)], xnT[x_piece(n)], xnH[x_piece(n)]).then_inc(x_rest, 1)
                        split_w(1)
                        nc.vector.memset(up[:, :, 0:1], 0.0).then_inc(edges, 1)
                        nc.vector.memset(up[:, :, T + 1:T + 2], 0.0).then_inc(edges, 1)
                        dve.wait_ge(edges, 2)
                        dve.wait_ge(gate_high, 1)
                        dve.wait_ge(weights_in, 48)
                        rest_of(gwL[:], gw[:], gwH[:]).then_inc(gate_rest, 1)
                        for i in range(CONV):
                            split_w(i + 2)
                            a, u = acc[:, i % 2, :], up[:, i % 2, :]
                            dve.wait_ge(padded, i + 1)
                            if i >= 2:
                                dve.wait_ge(silued, i - 1)
                            m = did(nc.vector.tensor_scalar(a, u[:, 0:T], cw[:, i, 0:1], cb[:, i:i + 1],
                                                            ALU.mult, ALU.add))
                            dve.wait_ge(chain, m)
                            m = did(nc.vector.scalar_tensor_tensor(out=a, in0=u[:, 1:T + 1], scalar=cw[:, i, 1:2],
                                                                   in1=a, op0=ALU.mult, op1=ALU.add))
                            dve.wait_ge(chain, m)
                            nc.vector.scalar_tensor_tensor(out=a, in0=u[:, 2:T + 2], scalar=cw[:, i, 2:3],
                                                           in1=a, op0=ALU.mult, op1=ALU.add).then_inc(convolved, 1)
                end_phase()

        @phase
        def ml_project_vo(vA, xnH):
            (proj, evac, staged0, staged1, edges, w_high, w_rest) = take(7)
            staged = (staged0, staged1)
            with ExitStack() as st:
                so = sb(st, "ml_sigmoid_o", [P, 2, MV])
                wH = sb(st, "w_high_vo", [P, 2, KD, MV], F32R)
                C0 = S_ML + 2
                HEADS = 2 * MH
                STEPS, O0 = HEADS * NT, MH * NT

                def columns(w, n):
                    return w(C0 + n // 2)[:, :, (n % 2) * MV:(n % 2 + 1) * MV]

                with nc.Block() as block:
                    @block.sync
                    def _(sp):
                        refill(sp, C0, S_OUT1, proj, 2 * NT)

                    @block.tensor
                    def _(pe):
                        for s in range(STEPS):
                            n, j = divmod(s, NT)
                            js = slice(j * P, (j + 1) * P)
                            if j == 0:
                                pe.wait_ge(w_rest, n + 1)
                            if s >= 8:
                                pe.wait_ge(evac, s - 7)
                            for k in range(KD):
                                last = split_product(psum[:, s % 8, 0:MV], (xnH[:, k, js], xnL[:, k, js]),
                                                     (wH[:, n % 2, k, :], columns(wide_rest, n)[:, k, :]),
                                                     k == 0, k == KD - 1)
                            last.then_inc(proj, 1)

                    @block.scalar
                    def _(act):
                        def split_w(n):
                            if n < HEADS:
                                if n % 2 == 0:
                                    chunk_wait(act, C0 + n // 2)
                                if n >= 2:
                                    act.wait_ge(proj, NT * (n - 1))
                                nc.scalar.copy(wH[:, n % 2, :, :], columns(wide, n)).then_inc(w_high, 1)

                        split_w(0)
                        split_w(1)
                        act.wait_ge(edges, 1)
                        for s in range(STEPS):
                            n, j = divmod(s, NT)
                            act.wait_ge(proj, s + 1)
                            bank = psum[:, s % 8, 0:MV]
                            if s < O0:
                                nc.scalar.copy(vA[:, j, n, 0:MV], bank).then_inc(evac, 1)
                            else:
                                b = s % 2
                                if s - O0 >= 2:
                                    act.wait_ge(staged[b], 16 * ((s - O0) // 2))
                                nc.scalar.activation(so[:, b, :], bank, ACT.Sigmoid).then_inc(evac, 1)
                                act.wait_ge(evac, s + 1)
                                act.dma_start(so_d[j * P:(j + 1) * P, (n - MH) * MV:(n - MH + 1) * MV], so[:, b, :]
                                              ).then_inc(staged[b], 16)
                            if j == NT - 1:
                                split_w(n + 2)
                        for b in range(2):
                            act.wait_ge(staged[b], 16 * (O0 // 2))

                    @block.vector
                    def _(dve):
                        nc.vector.memset(vA[:, :, :, MV:MVA], 1.0).then_inc(edges, 1)
                        for n in range(HEADS):
                            dve.wait_ge(w_high, n + 1)
                            rest_of(columns(wide_rest, n), columns(wide, n), wH[:, n % 2, :, :]).then_inc(w_rest, 1)
                end_phase()

        @phase
        def ml_gates(G, cols, colb, apr, qkT, kn):
            (bias_in, rows_ok, shifted, sized, expd, logd, ready, powered, turned, moved, flipped, diag_ok,
             chain, k_turned, k_moved) = take(15)
            with ExitStack() as st:
                gb = sb(st, "gate_bias", [GROWS, 2])
                mst = sb(st, "carried_max", [GROWS, NT + 1])
                ap = sb(st, "decay_rows", [GROWS, NT])
                dg = sb(st, "decay_diag", [GROWS, NT, GROWS])
                R = [xnT[0:GROWS, n, :] for n in range(8)]
                XF, KW, LF, LI, BC, A, M, WI = R
                ENM, NEGM = XF, LF

                def chunked(row):
                    return row.rearrange("g (c t) -> g c t", c=NT)

                with nc.Block() as block:
                    @block.sync
                    def _(sp):
                        sp.dma_start(gb[:], I["ml_gate_b"]).then_inc(bias_in, 16)

                    @block.tensor
                    def _(pe):
                        for gate in range(2):
                            for c in range(NT):
                                dst = psum[0:GROWS, 2 * gate + c // 4, (c % 4) * P:(c % 4 + 1) * P]
                                o = 2 * GROWS * gate
                                nc.tensor.matmul(dst, G[:, c, o:o + GROWS], ident[:], start=True, stop=False)
                                last = nc.tensor.matmul(dst, G[:, NT - 1 - c, o + GROWS:o + 2 * GROWS], flip[:],
                                                        start=False, stop=True)
                        last.then_inc(rows_ok, 1)
                        for j in range(NT):
                            if j >= 2:
                                pe.wait_ge(k_moved, j - 1)
                            for h in range(MH):
                                last = nc.tensor.transpose(psum[:, 4 + j % 2, h * P:(h + 1) * P],
                                                           qkT[:, 4 + h, j * P:(j + 1) * P], ident[:])
                            last.then_inc(k_turned, 1)
                        pe.wait_ge(k_moved, NT)
                        pe.wait_ge(powered, 3)
                        pe.wait_ge(ready, 1)
                        for n in range(5 * NT):
                            q, c = divmod(n, NT)
                            row = (A, WI, ENM, KW, NEGM)[q]
                            last = nc.tensor.transpose(psum[:, 4 + n // 14, (n % 14) * GROWS:(n % 14 + 1) * GROWS],
                                                       row[:, c * P:(c + 1) * P], ident[0:GROWS, 0:GROWS])
                        last.then_inc(turned, 1)
                        pe.wait_ge(moved, 3)
                        nc.tensor.matmul(psum[:, 7, 0:160], flip[:], cols[:, :, :, 32:36],
                                         start=True, stop=True).then_inc(flipped, 1)
                        pe.wait_ge(diag_ok, 1)
                        nc.tensor.matmul(psum[:, 4, 0:NT * GROWS], ones[0:GROWS, :],
                                         dg[:].rearrange("g c h -> g (c h)"), start=True, stop=True
                                         ).then_inc(flipped, 1)

                    @block.scalar
                    def _(act):
                        act.wait_ge(shifted, 1)
                        nc.scalar.activation(KW, XF, ACT.Abs).then_inc(sized, 1)
                        act.wait_ge(sized, 1)
                        nc.scalar.activation(KW, KW, ACT.Exp, scale=-1.0).then_inc(expd, 1)
                        act.wait_ge(expd, 1)
                        nc.scalar.activation(KW, KW, ACT.Ln, bias=1.0).then_inc(logd, 1)
                        for j in range(NT):
                            act.wait_ge(k_turned, j + 1)
                            nc.scalar.copy(kn[:, j, :], psum[:, 4 + j % 2, :]).then_inc(k_moved, 1)
                        act.wait_ge(shifted, 2)
                        nc.scalar.activation(ap[:], ap[:], ACT.Exp).then_inc(expd, 1)
                        nc.scalar.activation(WI, WI, ACT.Exp).then_inc(powered, 1)
                        nc.scalar.activation(ENM, ENM, ACT.Exp, scale=-1.0).then_inc(powered, 1)
                        nc.scalar.activation(KW, KW, ACT.Exp).then_inc(powered, 1)

                    @block.vector
                    def _(dve):
                        V = nc.vector
                        did = Tally(chain)

                        def step(ins):
                            dve.wait_ge(chain, did(ins))

                        def two(b):
                            return psum[0:GROWS, b:b + 2, :].rearrange("p a b -> p (a b)")

                        dve.wait_ge(bias_in, 16)
                        dve.wait_ge(rows_ok, 1)
                        V.tensor_scalar(XF, two(2), gb[:, 1:2], None, ALU.add).then_inc(shifted, 1)
                        did(V.tensor_scalar(LI, two(0), gb[:, 0:1], None, ALU.add))
                        did(V.memset(mst[:, 0:1], 0.0))
                        dve.wait_ge(chain, did.n)
                        dve.wait_ge(logd, 1)
                        step(V.scalar_tensor_tensor(out=LF, in0=XF, scalar=0.0, in1=KW, op0=ALU.min,
                                                    op1=ALU.subtract))
                        for c in range(NT):
                            t = slice(c * P, (c + 1) * P)
                            did(V.tensor_tensor_scan(BC[:, t], ones[0:GROWS, :], LF[:, t], 0.0, ALU.mult, ALU.add))
                        dve.wait_ge(chain, did.n)
                        step(V.tensor_tensor(A, LI, BC, ALU.subtract))
                        for c in range(NT):
                            t, end = slice(c * P, (c + 1) * P), slice((c + 1) * P - 1, (c + 1) * P)
                            step(V.tensor_tensor_scan(M[:, t], A[:, t], A[:, t], mst[:, c:c + 1], ALU.max, ALU.max))
                            step(V.tensor_tensor(mst[:, c + 1:c + 2], BC[:, end], M[:, end], ALU.add))
                        last = chunked(M)[:, :, P - 1:P]
                        did(V.tensor_tensor(chunked(WI), mst[:, 0:NT].unsqueeze(2).broadcast_to([GROWS, NT, P]),
                                            chunked(M), ALU.subtract))
                        did(V.tensor_tensor(ENM, BC, M, ALU.add))
                        did(V.tensor_tensor(chunked(KW), chunked(A), last.broadcast_to([GROWS, NT, P]), ALU.subtract))
                        dve.wait_ge(chain, did.n)
                        V.tensor_tensor(ap[:].unsqueeze(2), mst[:, 0:NT].unsqueeze(2), last, ALU.subtract
                                        ).then_inc(shifted, 1)
                        V.tensor_scalar(NEGM, M, -1.0, None, ALU.mult).then_inc(ready, 1)
                        dve.wait_ge(expd, 2)
                        V.tensor_tensor(dg[:], ap[:].unsqueeze(2).broadcast_to([GROWS, NT, GROWS]),
                                        ident[0:GROWS, 0:GROWS].unsqueeze(1).broadcast_to([GROWS, NT, GROWS]),
                                        ALU.mult).then_inc(diag_ok, 1)
                        dve.wait_ge(turned, 1)
                        flat = cols[:].rearrange("p q c g -> p (q c g)")
                        for b in range(3):
                            n = min(14, 5 * NT - 14 * b) * GROWS
                            V.tensor_copy(flat[:, b * 14 * GROWS:b * 14 * GROWS + n], psum[:, 4 + b, 0:n]
                                          ).then_inc(moved, 1)
                        dve.wait_ge(flipped, 1)
                        dve.wait_ge(moved, 3)
                        step(V.tensor_copy(colb[:], psum[:, 7, 0:160].rearrange("p (q c h) -> p q c h", q=5, c=NT)))
                        did(V.tensor_scalar(cols[:, 1, :, :], cols[:, 1, :, :], KSCALE, None, ALU.mult))
                        did(V.tensor_scalar(colb[:, 1, :, :], colb[:, 1, :, :], KSCALE, None, ALU.mult))
                        dve.wait_ge(flipped, 2)
                        did(V.tensor_copy(apr[:], psum[:, 4, 0:NT * GROWS].rearrange("p (c g) -> p c g", c=NT)))
                end_phase()

        @phase
        def ml_scan(qkT, kn, vA, cols, colb, apr, hs):
            (s_ok, qc_ok, v_ok, cc_ok, e_ok, w_ok, scw_ok, t_ok, num_ok, h_ok, c_ok, kw_ok, den_ok,
             chain, recip_ok) = take(15)
            with ExitStack() as st:
                C = sb(st, "ml_state", [P, 2 * MH, MVA])
                e0 = sb(st, "ml_exponent", [P, 2, P])
                wT = sb(st, "ml_weight", [P, 2, P])
                scw = sb(st, "ml_scores", [P, 2, P])
                kw = sb(st, "ml_kw", [P, 2, P])
                t1 = sb(st, "ml_inter", [P, 3, MVA])
                num = sb(st, "ml_num", [P, 2, MVA])
                den = sb(st, "ml_den", [P, 2, 2])
                UNITS = NT * 2 * MH
                SB, QB = (0, 1, 3), 2
                FIRST = UNITS // 2
                STATED = UNITS - 2 * MH

                def unit(u):
                    c, gi = divmod(u, 2 * MH)
                    d, h = divmod(gi, MH)
                    n = NT - 1 - c if d else c
                    col = (lambda q: colb[:, q, c, h:h + 1]) if d else (lambda q: cols[:, q, c, h:h + 1])
                    return c, d, h, gi, n, col

                with nc.Block() as block:
                    @block.tensor
                    def _(pe):
                        def scores(u):
                            c, d, h, gi, n, col = unit(u)
                            b = SB[u % 3]
                            t = slice(n * P, (n + 1) * P)
                            if u >= 3:
                                pe.wait_ge(scw_ok, u - 2)
                            nc.tensor.matmul(psum[:, b, 0:P], qkT[:, 4 + h, t], qkT[:, h, t], start=True, stop=True)
                            nc.tensor.matmul(psum[:, b, P:2 * P], col(4).broadcast_to([P, P]), ident[:],
                                             start=True, stop=True).then_inc(s_ok, 1)
                            if c:
                                pe.wait_ge(c_ok, u - 2 * MH + 1)
                                if u - 2 * MH >= 1:
                                    pe.wait_ge(t_ok, u - 2 * MH)
                                nc.tensor.matmul(psum[:, QB, 0:MVA], qkT[:, h, t], C[:, gi, :],
                                                 start=True, stop=True).then_inc(qc_ok, 1)

                        def values(u):
                            c, d, h, gi, n, col = unit(u)
                            b = u % 2
                            pe.wait_ge(scw_ok, u + 1)
                            if u >= 2:
                                pe.wait_ge(num_ok, u - 1)
                            nc.tensor.matmul(psum[:, 4 + b, 0:MVA], scw[:, b, :], vA[:, n, h, :],
                                             start=True, stop=True).then_inc(v_ok, 1)
                            if u < STATED:
                                pe.wait_ge(kw_ok, u + 1)
                                if u >= 2:
                                    pe.wait_ge(c_ok, u - 1)
                                nc.tensor.matmul(psum[:, 6 + b, 0:MVA], kw[:, b, :], vA[:, n, h, :],
                                                 start=True, stop=True).then_inc(cc_ok, 1)

                        scores(0)
                        scores(1)
                        for u in range(UNITS):
                            if u + 2 < UNITS:
                                scores(u + 2)
                            values(u)

                    @block.scalar
                    def _(act):
                        def inter(u):
                            c, d, h, gi, n, col = unit(u)
                            if c:
                                act.wait_ge(qc_ok, u - 2 * MH + 1)
                                if u - 2 * MH >= 3:
                                    act.wait_ge(num_ok, u - 2)
                                nc.scalar.activation(t1[:, u % 3, :], psum[:, QB, 0:MVA], ACT.Copy,
                                                     scale=col(1)).then_inc(t_ok, 1)

                        def scaled(u):
                            c, d, h, gi, n, col = unit(u)
                            act.wait_ge(recip_ok, u + 1)
                            nc.scalar.activation(hs[:, n, h * MV:(h + 1) * MV], num[:, u % 2, 0:MV], ACT.Copy,
                                                 scale=den[:, u % 2, 1:2]).then_inc(h_ok, 1)

                        for u in range(UNITS):
                            act.wait_ge(e_ok, u + 1)
                            if u >= 2:
                                act.wait_ge(scw_ok, u - 1)
                            nc.scalar.activation(wT[:, u % 2, :], e0[:, u % 2, :], ACT.Exp).then_inc(w_ok, 1)
                            inter(u)
                            if 2 <= u < FIRST + 2:
                                scaled(u - 2)

                    @block.gpsimd
                    def _(pool_e):
                        for u in range(STATED):
                            c, d, h, gi, n, col = unit(u)
                            if u >= 2:
                                pool_e.wait_ge(cc_ok, u - 1)
                            nc.gpsimd.tensor_scalar(kw[:, u % 2, :], kn[:, n, h * P:(h + 1) * P], col(3), None,
                                                    ALU.mult).then_inc(kw_ok, 1)

                    @block.vector
                    def _(dve):
                        V = nc.vector
                        did = Tally(chain)

                        def exponent(u):
                            c, d, h, gi, n, col = unit(u)
                            dve.wait_ge(s_ok, u + 1)
                            if u >= 2:
                                dve.wait_ge(w_ok, u - 1)
                            V.scalar_tensor_tensor(out=e0[:, u % 2, :], in0=psum[:, SB[u % 3], P:2 * P], scalar=col(0),
                                                   in1=(cap_b if d else cap_f)[:], op0=ALU.add, op1=ALU.min
                                                   ).then_inc(e_ok, 1)

                        def weigh(u):
                            dve.wait_ge(w_ok, u + 1)
                            if u >= 2:
                                dve.wait_ge(v_ok, u - 1)
                            V.scalar_tensor_tensor(out=scw[:, u % 2, :], in0=psum[:, SB[u % 3], 0:P], scalar=KSCALE,
                                                   in1=wT[:, u % 2, :], op0=ALU.mult, op1=ALU.mult
                                                   ).then_inc(scw_ok, 1)

                        def finish(u):
                            c, d, h, gi, n, col = unit(u)
                            b = u % 2
                            dve.wait_ge(v_ok, u + 1)
                            if 2 <= u < FIRST + 2:
                                dve.wait_ge(h_ok, u - 1)
                            if c:
                                dve.wait_ge(t_ok, u - 2 * MH + 1)
                                V.tensor_tensor(num[:, b, :], t1[:, u % 3, :], psum[:, 4 + b, 0:MVA], ALU.add
                                                ).then_inc(num_ok, 1)
                            else:
                                V.tensor_copy(num[:, b, :], psum[:, 4 + b, 0:MVA]).then_inc(num_ok, 1)
                            if u < STATED:
                                dve.wait_ge(cc_ok, u + 1)
                                if c:
                                    V.scalar_tensor_tensor(out=C[:, gi, :], in0=C[:, gi, :],
                                                           scalar=apr[:, c, 32 * d + h:32 * d + h + 1],
                                                           in1=psum[:, 6 + b, 0:MVA], op0=ALU.mult, op1=ALU.add
                                                           ).then_inc(c_ok, 1)
                                else:
                                    V.tensor_copy(C[:, gi, :], psum[:, 6 + b, 0:MVA]).then_inc(c_ok, 1)
                            dve.wait_ge(num_ok, u + 1)
                            q = num[:, b, MV:MVA]
                            V.scalar_tensor_tensor(out=den[:, b, 0:1], in0=q, scalar=-1.0, in1=q, op0=ALU.mult,
                                                   op1=ALU.max).then_inc(den_ok, 1)
                            dve.wait_ge(den_ok, u + 1)
                            dve.wait_ge(chain, did(V.tensor_scalar(den[:, b, 0:1], den[:, b, 0:1], col(2), None,
                                                                   ALU.max)))
                            V.reciprocal(den[:, b, 1:2], den[:, b, 0:1]).then_inc(recip_ok, 1)
                            if c >= NT // 2:
                                dst = hs[:, n, h * MV:(h + 1) * MV]
                                dve.wait_ge(recip_ok, u + 1)
                                first = (NT - 1 - c) * 2 * MH + (1 - d) * MH + h
                                dve.wait_ge(h_ok, first + 1)
                                V.scalar_tensor_tensor(out=dst, in0=num[:, b, 0:MV], scalar=den[:, b, 1:2],
                                                       in1=dst, op0=ALU.mult, op1=ALU.add).then_inc(h_ok, 1)

                        exponent(0)
                        for u in range(UNITS):
                            if u + 1 < UNITS:
                                exponent(u + 1)
                            weigh(u)
                            if u:
                                finish(u - 1)
                        finish(UNITS - 1)
                end_phase()

        first_norm(I["x"], I["mix_norm"][0, :])
        with ExitStack() as mixer:
            with ExitStack() as att:
                qkT = sb(att, "qkT", [P, 2, AH, T], side="right")
                v = sb(att, "v_att", [P, NT, 512], side="right")
                attention_project(qkT, v)
                yT, yL = sb_pair(mixer, "yT", [P, KD, T])
                o = yT[:, 4:8, :].rearrange("p k t -> p (k t)").rearrange("p (j c) -> p j c", j=NT)
                attention(qkT, v, o)
                head_norm("att", o, AH, DV, I["ev_subln"], 1.0 - (0.8 - 0.6), None, yT)
            with ExitStack() as hy:
                z = sb(hy, "z", [P, HC, T])
                hinv = sb(hy, "hinv", [P, HC])
                with ExitStack() as proj:
                    hyena_project(z, yT, sb(proj, "xn_high", [P, KD, T], F32R, side="right"))
                zT = sb(hy, "zT", [P, NT, 512])
                both = xnT[:].rearrange("p k t -> p (k t)").rearrange("p (n c) -> p n c", c=512)
                hs, hd = both[:, 0:NT, :], both[:, NT:2 * NT, :]
                hyena_filter(z, zT, hs, hd, hinv)
                Z = sb(hy, "Z", [P, 4, NF, 512])
                hyena_forward(zT, hs, hd, Z)
                hyena_inverse(z, zT, Z, hinv, yT)
            out_phase("0", yT, yL, S_OUT0, I["x"], I["ffn_norm"][0, :])
        moe(0, xs, I["mix_norm"][1, :])
        hs = xnT[:].rearrange("p k t -> p (k t)").rearrange("p (j c) -> p j c", j=NT)
        with ExitStack() as ml:
            qkT = sb(ml, "ml_qkT", [P, 8, T])
            G = sb(ml, "ml_G", [P, NT, 4 * GROWS])
            with ExitStack() as proj:
                xnH = sb(proj, "xn_high1", [P, KD, T], F32R, side="right")
                ml_project_qk(qkT, G, xnH)
                vA = sb(ml, "ml_v", [P, NT, MH, MVA])
                ml_project_vo(vA, xnH)
            kn = sb(ml, "ml_k", [P, NT, 512])
            cols = sb(ml, "ml_cols", [P, 5, NT, GROWS])
            colb = sb(ml, "ml_colb", [P, 5, NT, MH])
            apr = sb(ml, "ml_decay", [P, NT, GROWS])
            ml_gates(G, cols, colb, apr, qkT, kn)
            ml_scan(qkT, kn, vA, cols, colb, apr, hs)
        with ExitStack() as ml:
            yT, yL = sb_pair(ml, "yT1", [P, KD, T])
            head_norm("ml", hs, MH, MV, I["od_out_norm"], 1.0, so_d, yT)
            out_phase("1", yT, yL, S_OUT1, xs, I["ffn_norm"][1, :])
        moe(1, out, None)
        if phases[0] >= LAST_PHASE[0]:
            with nc.Block() as block:
                @block.sync
                def _(sp):
                    for n in range(RING):
                        sp.wait_ge(chunk_in[n], 16 * issued[n])


def constants():
    f = np.float32
    i = np.arange(P)
    c = {
        "c_ident": np.eye(P, dtype=f),
        "c_flip": np.ascontiguousarray(np.eye(P, dtype=f)[::-1]),
        "c_ones": np.ones((P, P), f),
        "c_upper": (i[:, None] < i[None, :]).astype(f),
        "c_cap_f": np.where(i[:, None] <= i[None, :], 0.0, NEG).astype(f),
        "c_cap_b": np.where(i[:, None] >= i[None, :], 0.0, NEG).astype(f),
    }
    inv = (1.0 / (500000.0 ** (np.arange(0, ROPE, 2, dtype=np.float64) / ROPE))).astype(f)
    ang = (np.arange(T, dtype=f)[:, None] * inv[None, :]).astype(np.float64)
    cos, sin = np.cos(ang), np.sin(ang)
    def tiles(a):
        return np.ascontiguousarray(a.reshape(NT, P, -1).transpose(1, 0, 2)).astype(f)
    c["c_cos2"] = tiles(np.concatenate([cos, cos], 1))
    c["c_sin2"] = tiles(np.concatenate([-sin, sin], 1))
    t = np.linspace(0.0, 1.0, T, dtype=f)
    bands = np.linspace(1e-4, 15, 16, dtype=f)
    ang = (f(2.0 * np.pi / T) * np.arange(T, dtype=f)[:, None] * bands[None, :]).astype(np.float64)
    c["c_positions"] = np.ascontiguousarray(
        np.concatenate([t[:, None].astype(np.float64), np.cos(ang), -np.sin(ang)], 1).T).astype(f)
    c["c_delta"] = np.abs(np.linspace(np.log(1e-2) / 1.5, np.log(1e-2) / 0.3, 512, dtype=f))
    c["c_tneg"] = np.ascontiguousarray(-t.reshape(NF, P, 2).transpose(1, 2, 0).reshape(P, NT))
    k = np.arange(512)[:, None]
    m = np.arange(512)[None, :]
    tabs = []
    for par in range(2):
        theta = 2 * np.pi * ((k * (2 * m + par)) % 2048) / 2048
        tabs.append((np.cos(theta), np.sin(theta)))
    sign = (-1.0) ** np.arange(512)
    cs = [tabs[0][0], tabs[1][0], tabs[0][1].copy(), tabs[1][1].copy()]
    for s in (2, 3):
        cs[s][0, :] = sign
    fwd = np.stack([a.T for a in cs])
    c["c_dft"] = np.ascontiguousarray(
        fwd.reshape(4, NF, P, NF, P).transpose(3, 2, 0, 1, 4)).astype(f)
    inv = np.stack(cs) * (4.0 / 2048)
    inv[:, 0, :] /= 2
    c["c_idft"] = np.ascontiguousarray(inv.reshape(4, NF, P, 512).transpose(0, 2, 1, 3)).astype(f)
    c["c_router"] = np.concatenate([
        np.arange(NG, 0, -1), np.arange(EG, 0, -1), np.arange(NE), P * np.arange(1, 8), np.arange(P),
        np.arange(NBLKP), np.arange(16)]).astype(f)
    c["c_tok"] = np.ascontiguousarray(np.arange(T).reshape(NT, P).T).astype(f)
    return c


def layouts(a):
    r = {
        "x": a["x"].reshape(T, D),
        "mix_norm": a["mix_norm"], "ffn_norm": a["ffn_norm"],
        "ev_w_in": a["ev_w_in"][0], "ev_w_out": a["ev_w_out"][0],
        "od_w_in": a["od_w_in"][0], "od_w_out": a["od_w_out"][0],
        "ev_q_norm": a["ev_q_norm"][0], "ev_k_norm": a["ev_k_norm"][0],
        "ev_lam_q1": a["ev_lam_q1"][0], "ev_lam_k1": a["ev_lam_k1"][0],
        "ev_lam_q2": a["ev_lam_q2"][0], "ev_lam_k2": a["ev_lam_k2"][0],
        "ev_subln": np.tile(a["ev_subln"], (AH, 1)).reshape(AH * DV),
        "moe_w1": a["moe_w1"].reshape(2 * NE * D, DE),
        "moe_w3": a["moe_w3"].reshape(2 * NE * D, DE),
        "moe_w2": a["moe_w2"].reshape(2 * NE * DE, D),
    }
    w = a["ev_hy_conv_w"][0]
    r["hy_conv_w"] = w.reshape(3, 3 * HC, P).transpose(2, 1, 0)
    r["hy_conv_b"] = a["ev_hy_conv_b"][0].reshape(3 * HC, P).T
    r["hy_w1"], r["hy_w2"], r["hy_w3"] = a["ev_hy_f_w1"][0], a["ev_hy_f_w2"][0], a["ev_hy_f_w3"][0]
    r["hy_fb"] = np.stack([a["ev_hy_f_b1"][0], a["ev_hy_f_freq"][0], a["ev_hy_f_b2"][0]], 1)
    r["hy_skip"] = a["ev_hy_skip"][0].reshape(HC, P).T
    r["r_w"] = np.concatenate([a["moe_wg"], a["moe_we"]], 2).reshape(2, KD, P, NG + NE).transpose(0, 2, 1, 3)
    r["r_b"] = np.concatenate([a["moe_bg"], a["moe_be"]], 1)
    r["ml_conv_w"] = a["od_conv_w"][0].reshape(3, 8, P).transpose(2, 1, 0)
    r["ml_conv_b"] = a["od_conv_b"][0].reshape(8, P).T
    r["od_out_norm"] = a["od_out_norm"][0]
    gate = a["od_w_in"][0][:, 3072:]
    gw = np.zeros((D, 4, GROWS), np.float32)
    gb = np.zeros((GROWS, 2), np.float32)
    for n, (src, at) in enumerate(((0, 0), (8, 32), (4, 0), (12, 32))):
        gw[:, n, at:at + 4] = gate[:, src:src + 4]
        gb[at:at + 4, n // 2] = a["od_gate_b"][0][src:src + 4]
    r["ml_gate_w"] = gw.reshape(KD, P, 4 * GROWS).transpose(1, 0, 2)
    r["ml_gate_b"] = gb
    return r


def kernel(**inputs):
    import concourse.bacc as bacc
    from concourse.bass_utils import run_bass_kernel_spmd

    arrays = layouts({k: np.asarray(v) for k, v in inputs.items()})
    arrays.update(constants())
    nc = bacc.Bacc("TRN2", target_bir_lowering=False, num_devices=1)
    feeds, aps = {}, {}
    for name, a in arrays.items():
        a = np.ascontiguousarray(a)
        feeds[f"in_{name}"] = a
        aps[name] = nc.dram_tensor(f"in_{name}", a.shape, mybir.dt.from_np(a.dtype), kind="ExternalInput").ap()
    out = nc.dram_tensor("out_0", (T, D), F32, kind="ExternalOutput").ap()
    build(nc, aps, out)
    r = run_bass_kernel_spmd(nc, [feeds], core_ids=[0])
    return r.results[0]["out_0"].reshape(1, T, D)
```
